# Optimizing a Trainium2 kernel written in Bass

```python
import math
import jax, jax.numpy as jnp
from jax import lax
import numpy as np
import jax
import jax.numpy as jnp

D_MODEL = 1024
BATCH = 1
SEQ = 512
DEPTH = 2

CTX_LEN = 256
GRID_W = 64
EPS = 1e-6

MLSTM_HEADS = 4
MLSTM_HEAD_DIM = D_MODEL // 8
MLSTM_WIDTH = MLSTM_HEADS * MLSTM_HEAD_DIM
MLSTM_CHUNK = 128
FORGET_BIAS = 4.0
SGU_GROUPS = 4
SGU_WIDTH = D_MODEL // 4
SGU_CHUNK = 128
CONV_WIDTH = D_MODEL // 4
CONV_K = 31

MIX_WIDTH = MLSTM_WIDTH + SGU_WIDTH + CONV_WIDTH
FFN_HIDDEN = int(math.ceil(8 * D_MODEL / 3 / 256)) * 256

Q_OFF = 0
K_OFF = MLSTM_WIDTH
V_OFF = 2 * MLSTM_WIDTH
O_OFF = 3 * MLSTM_WIDTH
GATE_OFF = 4 * MLSTM_WIDTH
SGU_OFF = GATE_OFF + 4 * MLSTM_HEADS
CONV_OFF = SGU_OFF + 2 * SGU_WIDTH
IN_COLS = CONV_OFF + 2 * CONV_WIDTH


def rmsnorm(t, g):
    t32 = t.astype(jnp.float32)
    y = t32 * lax.rsqrt(jnp.mean(t32 * t32, axis=-1, keepdims=True) + EPS)
    return (y * g).astype(t.dtype)

def layernorm(t, g, b):
    t32 = t.astype(jnp.float32)
    mu = jnp.mean(t32, axis=-1, keepdims=True)
    d = t32 - mu
    var = jnp.mean(d * d, axis=-1, keepdims=True)
    return (d * lax.rsqrt(var + EPS) * g + b).astype(t.dtype)

def swiglu(h, w_gu, w_down):
    gate, up = jnp.split(h @ w_gu, 2, axis=-1)
    return (jax.nn.silu(gate) * up) @ w_down

def mlstm_inputs(p):
    B, L, _ = p.shape
    def heads(t):
        return t.reshape(B, L, MLSTM_HEADS, MLSTM_HEAD_DIM).transpose(0, 2, 1, 3).astype(jnp.float32)
    q = heads(p[..., Q_OFF:K_OFF])
    k = heads(p[..., K_OFF:V_OFF]) * (MLSTM_HEAD_DIM ** -0.5)
    v = heads(p[..., V_OFF:O_OFF])
    g = p[..., GATE_OFF:SGU_OFF].astype(jnp.float32).reshape(B, L, 4, MLSTM_HEADS).transpose(2, 0, 3, 1)
    gates = (g[0], jax.nn.log_sigmoid(g[1]), g[2], jax.nn.log_sigmoid(g[3]))
    return q, k, v, gates

def zero_state(batch):
    return (jnp.zeros((batch, MLSTM_HEADS, MLSTM_HEAD_DIM, MLSTM_HEAD_DIM), jnp.float32),
            jnp.zeros((batch, MLSTM_HEADS, MLSTM_HEAD_DIM), jnp.float32),
            jnp.zeros((batch, MLSTM_HEADS), jnp.float32))

def mlstm_scan(q, k, v, logi, logf, state, with_output):
    B, H, L, d = q.shape
    nc = L // MLSTM_CHUNK
    def to_chunks(t):
        t = t.reshape((B, H, nc, MLSTM_CHUNK) + t.shape[3:])
        return jnp.moveaxis(t, 2, 0)
    xs = tuple(to_chunks(t) for t in (q, k, v, logi, logf))
    order = jnp.tril(jnp.ones((MLSTM_CHUNK, MLSTM_CHUNK), bool))

    def step(carry, inp):
        C, n, m = carry
        qc, kc, vc, ic, fc = inp
        b = jnp.cumsum(fc, axis=-1)
        b_last = b[..., -1]
        w_log = b_last[..., None] - b + ic
        m_new = jnp.maximum(b_last + m, jnp.max(w_log, axis=-1))
        decay = jnp.exp(b_last + m - m_new)
        ks = kc * jnp.exp(w_log - m_new[..., None])[..., None]
        C_new = decay[..., None, None] * C + jnp.einsum('bhsk,bhsv->bhkv', ks, vc)
        n_new = decay[..., None] * n + jnp.sum(ks, axis=2)
        if not with_output:
            return (C_new, n_new, m_new), None
        a = b + m[..., None]
        Dlog = b[..., :, None] - b[..., None, :] + ic[..., None, :]
        Dlog = jnp.where(order, Dlog, -jnp.inf)
        m_t = jnp.maximum(a, jnp.max(Dlog, axis=-1))
        w_inter = jnp.exp(a - m_t)
        s = jnp.einsum('bhtk,bhsk->bhts', qc, kc) * jnp.exp(Dlog - m_t[..., None])
        num = w_inter[..., None] * jnp.einsum('bhtk,bhkv->bhtv', qc, C) + jnp.einsum('bhts,bhsv->bhtv', s, vc)
        den = w_inter * jnp.einsum('bhtk,bhk->bht', qc, n) + jnp.sum(s, axis=-1)
        h = num / jnp.maximum(jnp.abs(den), jnp.exp(-m_t))[..., None]
        return (C_new, n_new, m_new), h

    state, hs = lax.scan(step, state, xs)
    if not with_output:
        return None, state
    h = jnp.moveaxis(hs, 0, 2).reshape(B, H, L, d)
    return h, state

def _flip(t):
    return jnp.flip(t, axis=2)

def mlstm_bidir(q, k, v, gates, init_f, init_b, with_output):
    logi_f, logf_f, logi_b, logf_b = gates
    h_f, st_f = mlstm_scan(q, k, v, logi_f, logf_f, init_f, with_output)
    h_b, st_b = mlstm_scan(_flip(q), _flip(k), _flip(v), _flip(logi_b), _flip(logf_b), init_b, with_output)
    h = h_f + _flip(h_b) if with_output else None
    return h, st_f, st_b

def mlstm_post(h, o_pre, g):
    B, H, L, d = h.shape
    h = h * lax.rsqrt(jnp.mean(h * h, axis=-1, keepdims=True) + EPS)
    h = h.transpose(0, 2, 1, 3).reshape(B, L, H * d) * g
    return (h * jax.nn.sigmoid(o_pre.astype(jnp.float32))).astype(o_pre.dtype)

def chunk_sgu(z, ln_g, ln_b, w_s, b_s):
    z = jax.nn.gelu(z)
    u, v = jnp.split(z, 2, axis=-1)
    v = layernorm(v, ln_g, ln_b)
    B, L, C = v.shape
    vg = v.reshape(B, L // SGU_CHUNK, SGU_CHUNK, SGU_GROUPS, C // SGU_GROUPS)
    mixed = jnp.einsum('gpq,bnqgc->bnpgc', w_s, vg) + b_s.T[:, :, None]
    return u * mixed.reshape(B, L, C)

def dwconv1d(y, w, b):
    kw, ch = w.shape
    out = lax.conv_general_dilated(y, w.reshape(kw, 1, ch).astype(y.dtype), window_strides=(1,),
                                   padding=[(kw // 2, kw // 2)], dimension_numbers=('NWC', 'WIO', 'NWC'),
                                   feature_group_count=ch)
    return out + b

def axial_dwconv(y, w, b):
    B, L, C = y.shape
    rows = L // GRID_W
    half = C // 2
    yr = dwconv1d(y[..., :half].reshape(B * rows, GRID_W, half), w[:, :half], b[:half]).reshape(B, L, half)
    yc = y[..., half:].reshape(B, rows, GRID_W, half).transpose(0, 2, 1, 3).reshape(B * GRID_W, rows, half)
    yc = dwconv1d(yc, w[:, half:], b[half:]).reshape(B, GRID_W, rows, half).transpose(0, 2, 1, 3).reshape(B, L, half)
    return jnp.concatenate([yr, yc], axis=-1)

def conformer_conv(z, w_dw, b_dw, ln_g, ln_b, grid):
    a, g = jnp.split(z, 2, axis=-1)
    y = a * jax.nn.sigmoid(g)
    y = axial_dwconv(y, w_dw, b_dw) if grid else dwconv1d(y, w_dw, b_dw)
    return jax.nn.silu(layernorm(y, ln_g, ln_b))

def mix_groups(p, h_mlstm, mlstm_g, sgu_ln_g, sgu_ln_b, sgu_w, sgu_b, conv_w, conv_b, conv_ln_g, conv_ln_b, grid):
    y_a = mlstm_post(h_mlstm, p[..., O_OFF:GATE_OFF], mlstm_g)
    y_b = chunk_sgu(p[..., SGU_OFF:CONV_OFF], sgu_ln_g, sgu_ln_b, sgu_w, sgu_b)
    y_c = conformer_conv(p[..., CONV_OFF:IN_COLS], conv_w, conv_b, conv_ln_g, conv_ln_b, grid)
    return jnp.concatenate([y_a, y_b, y_c], axis=-1)

def first_inputs(seed: int = 0) -> dict:
    key = jax.random.key(seed)
    ks = jax.random.split(key, 24)
    def nrm(k, shape, scale):
        return jax.random.normal(k, shape, jnp.float32) * scale
    fb = np.zeros((IN_COLS,), np.float32)
    fb[GATE_OFF + MLSTM_HEADS:GATE_OFF + 2 * MLSTM_HEADS] = FORGET_BIAS
    fb[GATE_OFF + 3 * MLSTM_HEADS:GATE_OFF + 4 * MLSTM_HEADS] = FORGET_BIAS
    return {
        'x': nrm(ks[0], (BATCH, SEQ, D_MODEL), 1.0),
        'c': nrm(ks[1], (BATCH, D_MODEL), 1.0),
        'ctx': nrm(ks[2], (BATCH, CTX_LEN, D_MODEL), 1.0),
        'c_ctx': nrm(ks[3], (D_MODEL,), 1.0),
        'w_mod': nrm(ks[4], (DEPTH, D_MODEL, 6 * D_MODEL), 0.5 * D_MODEL ** -0.5),
        'b_mod': nrm(ks[5], (DEPTH, 6 * D_MODEL), 0.02),
        'norm1_g': 1.0 + nrm(ks[6], (DEPTH, D_MODEL), 0.02),
        'w_in': nrm(ks[7], (DEPTH, D_MODEL, IN_COLS), D_MODEL ** -0.5),
        'b_in': nrm(ks[8], (DEPTH, IN_COLS), 0.02) + jnp.asarray(fb),
        'mlstm_g': 1.0 + nrm(ks[9], (DEPTH, MLSTM_WIDTH), 0.02),
        'sgu_ln_g': 1.0 + nrm(ks[10], (DEPTH, SGU_WIDTH), 0.02),
        'sgu_ln_b': nrm(ks[11], (DEPTH, SGU_WIDTH), 0.02),
        'sgu_w': nrm(ks[12], (DEPTH, SGU_GROUPS, SGU_CHUNK, SGU_CHUNK), SGU_CHUNK ** -0.5),
        'sgu_b': nrm(ks[13], (DEPTH, SGU_GROUPS, SGU_CHUNK), 0.02),
        'conv_w': nrm(ks[14], (DEPTH, CONV_K, CONV_WIDTH), CONV_K ** -0.5),
        'conv_b': nrm(ks[15], (DEPTH, CONV_WIDTH), 0.02),
        'conv_ln_g': 1.0 + nrm(ks[16], (DEPTH, CONV_WIDTH), 0.02),
        'conv_ln_b': nrm(ks[17], (DEPTH, CONV_WIDTH), 0.02),
        'w_out': nrm(ks[18], (DEPTH, MIX_WIDTH, D_MODEL), MIX_WIDTH ** -0.5),
        'norm2_g': 1.0 + nrm(ks[19], (DEPTH, D_MODEL), 0.02),
        'w_gu': nrm(ks[20], (DEPTH, D_MODEL, 2 * FFN_HIDDEN), D_MODEL ** -0.5),
        'w_down': nrm(ks[21], (DEPTH, FFN_HIDDEN, D_MODEL), FFN_HIDDEN ** -0.5),
        'final_g': 1.0 + nrm(ks[22], (D_MODEL,), 0.02),
    }

def first_block(x, c, ctx, c_ctx, w_mod, b_mod, norm1_g, w_in, b_in, mlstm_g, sgu_ln_g, sgu_ln_b, sgu_w, sgu_b,
              conv_w, conv_b, conv_ln_g, conv_ln_b, w_out, norm2_g, w_gu, w_down, final_g):
    batch = x.shape[0]
    c_act = jax.nn.silu(c)
    cc_act = jax.nn.silu(c_ctx)
    xc = ctx
    for l in range(DEPTH):
        last = l == DEPTH - 1
        mod = (c_act @ w_mod[l] + b_mod[l])[:, None, :]
        modc = cc_act @ w_mod[l] + b_mod[l]
        sh1, sc1, g1, sh2, sc2, g2 = jnp.split(mod, 6, axis=-1)
        shc1, scc1, gc1, shc2, scc2, gc2 = jnp.split(modc, 6, axis=-1)

        px = (rmsnorm(x, norm1_g[l]) * (1.0 + sc1) + sh1) @ w_in[l] + b_in[l]
        pc = (rmsnorm(xc, norm1_g[l]) * (1.0 + scc1) + shc1) @ w_in[l] + b_in[l]
        qx, kx, vx, gtx = mlstm_inputs(px)
        qc, kc, vc, gtc = mlstm_inputs(pc)
        zs = zero_state(batch)
        h_c, st_f, st_b = mlstm_bidir(qc, kc, vc, gtc, zs, zs, not last)
        h_x, _, _ = mlstm_bidir(qx, kx, vx, gtx, st_f, st_b, True)

        y_x = mix_groups(px, h_x, mlstm_g[l], sgu_ln_g[l], sgu_ln_b[l], sgu_w[l], sgu_b[l],
                         conv_w[l], conv_b[l], conv_ln_g[l], conv_ln_b[l], True)
        x = x + g1 * (y_x @ w_out[l])
        x = x + g2 * swiglu(rmsnorm(x, norm2_g[l]) * (1.0 + sc2) + sh2, w_gu[l], w_down[l])

        if not last:
            y_c = mix_groups(pc, h_c, mlstm_g[l], sgu_ln_g[l], sgu_ln_b[l], sgu_w[l], sgu_b[l],
                             conv_w[l], conv_b[l], conv_ln_g[l], conv_ln_b[l], False)
            xc = xc + gc1 * (y_c @ w_out[l])
            xc = xc + gc2 * swiglu(rmsnorm(xc, norm2_g[l]) * (1.0 + scc2) + shc2, w_gu[l], w_down[l])
    return rmsnorm(x, final_g)


HEAD_DIM = 64
PLE_DIM = 256
ROPE_THETA = 10000.0
BLOCK = 128
N_MIXERS = 3
LN_EPS = 1e-5
DEEPNORM_ALPHA = (2 * DEPTH) ** 0.25
DEEPNORM_BETA = (8 * DEPTH) ** -0.25

A_GROUPS = ((128, 1), (512, 4), (2048, 16))
A_HEADS = D_MODEL // HEAD_DIM
A_WIDTH = A_HEADS * HEAD_DIM
A_IN = 3 * len(A_GROUPS) * A_WIDTH + A_WIDTH

B_HEADS = D_MODEL // HEAD_DIM
B_KV_HEADS = 2
B_WINDOW = 128
B_WIDTH = B_HEADS * HEAD_DIM
B_KV = B_KV_HEADS * HEAD_DIM
B_IN = 2 * B_WIDTH + 2 * B_KV

C_HEADS = D_MODEL // HEAD_DIM
C_KV_HEADS = 4
C_WIDTH = C_HEADS * HEAD_DIM
C_KV = C_KV_HEADS * HEAD_DIM
C_CMP_LEN = 32
C_CMP_STRIDE = 16
C_SEL_LEN = 64
C_N_SEL = 16
C_WINDOW = 512
C_SEL_OVERLAP = (1.0, 2.0, 2.0, 2.0, 1.0)
C_IN = 2 * C_WIDTH + 6 * C_KV + 3 * C_HEADS

N_A_LAYERS = len(range(0, DEPTH, N_MIXERS))
N_B_LAYERS = len(range(1, DEPTH, N_MIXERS))
N_C_LAYERS = len(range(2, DEPTH, N_MIXERS))


def split_cols(h, sizes):
    out, start = [], 0
    for s in sizes:
        out.append(h[..., start:start + s])
        start += s
    return out

def rope_tables(seq_len):
    inv = 1.0 / (ROPE_THETA ** (jnp.arange(0, HEAD_DIM, 2, dtype=jnp.float32) / HEAD_DIM))
    ang = jnp.arange(seq_len, dtype=jnp.float32)[:, None] * inv[None, :]
    return jnp.cos(ang), jnp.sin(ang)

def apply_rope(t, cos, sin):
    tf = t.astype(jnp.float32)
    half = HEAD_DIM // 2
    t1, t2 = tf[..., :half], tf[..., half:]
    c, s = cos[None, :, None, :], sin[None, :, None, :]
    return jnp.concatenate([t1 * c - t2 * s, t2 * c + t1 * s], axis=-1).astype(t.dtype)

def layer_norm(x, g, b):
    xf = x.astype(jnp.float32)
    mu = jnp.mean(xf, axis=-1, keepdims=True)
    var = jnp.mean(jnp.square(xf - mu), axis=-1, keepdims=True)
    y = (xf - mu) * lax.rsqrt(var + LN_EPS) * g.astype(jnp.float32) + b.astype(jnp.float32)
    return y.astype(x.dtype)

def banded_attention(q, k, v, max_dist, sinks=None):
    B_, L, Hk, G, dh = q.shape
    nb = -(-L // BLOCK)
    pad = nb * BLOCK - L
    npv = -(-max_dist // BLOCK)
    W = (npv + 1) * BLOCK
    qb = jnp.pad(q, ((0, 0), (0, pad), (0, 0), (0, 0), (0, 0))).reshape(B_, nb, BLOCK, Hk, G, dh)

    def windows(t):
        tp = jnp.pad(t, ((0, 0), (npv * BLOCK, pad), (0, 0), (0, 0))).reshape(B_, nb + npv, BLOCK, Hk, dh)
        return jnp.concatenate([tp[:, j:j + nb] for j in range(npv + 1)], axis=2)

    kw, vw = windows(k), windows(v)
    s = jnp.einsum('bnqhgd,bnkhd->bnhgqk', qb, kw).astype(jnp.float32) * (dh ** -0.5)
    dist = np.arange(BLOCK)[:, None] + npv * BLOCK - np.arange(W)[None, :]
    band = (dist >= 0) & (dist <= max_dist)
    kpos = np.arange(nb)[:, None] * BLOCK - npv * BLOCK + np.arange(W)[None, :]
    mask = band[None, :, :] & (kpos >= 0)[:, None, :]
    s = jnp.where(mask[None, :, None, None, :, :], s, -jnp.inf)
    m = jnp.max(s, axis=-1, keepdims=True)
    if sinks is not None:
        sk = sinks.astype(jnp.float32).reshape(1, 1, Hk, G, 1, 1)
        m = jnp.maximum(m, sk)
    e = jnp.exp(s - m)
    l = jnp.sum(e, axis=-1, keepdims=True)
    if sinks is not None:
        l = l + jnp.exp(sk - m)
    o = jnp.einsum('bnhgqk,bnkhd->bnqhgd', e, vw.astype(jnp.float32))
    o = o / jnp.transpose(l, (0, 1, 4, 2, 3, 5))
    lse = jnp.transpose((m + jnp.log(l))[..., 0], (0, 1, 4, 2, 3))
    o = o.reshape(B_, nb * BLOCK, Hk, G, dh)[:, :L]
    lse = lse.reshape(B_, nb * BLOCK, Hk, G)[:, :L]
    return o, lse

def mixer_a(x, w_in, w_out, cos, sin):
    B_, S, _ = x.shape
    h = x @ w_in
    outs, lses = [], []
    for gi, (window, dil) in enumerate(A_GROUPS):
        base = 3 * gi * A_WIDTH
        q, k, v = split_cols(h[..., base:base + 3 * A_WIDTH], [A_WIDTH] * 3)
        q = apply_rope(q.reshape(B_, S, A_HEADS, HEAD_DIM), cos, sin)
        k = apply_rope(k.reshape(B_, S, A_HEADS, HEAD_DIM), cos, sin)
        v = v.reshape(B_, S, A_HEADS, HEAD_DIM)
        Ls = S // dil

        def strided(t):
            return jnp.transpose(t.reshape(B_, Ls, dil, A_HEADS, HEAD_DIM), (0, 2, 1, 3, 4)).reshape(B_ * dil, Ls, A_HEADS, HEAD_DIM)

        o, lse = banded_attention(strided(q)[:, :, :, None, :], strided(k), strided(v), window // dil)
        o = jnp.transpose(o.reshape(B_, dil, Ls, A_HEADS, HEAD_DIM), (0, 2, 1, 3, 4)).reshape(B_, S, A_HEADS, HEAD_DIM)
        lse = jnp.transpose(lse.reshape(B_, dil, Ls, A_HEADS), (0, 2, 1, 3)).reshape(B_, S, A_HEADS)
        outs.append(o)
        lses.append(lse)
    wts = jax.nn.softmax(jnp.stack(lses, axis=0), axis=0)
    o = jnp.einsum('gbsh,gbshd->bshd', wts, jnp.stack(outs, axis=0))
    z = h[..., -A_WIDTH:]
    o = o.reshape(B_, S, A_WIDTH).astype(x.dtype)
    return (o * jax.nn.silu(z)) @ w_out

def mixer_b(x, w_in, sinks, w_out, cos, sin):
    B_, S, _ = x.shape
    G = B_HEADS // B_KV_HEADS
    q, k, v, z = split_cols(x @ w_in, [B_WIDTH, B_KV, B_KV, B_WIDTH])
    q = apply_rope(q.reshape(B_, S, B_HEADS, HEAD_DIM), cos, sin).reshape(B_, S, B_KV_HEADS, G, HEAD_DIM)
    k = apply_rope(k.reshape(B_, S, B_KV_HEADS, HEAD_DIM), cos, sin)
    v = v.reshape(B_, S, B_KV_HEADS, HEAD_DIM)
    o, _ = banded_attention(q, k, v, B_WINDOW - 1, sinks)
    o = o.reshape(B_, S, B_WIDTH).astype(x.dtype)
    return (o * jax.nn.silu(z)) @ w_out

def mixer_c(x, w_in, w_ck, w_cv, pos_cmp, w_out, cos, sin):
    B_, S, _ = x.shape
    Hk, G, dh = C_KV_HEADS, C_HEADS // C_KV_HEADS, HEAD_DIM
    scale = dh ** -0.5
    q, kc, vc, ks, vs, kw, vw, gl, z = split_cols(x @ w_in, [C_WIDTH] + [C_KV] * 6 + [3 * C_HEADS, C_WIDTH])
    q = apply_rope(q.reshape(B_, S, C_HEADS, dh), cos, sin).reshape(B_, S, Hk, G, dh)
    kv_shape = (B_, S, Hk, dh)
    kc = apply_rope(kc.reshape(kv_shape), cos, sin)
    ks = apply_rope(ks.reshape(kv_shape), cos, sin)
    kw = apply_rope(kw.reshape(kv_shape), cos, sin)
    vc, vs, vw = vc.reshape(kv_shape), vs.reshape(kv_shape), vw.reshape(kv_shape)

    n_c = S // C_CMP_STRIDE - 1

    def compress(t, w):
        tr = t.reshape(B_, S // C_CMP_STRIDE, C_CMP_STRIDE, Hk, dh)
        blk = jnp.concatenate([tr[:, :-1], tr[:, 1:]], axis=2)
        return jnp.einsum('bnjhd,jde->bnhe', blk + pos_cmp[None, None, :, None, :], w)

    k_cmp, v_cmp = compress(kc, w_ck), compress(vc, w_cv)
    cmp_end = jnp.arange(n_c) * C_CMP_STRIDE + C_CMP_LEN - 1

    n_s = S // C_SEL_LEN
    n_sel = min(C_N_SEL, n_s)
    ks_blocks = jnp.transpose(ks.reshape(B_, n_s, C_SEL_LEN, Hk, dh), (0, 3, 1, 2, 4))
    vs_blocks = jnp.transpose(vs.reshape(B_, n_s, C_SEL_LEN, Hk, dh), (0, 3, 1, 2, 4))
    bi = jnp.arange(B_)[:, None, None, None]
    hi = jnp.arange(Hk)[None, None, :, None]
    blk_ids = jnp.arange(n_s)

    def query_block(args):
        qb, t0 = args
        tq = t0 + jnp.arange(BLOCK)
        s = jnp.einsum('bqhgd,bnhd->bqhgn', qb, k_cmp).astype(jnp.float32) * scale
        cvalid = cmp_end[None, :] <= tq[:, None]
        s = jnp.where(cvalid[None, :, None, None, :], s, -jnp.inf)
        m = jnp.max(s, axis=-1, keepdims=True)
        m = jnp.where(jnp.isfinite(m), m, 0.0)
        e = jnp.exp(s - m)
        pc = e / jnp.maximum(jnp.sum(e, axis=-1, keepdims=True), 1e-30)
        o_cmp = jnp.einsum('bqhgn,bnhd->bqhgd', pc, v_cmp.astype(jnp.float32))
        imp = jnp.pad(jnp.sum(pc, axis=3), ((0, 0), (0, 0), (0, 0), (1, 1)))
        imp_s = C_SEL_OVERLAP[0] * imp[..., 0::4][..., :n_s]
        for o_off in range(1, len(C_SEL_OVERLAP)):
            imp_s = imp_s + C_SEL_OVERLAP[o_off] * imp[..., o_off::4][..., :n_s]
        cur = tq // C_SEL_LEN
        forced = (blk_ids[None, :] == 0) | (blk_ids[None, :] == cur[:, None]) | (blk_ids[None, :] == cur[:, None] - 1)
        bvalid = blk_ids[None, :] * C_SEL_LEN <= tq[:, None]
        score = jnp.where(forced[None, :, None, :], 1e4, jnp.where(bvalid[None, :, None, :], imp_s, -1.0))
        _, idx = lax.top_k(score, n_sel)
        ksel = ks_blocks[bi, hi, idx]
        vsel = vs_blocks[bi, hi, idx]
        kpos = idx[..., None] * C_SEL_LEN + jnp.arange(C_SEL_LEN)
        smask = kpos <= tq[None, :, None, None, None]
        ss = jnp.einsum('bqhgd,bqhnkd->bqhgnk', qb, ksel).astype(jnp.float32) * scale
        ss = jnp.where(smask[:, :, :, None], ss, -jnp.inf)
        ps = jax.nn.softmax(ss.reshape(ss.shape[:4] + (n_sel * C_SEL_LEN,)), axis=-1).reshape(ss.shape)
        o_slc = jnp.einsum('bqhgnk,bqhnkd->bqhgd', ps, vsel.astype(jnp.float32))
        return o_cmp, o_slc

    nqb = S // BLOCK
    q_blocks = jnp.transpose(q.reshape(B_, nqb, BLOCK, Hk, G, dh), (1, 0, 2, 3, 4, 5))
    t0s = jnp.arange(nqb, dtype=jnp.int32) * BLOCK
    o_cmp, o_slc = lax.map(query_block, (q_blocks, t0s))
    o_cmp = jnp.transpose(o_cmp, (1, 0, 2, 3, 4, 5)).reshape(B_, S, Hk, G, dh)
    o_slc = jnp.transpose(o_slc, (1, 0, 2, 3, 4, 5)).reshape(B_, S, Hk, G, dh)
    o_win, _ = banded_attention(q, kw, vw, C_WINDOW - 1)
    g = jax.nn.sigmoid(gl.astype(jnp.float32)).reshape(B_, S, 3, Hk, G, 1)
    o = g[:, :, 0] * o_cmp + g[:, :, 1] * o_slc + g[:, :, 2] * o_win
    o = o.reshape(B_, S, C_WIDTH).astype(x.dtype)
    return (o * jax.nn.silu(z)) @ w_out

def second_inputs(seed: int = 0) -> dict:
    key = jax.random.key(seed)
    ks = jax.random.split(key, 16)

    def nrm(k, shape, scale):
        return jax.random.normal(k, shape, jnp.float32) * scale

    return {
        'x': nrm(ks[0], (BATCH, SEQ, D_MODEL), 1.0),
        'p': nrm(ks[1], (DEPTH, BATCH, SEQ, PLE_DIM), 1.0),
        'a_w_in': nrm(ks[2], (N_A_LAYERS, D_MODEL, A_IN), D_MODEL ** -0.5),
        'a_w_out': nrm(ks[3], (N_A_LAYERS, A_WIDTH, D_MODEL), A_WIDTH ** -0.5 * DEEPNORM_BETA),
        'b_w_in': nrm(ks[4], (N_B_LAYERS, D_MODEL, B_IN), D_MODEL ** -0.5),
        'b_sinks': nrm(ks[5], (N_B_LAYERS, B_HEADS), 1.0),
        'b_w_out': nrm(ks[6], (N_B_LAYERS, B_WIDTH, D_MODEL), B_WIDTH ** -0.5 * DEEPNORM_BETA),
        'c_w_in': nrm(ks[7], (N_C_LAYERS, D_MODEL, C_IN), D_MODEL ** -0.5),
        'c_w_ck': nrm(ks[8], (N_C_LAYERS, C_CMP_LEN, HEAD_DIM, HEAD_DIM), (C_CMP_LEN * HEAD_DIM) ** -0.5),
        'c_w_cv': nrm(ks[9], (N_C_LAYERS, C_CMP_LEN, HEAD_DIM, HEAD_DIM), (C_CMP_LEN * HEAD_DIM) ** -0.5),
        'c_pos': nrm(ks[10], (N_C_LAYERS, C_CMP_LEN, HEAD_DIM), 0.5),
        'c_w_out': nrm(ks[11], (N_C_LAYERS, C_WIDTH, D_MODEL), C_WIDTH ** -0.5 * DEEPNORM_BETA),
        'ln_g': 1.0 + nrm(ks[12], (DEPTH, D_MODEL), 0.05),
        'ln_b': nrm(ks[13], (DEPTH, D_MODEL), 0.05),
        'ple_w_proj': nrm(ks[14], (DEPTH, PLE_DIM, D_MODEL), PLE_DIM ** -0.5),
        'ple_w_gate': nrm(ks[15], (DEPTH, D_MODEL, D_MODEL), D_MODEL ** -0.5),
    }

def second_block(x, p, a_w_in, a_w_out, b_w_in, b_sinks, b_w_out, c_w_in, c_w_ck, c_w_cv, c_pos, c_w_out, ln_g, ln_b, ple_w_proj, ple_w_gate):
    cos, sin = rope_tables(x.shape[1])
    for i in range(DEPTH):
        j = i // N_MIXERS
        kind = i % N_MIXERS
        if kind == 0:
            h = mixer_a(x, a_w_in[j], a_w_out[j], cos, sin)
        elif kind == 1:
            h = mixer_b(x, b_w_in[j], b_sinks[j], b_w_out[j], cos, sin)
        else:
            h = mixer_c(x, c_w_in[j], c_w_ck[j], c_w_cv[j], c_pos[j], c_w_out[j], cos, sin)
        x = layer_norm(DEEPNORM_ALPHA * x + h, ln_g[i], ln_b[i])
        gate = jax.nn.sigmoid((x @ ple_w_gate[i]).astype(jnp.float32))
        x = (x.astype(jnp.float32) + gate * (p[i] @ ple_w_proj[i]).astype(jnp.float32)).astype(x.dtype)
    return x


def setup_inputs(seed=0):
    out = dict(first_inputs(seed))
    for name, value in second_inputs(seed + 1).items():
        if name != "x":
            out[name + "_2"] = value
    return out


def reference(
    x, c, ctx, c_ctx, w_mod, b_mod, norm1_g, w_in, b_in, mlstm_g, sgu_ln_g, sgu_ln_b, sgu_w,
    sgu_b, conv_w, conv_b, conv_ln_g, conv_ln_b, w_out, norm2_g, w_gu, w_down, final_g, p_2,
    a_w_in_2, a_w_out_2, b_w_in_2, b_sinks_2, b_w_out_2, c_w_in_2, c_w_ck_2, c_w_cv_2, c_pos_2,
    c_w_out_2, ln_g_2, ln_b_2, ple_w_proj_2, ple_w_gate_2,
):
    x = first_block(
        x, c, ctx, c_ctx, w_mod, b_mod, norm1_g, w_in, b_in, mlstm_g, sgu_ln_g, sgu_ln_b, sgu_w,
        sgu_b, conv_w, conv_b, conv_ln_g, conv_ln_b, w_out, norm2_g, w_gu, w_down, final_g,
    )
    return second_block(
        x, p_2, a_w_in_2, a_w_out_2, b_w_in_2, b_sinks_2, b_w_out_2, c_w_in_2, c_w_ck_2,
        c_w_cv_2, c_pos_2, c_w_out_2, ln_g_2, ln_b_2, ple_w_proj_2, ple_w_gate_2,
    )


_drawn_inputs = setup_inputs


def setup_inputs(seed=0):
    import zlib

    import numpy as np

    out = dict(_drawn_inputs(seed))
    spreads = {}
    factors = {'norm1_g': 6.718,
     'mlstm_g': 21.536,
     'sgu_ln_g': 8.0,
     'sgu_ln_b': 8.0,
     'sgu_b': 8.0,
     'conv_b': 8.0,
     'conv_ln_g': 27.886,
     'conv_ln_b': 30.295,
     'norm2_g': 8.0,
     'final_g': 3.489,
     'b_sinks_2': 21.867}
    for name, (base, spread) in spreads.items():
        noise = np.random.default_rng([zlib.crc32(name.encode()), seed]).standard_normal(out[name].shape)
        drawn = base * np.exp(spread * noise) if base else spread * noise
        out[name] = jnp.asarray(drawn.astype(out[name].dtype))
    for name, factor in factors.items():
        out[name] = (out[name] * factor).astype(out[name].dtype)
    return out
```

```python
import numpy as np
import concourse.bass as bass
from concourse import mybir
from contextlib import ExitStack

FP32 = mybir.dt.float32
FP32R = mybir.dt.float32r
ALU = mybir.AluOpType
ACT = mybir.ActivationFunctionType

P = 128
D = 1024
KT = D // P
SEQ, CTX = 512, 256
T = SEQ + CTX
NJ, NX = T // P, SEQ // P
DEPTH = 2
HEADS, HD = 4, 128
FFN = 2816
FT = FFN // P
PARTS = ((0, 8), (8, 8), (16, 6))
GRID = 64
CONV_K = 31
EPS, LN_EPS = 1e-6, 1e-5
K_SCALE = HD ** -0.5
ALPHA = float((2 * DEPTH) ** 0.25)
AH, ADIM = 16, 64
A_SCALE = ADIM ** -0.5
NEG = -1e30
GELU_C, GELU_A = 0.7978845608028654, 0.044715
RING = 4

GA_T, U_T, SV_T, K_T, V_T, Q_T, O_T = 0, 4, 6, 8, 12, 16, 20
N_IN = 24
LAYER_TILES = N_IN + KT + 2 * FT + len(PARTS) * KT
HP = AH // 2
A_TILES = 10
N_A = DEPTH * LAYER_TILES
N_AOUT = N_A + A_TILES * HP
N_PLE = (N_AOUT + KT, N_AOUT + KT + 2 * KT + 3 + 2 * HP + KT)
N_B = N_PLE[0] + 2 * KT
N_BQZ = N_B + 3
N_BOUT = N_BQZ + 2 * HP
N_ALL = N_PLE[1] + 2 * KT


def part_start(l, p):
    return l * LAYER_TILES + N_IN + KT + sum(2 * PARTS[q][1] + KT for q in range(p))


def staged(n):
    if n < N_A:
        return not U_T + 2 <= n % LAYER_TILES < N_IN
    if n < N_AOUT:
        return (n - N_A) % A_TILES == 9
    if n < N_B:
        return True
    if n < N_BQZ:
        return False
    if n < N_BOUT:
        return (n - N_BQZ) % 2 == 1
    return True


USED = [0]
for _n in range(N_ALL):
    USED.append(USED[-1] + staged(_n))


def used(n):
    return USED[max(n + 1, 0)]


PC = {}
NPC = 0
for _name, _w in (("norm1", 8), ("norm2", 8), ("b_in", 24), ("mg", 4), ("cw", 2 * CONV_K), ("cb", 2),
                  ("cg", 2), ("clb", 2), ("b_mod", 48)):
    PC[_name] = NPC
    NPC += _w
SROW_B = 512
SROW_G = SROW_B + 2 * P
N_SROW = SROW_G + 16
N_CONST = 5 * P + 2


def mlstm_steps(l):
    order = ([4, 5, 0, 1, 2, 3], [5, 4, 3, 2, 1, 0])
    return [(d, order[d][i], i == 0, l == 0 or order[d][i] < NX) for i in range(NJ) for d in range(2)] if l < DEPTH else []


def outputs_before(l, t):
    return sum(s[3] for m in range(l) for s in mlstm_steps(m)) + sum(s[3] for s in mlstm_steps(l)[:t])


def weighted_before(l, t):
    return (sum(s[3] and not s[2] for m in range(l) for s in mlstm_steps(m))
            + sum(s[3] and not s[2] for s in mlstm_steps(l)[:t]))


def width(l, t=None):
    return T if l == 0 or (t is not None and K_T <= t < Q_T) else SEQ


def ranges(w):
    return [(0, SEQ), (SEQ, T)] if w == T else [(0, SEQ)]


def build_program(nc, xT, cT, pc_d, fin_d, srow_d, consts_d, sguw_d, wg_d, wmod_d, win_d, wout_d, wgu_d, wdn_d,
                  b2_d, bmask_d, p_d, wa_d, wao_d, pleg_d, plep_d, wbk_d, wbqz_d, wbo_d, out_d):
    cursor = [nc.sbuf_base + (-nc.sbuf_base) % 64]
    addr_of = {}

    def place(name, shape, dt=FP32, addr=None):
        size = 4
        for s in shape[1:]:
            size *= s
        if addr is None:
            addr = cursor[0]
            cursor[0] += size + (-size) % 32
        assert addr + size <= nc.sbuf_usable_end, (name, addr + size, nc.sbuf_usable_end)
        addr_of[name] = addr
        return nc.alloc_sbuf_tensor_at(name, shape, dt, offset=addr)

    stack = ExitStack()
    with stack:
        def sem(name):
            return stack.enter_context(nc.semaphore(name))

        raw = [place(f"raw{i}", [P, KT * P]) for i in range(RING)]
        w_hi = [place(f"w_hi{i}", [P, KT, P], FP32R) for i in range(2)]
        w_lo = [place(f"w_lo{i}", [P, KT, P], FP32R) for i in range(2)]
        Z = place("Z", [P, 4, T])
        TH = place("TH", [P, N_SROW])
        ident = place("ident", [P, P])
        ones = place("ones", [P, P])
        word = place("word", [P, 8])
        eps_c = place("eps_c", [P, 2])
        X = place("X", [P, KT, T])
        XH = place("XH", [P, KT, T], FP32R)
        XL = place("XL", [P, KT, T], FP32R)
        tri = place("tri", [P, 2, P])
        mskd = place("mskd", [P, 2, P])
        dsel = place("dsel", [8, 2])
        pc = place("pc", [P, DEPTH, NPC])
        fin_g = place("fin_g", [P, KT])
        bcol = place("bcol", [P, N_IN])
        mod = place("mod", [P, 48, 2])
        nsc = place("nsc", [P, 2, KT, 2])
        cact = place("cact", [P, KT, 2])
        cth = place("cth", [P, KT, 2])
        sgw = place("sgw", [P, 4, P])
        wg = place("wg", [P, KT, 16])
        wgh = place("wgh", [P, KT, 16], FP32R)
        wgl = place("wgl", [P, KT, 16], FP32R)
        gt = place("gt", [P, NJ, 2, 2, HEADS])
        lf = place("lf", [P, 3, NJ, 8])
        gcol = place("gcol", [P, NJ, 8])
        btm = place("btm", [P, NJ, 8])
        bst = place("bst", [P, NJ, 6])
        bmv = place("bmv", [P, NJ, 2])
        mprev = place("mprev", [8, 2, NJ])
        work = cursor[0]
        kfm = place("kfm", [P, HEADS, T])
        qfm = place("qfm", [P, HEADS, T])
        tho = place("tho", [P, HEADS, T])
        ktm = place("ktm", [P, NJ, HEADS, P])
        vtm = place("vtm", [P, NJ, HEADS, P])
        YC = place("YC", [P, 2, T])
        AC = place("AC", [P, 2, T])
        Ug = place("Ug", [P, 2, T])
        srow = place("srow", [P, N_SROW], addr=addr_of["TH"])
        SVT = place("SVT", [P, NJ, 256], addr=addr_of["AC"])
        GT = place("GT", [P, HEADS, T], addr=addr_of["qfm"])
        MT = place("MT", [P, T], addr=addr_of["tho"])
        MU = place("MU", [P, T], addr=addr_of["kfm"])
        ri, rf, rb, rm = (place(f"row{i}", [8, T], addr=addr_of["XH"] + i * T * 4) for i in range(4))
        rhl = [[place(f"rhl{i}{j}", [8, T], FP32R, addr=addr_of["XH"] + (4 + 2 * i + j) * T * 4) for j in range(2)]
               for i in range(3)]
        r2 = place("row4", [8, T], addr=addr_of["XH"] + 10 * T * 4)
        selh = place("selh", [8, 8, P], FP32R, addr=addr_of["row4"])
        H = place("H", [P, HEADS, T], addr=addr_of["XL"] + 4 * T * 4)
        Ee, Pp, Qw, WIs, EMs, Ks = (place(f"mw{i}", [P, HEADS, P], addr=addr_of["Z"] + i * 2048) for i in range(6))
        ST = [place(f"ST{d}", [P, HEADS, 2, P], addr=addr_of[("YC", "row0")[d]]) for d in range(2)]
        W1 = place("W1", [P, HEADS, P], addr=addr_of["YC"] + 4096)
        AD = place("AD", [P, HEADS, P], addr=addr_of["TH"])
        HN = place("HN", [P, HEADS, P], addr=addr_of["row2"])
        RH = place("RH", [P, HEADS, T], addr=addr_of["ktm"])
        HH = place("HH", [P, 8, T], FP32R, addr=work)
        HL = place("HL", [P, 8, T], FP32R, addr=work + 8 * T * 4)
        modw = [place(f"modw{i}", [P, 2, KT, P], addr=work + i * 8192) for i in range(8)]
        PS = stack.enter_context(nc.psum_tensor("PS", [P, 8, 512], FP32))

        def banks(a, b):
            return PS[:, a:b, :].rearrange("p a b -> p (a b)")

        def acc(n):
            return banks(2 * (n % 2), 2 * (n % 2) + 2)

        s_const = sem("constants_loaded")
        s_par = sem("layer_parameters_loaded")
        s_raw = [sem(f"raw_weights_loaded{i}") for i in range(RING)]
        s_hi = sem("weights_upper_made")
        s_split = sem("weights_split")
        s_tile = sem("gemm_tile_done")
        s_evac = sem("gemm_tile_evacuated")
        s_used = sem("staged_tile_used")
        s_modw = [sem(f"mod_weights_loaded{i}") for i in range(8)]
        s_modd = sem("mod_chunk_done")
        s_mod = sem("modulation_ready")
        s_cact = sem("c_activated")
        s_cth = sem("c_tanh_made")
        s_one = sem("on_chip_constants_made")
        s_sq = sem("squares_made")
        s_squ = sem("squares_summed")
        s_rstd = sem("rstd_made")
        s_xn = sem("normed_made")
        s_xh = sem("operand_upper_made")
        s_xl = sem("operand_split")
        s_dch = sem("dve_chain")
        s_ach = sem("act_chain")
        s_gin = sem("gelu_argument_made")
        s_gth = sem("gelu_tanh_made")
        s_gel = sem("gelu_made")
        s_tr = sem("transposed")
        s_tre = sem("transposed_evacuated")
        s_svv = sem("sgu_variance_made")
        s_svr = sem("sgu_rstd_made")
        s_svt = sem("sgu_v_normed")
        s_mix = sem("sgu_mixed")
        s_mixu = sem("sgu_mixed_used")
        s_wgh = sem("gate_weights_upper_made")
        s_wgl = sem("gate_weights_split")
        s_gate = sem("gates_done")
        s_gtm = sem("gates_made")
        s_lfa = sem("log_forget_softplus_made")
        s_lf = sem("log_forget_made")
        s_bt = sem("forget_sums_done")
        s_btm = sem("forget_sums_evacuated")
        s_rows = sem("rows_done")
        s_row = sem("rows_made")
        s_rowh = sem("rows_upper_made")
        s_rowl = sem("rows_split")
        s_nm = sem("neg_max_spread")
        s_wi = sem("inter_weights_spread")
        s_wie = sem("inter_weights_made")
        s_w1 = sem("log_weights_made")
        s_e = sem("weights_made")
        s_s = sem("scores_done")
        s_p = sem("weighted_scores_made")
        s_qw = sem("weighted_q_made")
        s_ks = sem("weighted_k_made")
        s_nd = sem("num_den_done")
        s_nde = sem("num_den_evacuated")
        s_u = sem("state_update_done")
        s_st = sem("state_made")
        s_h = sem("h_made")
        s_hsq = sem("h_squares_made")
        s_hss = sem("h_squares_summed")
        s_hr = sem("h_rstd_made")
        s_csum = sem("conv_sum_done")
        s_cmu = sem("conv_mean_made")
        s_cd = sem("conv_centred")
        s_csq = sem("conv_squares_made")
        s_cvar = sem("conv_var_done")
        s_crs = sem("conv_rstd_made")
        s_cl = sem("conv_normed")
        s_cta = sem("conv_tanh_made")
        s_yf = sem("mixer_output_made")
        s_yh = sem("mixer_output_upper_made")
        s_y = sem("mixer_output_split")
        s_hf = sem("hidden_made")
        s_hh = sem("hidden_upper_made")
        s_out = sem("output_stored")

        def split_weights(pool, s, dyn=0, k=KT):
            pool.wait_ge(s_raw[s % RING], 16 * (s // RING + 1) + 4 * dyn)
            if s >= 2:
                pool.wait_ge(s_tile, s - 1 + dyn)
            pool.tensor_tensor(word[:, 0:1], ones[:, 0:1], ones[:, 0:1], ALU.mult)
            src = raw[s % RING][:, 0:k * P].rearrange("p (k c) -> p k c", c=P)
            hi, lo = w_hi[s % 2][:, 0:k, :], w_lo[s % 2][:, 0:k, :]
            pool.tensor_scalar(hi, src, 1.0, 0.0, ALU.mult, ALU.add).then_inc(s_hi, 1)
            pool.wait_ge(s_hi, s + 1 + dyn)
            pool.tensor_tensor(lo, src, hi.bitcast(FP32), ALU.subtract).then_inc(s_split, 1)

        def gemm_tile(pe, s, rh, rl, w, dyn=0, k=KT):
            pe.wait_ge(s_split, s + 1 + dyn)
            if s >= 2:
                pe.wait_ge(s_evac, s - 1 + dyn)
            for i in range(k):
                hi, lo = w_hi[s % 2][:, i, :], w_lo[s % 2][:, i, :]
                for a, b in ranges(w):
                    pe.matmul(acc(s)[:, a:b], hi, rh[:, i, a:b], start=i == 0, stop=False)
                    pe.matmul(acc(s)[:, a:b], hi, rl[:, i, a:b], start=False, stop=False)
                for a, b in ranges(w):
                    last = pe.matmul(acc(s)[:, a:b], lo, rh[:, i, a:b], start=False, stop=i == k - 1)
            last.then_inc(s_tile, 1)


        b2_at = addr_of["tri"]
        cursor[0] = b2_at
        B2 = place("B2", [P, 4 * 768 + 2 * SEQ + 4 * KT + AH])
        amask = B2[:, 0:4 * 768].rearrange("p (r s) -> p r s", r=4)
        ropet = B2[:, 4 * 768:4 * 768 + 2 * SEQ].rearrange("p (a t) -> p a t", a=2)
        lnp = B2[:, 4 * 768 + 2 * SEQ:4 * 768 + 2 * SEQ + 4 * KT].rearrange("p (l a k) -> p l a k", l=DEPTH, a=2)
        sink = B2[:, 4 * 768 + 2 * SEQ + 4 * KT:]
        bmask = place("bmask", [P, 7 * P], addr=addr_of["B2"])
        KB = place("KB", [P, 2, SEQ], addr=addr_of["B2"] + 7 * P * 4)
        YH2 = place("YH2", [P, KT, SEQ], FP32R)
        YL2 = place("YL2", [P, KT, SEQ], FP32R)
        VT = place("VT", [P, 3, NX, P])
        SM = [place(f"SM{i}", [P, 7 * P]) for i in range(2)]
        PT = [place(f"PT{i}", [P, 7, P]) for i in range(2)]
        ZS = place("ZS", [P, SEQ])
        PH = place("PH", [P, 2, SEQ], FP32R)
        PL = place("PL", [P, 2, SEQ], FP32R)
        smax = place("smax", [P, 2, 4])
        ssum = place("ssum", [P, 2, 4])
        esink = place("esink", [P, 2, 4])
        X2 = place("X2", [P, KT, SEQ], addr=addr_of["XH"])
        XH2 = place("XH2", [P, KT, SEQ], FP32R, addr=addr_of["XH"] + KT * SEQ * 4)
        XL2 = place("XL2", [P, KT, SEQ], FP32R, addr=addr_of["XH"] + 2 * KT * SEQ * 4)
        QK = place("QK", [P, 6, SEQ], addr=addr_of["X"])
        QS = place("QS", [P, 6, SEQ], addr=addr_of["X"] + 6 * SEQ * 4)
        Praw = place("Praw", [P, 2, SEQ], addr=addr_of["QS"])

        s_b2 = sem("second_block_constants_loaded")
        s_bm = sem("mixer_b_mask_loaded")
        s_swp = sem("rope_halves_swapped")
        s_rope = sem("rope_applied")
        s_sc = sem("attention_scores_done")
        s_sm = sem("attention_scores_masked")
        s_ex = sem("attention_exp_made")
        s_pn = sem("attention_probabilities_made")
        s_pt = sem("attention_probabilities_transposed")
        s_pte = sem("attention_probabilities_evacuated")
        s_pv = sem("attention_values_done")
        s_ao = sem("attention_output_made")
        s_praw = sem("p_loaded")
        s_ph = sem("p_upper_made")
        s_pl = sem("p_split")
        s_lsum = sem("ln_sum_done")
        s_mu = sem("ln_mean_made")
        s_lnd = sem("ln_centred")

        def head_pairs(eng, mixer):
            if mixer == "a":
                with eng.Fori(0, HP // 2) as i:
                    for e in range(2):
                        yield e, 2 * i, None
            else:
                for kv in range(2):
                    with eng.Fori(0, HP // 4) as i:
                        for e in range(2):
                            yield 4 * kv + e, 2 * i, kv

        def steps_of(mixer):
            return 2 * NX if mixer == "a" else 2

        def step0(mixer, hp):
            return 8 * hp if mixer == "a" else 8 * HP + 2 * hp

        def sc_banks(st):
            return banks(4 + 2 * (st % 2), 6 + 2 * (st % 2))

        def second_sp(sp, load, tile_of):
            sp.wait_ge(s_xl, KT * 5)
            sp.dma_start(B2[:], b2_d).then_inc(s_b2, 16)
            with sp.Fori(0, HP // 2) as i:
                for t in range(2 * A_TILES):
                    load(N_A + t, tile_of(wa_d, 2 * A_TILES * i + t), 2 * A_TILES * i)

            def eight(s, w):
                with sp.Fori(0, 2) as i:
                    for u in range(4):
                        load(s + u, tile_of(w, 4 * i + u), 4 * i)

            def ple(l):
                sp.wait_ge(s_rope, HP * (l + 1) + l)
                sp.dma_start(Praw[:], p_d[l]).then_inc(s_praw, 16)
                with sp.Fori(0, 4) as i:
                    for u in range(2):
                        load(N_PLE[l] + 2 * u, tile_of(pleg_d[l], 2 * i + u), 4 * i)
                        load(N_PLE[l] + 2 * u + 1, tile_of(plep_d[l], 2 * i + u), 4 * i, 2 * P)
            eight(N_AOUT, wao_d)
            ple(0)
            sp.wait_ge(s_sm, 8 * HP)
            sp.dma_start(bmask[:], bmask_d).then_inc(s_bm, 16)
            for t in range(3):
                load(N_B + t, wbk_d[t])
            for kv in range(2):
                with sp.Fori(0, HP // 4) as i:
                    for u in range(4):
                        load(N_BQZ + 8 * kv + u, tile_of(wbqz_d, 4 * i + 8 * kv + u), 4 * i)
            eight(N_BOUT, wbo_d)
            ple(1)
            sp.wait_ge(s_used, used(N_ALL - 1))
            sp.dma_start(out_d, X2[:]).then_inc(s_out, 16)
            sp.wait_ge(s_out, 16)

        def second_pool(pool):
            def eight(s):
                with pool.Fori(0, 2) as i:
                    for u in range(4):
                        split_weights(pool, s + u, 4 * i)

            def ple(l):
                with pool.Fori(0, 4) as i:
                    for u in range(2):
                        split_weights(pool, N_PLE[l] + 2 * u, 4 * i)
                        split_weights(pool, N_PLE[l] + 2 * u + 1, 4 * i, 2)
            with pool.Fori(0, HP // 2) as i:
                for t in range(2 * A_TILES):
                    split_weights(pool, N_A + t, 2 * A_TILES * i)
            eight(N_AOUT)
            ple(0)
            for t in range(3):
                split_weights(pool, N_B + t)
            for kv in range(2):
                with pool.Fori(0, HP // 4) as i:
                    for u in range(4):
                        split_weights(pool, N_BQZ + 8 * kv + u, 4 * i)
            eight(N_BOUT)
            ple(1)

        def second_pe(pe, norm):
            def transpose_v(event, dyn, src, strided):
                pe.wait_ge(s_tre, event + dyn)
                for j in range(NX):
                    part = src[:, j:SEQ:4] if strided else src[:, j * P:(j + 1) * P]
                    last = pe.transpose(PS[:, 4, j * P:(j + 1) * P], part, ident[:])
                last.then_inc(s_tr, 1)

            def attention(mixer, e, dyn, kv, tiles):
                n = steps_of(mixer)
                c0, cd = step0(mixer, e), n * dyn
                hp = e + (0 if mixer == "a" else HP)
                pe.wait_ge(s_rope, HP * (mixer == "b") + (mixer == "b") + e + 1 + dyn)
                pe.wait_ge(s_evac, tiles[0] + tiles[1])
                pe.wait_ge(s_tre, (20 + 3 * (e + 1) if mixer == "a" else 20 + 3 * HP + 1) + (3 * dyn if mixer == "a" else 0))

                def scores(st):
                    c = c0 + st
                    if c >= 2:
                        pe.wait_ge(s_sm, c - 1 + cd)
                    sc = sc_banks(st)
                    if mixer == "a":
                        h, r = 64 * (st // NX), st % NX
                        pe.matmul(sc[:, 0:SEQ], QK[h:h + 64, 0, r:SEQ:4], QK[h:h + 64, 1, :], start=True, stop=True)
                        for g in (1, 2):
                            last = pe.matmul(sc[:, SEQ + (g - 1) * P:SEQ + g * P], QK[h:h + 64, 2 * g, r:SEQ:4],
                                             QK[h:h + 64, 2 * g + 1, r:SEQ:4], start=True, stop=True)
                    else:
                        h = 64 * st
                        for b in range(NX):
                            a = max(b - 1, 0) * P
                            at = 2 * P * b + (P if b == 0 else 0)
                            last = pe.matmul(sc[:, at:2 * P * (b + 1)], QK[h:h + 64, 0, b * P:(b + 1) * P],
                                             KB[h:h + 64, kv, a:(b + 1) * P], start=True, stop=True)
                    last.then_inc(s_sc, 1)

                def values(st):
                    c = c0 + st
                    pe.wait_ge(s_pn, c + 1 + cd)
                    if c:
                        pe.wait_ge(s_pte, c + cd)
                    nb = 6 if mixer == "a" else 7
                    for b in range(nb):
                        last = pe.transpose(banks(0, 2)[:, b * P:(b + 1) * P], SM[st % 2][:, b * P:(b + 1) * P], ident[:])
                    last.then_inc(s_pt, 1)
                    pe.wait_ge(s_pte, c + 1 + cd)
                    if st == 0 and hp:
                        pe.wait_ge(s_ao, hp + dyn)
                    pt = PT[st % 2]
                    if mixer == "a":
                        h, r = 64 * (st // NX), st % NX
                        for b in range(6):
                            g, blk = (0, b) if b < NX else (b - NX + 1, r)
                            last = pe.matmul(PS[h:h + 64, 2, r:SEQ:4], VT[:, g, blk, h:h + 64], pt[:, b, :], start=b == 0, stop=b == 5)
                    else:
                        h = 64 * st
                        for b in range(NX):
                            blocks = [(2 * b - 1, b - 1), (2 * b, b)] if b else [(0, 0)]
                            for m, (src, blk) in enumerate(blocks):
                                last = pe.matmul(PS[h:h + 64, 2, b * P:(b + 1) * P], VT[:, 0, blk, 64 * kv:64 * kv + 64], pt[:, src, :],
                                                 start=m == 0, stop=m == len(blocks) - 1)
                    last.then_inc(s_pv, 1)
                scores(0)
                for st in range(n):
                    if st + 1 < n:
                        scores(st + 1)
                    values(st)
                pe.wait_ge(s_ao, hp + 1 + dyn)

            def eight(s):
                with pe.Fori(0, 2) as i:
                    for u in range(4):
                        gemm_tile(pe, s + u, YH2, YL2, SEQ, 4 * i)

            def layer_norm(l):
                pe.wait_ge(s_used, used(N_PLE[l] - 1))
                for k in range(KT):
                    last = pe.matmul(PS[:, 6, :], ones[:], X2[:, k, :], start=k == 0, stop=k == KT - 1)
                last.then_inc(s_lsum, 1)
                norm(5 + l, SEQ)

            def ple(l):
                pe.wait_ge(s_xl, KT * (6 + 2 * l))
                pe.wait_ge(s_pl, l + 1)
                with pe.Fori(0, 4) as i:
                    for u in range(2):
                        gemm_tile(pe, N_PLE[l] + 2 * u, XH2, XL2, SEQ, 4 * i)
                        gemm_tile(pe, N_PLE[l] + 2 * u + 1, PH, PL, SEQ, 4 * i, 2)

            pe.wait_ge(s_xl, KT * 5)
            for e, dyn, _ in head_pairs(pe, "a"):
                n = N_A + A_TILES * e
                for t in range(A_TILES):
                    gemm_tile(pe, n + t, XH2, XL2, SEQ, A_TILES * dyn)
                    if t >= 7:
                        g = t - 7
                        pe.wait_ge(s_evac, n + t + A_TILES * dyn)
                        transpose_v(20 + 3 * e + g, 3 * dyn, Z[:, (n + t - 1) % 4, 0:SEQ], g > 0)
                attention("a", e, dyn, None, (n + A_TILES, A_TILES * dyn))
            pe.wait_ge(s_y, KT * 3)
            eight(N_AOUT)
            layer_norm(0)
            ple(0)
            pe.wait_ge(s_xl, KT * 7)
            for t in range(3):
                gemm_tile(pe, N_B + t, XH2, XL2, SEQ)
            pe.wait_ge(s_evac, N_B + 3)
            transpose_v(20 + 3 * HP, 0, Z[:, (N_B + 2) % 4, 0:SEQ], False)
            for e, dyn, kv in head_pairs(pe, "b"):
                n = N_BQZ + 2 * e
                for t in range(2):
                    gemm_tile(pe, n + t, XH2, XL2, SEQ, 2 * dyn)
                attention("b", e, dyn, kv, (n + 2, 2 * dyn))
            pe.wait_ge(s_y, KT * 4)
            eight(N_BOUT)
            layer_norm(1)
            ple(1)

        def second_act(act, link, rstd, evacuate):
            def swap(dst, src, wait_tile, dyn):
                act.wait_ge(s_evac, wait_tile + dyn)
                for q in range(4):
                    act.dma_start(dst[32 * (q ^ 1):32 * (q ^ 1) + 32], src[32 * q:32 * q + 32]).then_inc(s_swp, 16)

            def z_tile(n, dyn, per):
                act.wait_ge(s_tile, n + 1 + dyn)
                act.wait_ge(s_used, used(n - 1) + per)
                act.activation(Z[:, n % 4, 0:SEQ], acc(n)[:, 0:SEQ], ACT.Identity)
                act.activation(TH[:, 0:SEQ], acc(n)[:, 0:SEQ], ACT.Tanh, scale=0.5).then_inc(s_evac, 1)

            def attention(mixer, e, dyn):
                n = steps_of(mixer)
                c0, cd = step0(mixer, e), n * dyn

                def exps(st):
                    c = c0 + st
                    act.wait_ge(s_sm, c + 1 + cd)
                    m = smax[:, st % 2]
                    if mixer == "a":
                        s = SM[st % 2][:, 0:768]
                        act.activation(s, s, ACT.Exp, bias=m[:, 1:2], accum_out=ssum[:, st % 2, 0:1]).then_inc(s_ex, 1)
                    else:
                        for b in range(NX):
                            s = SM[st % 2][:, max(2 * b - 1, 0) * P:(2 * b + 1) * P]
                            act.activation(s, s, ACT.Exp, bias=m[:, b:b + 1], accum_out=ssum[:, st % 2, b:b + 1])
                        head = sink[:, bass.ds(2 * e + st + 2 * dyn, 1)]
                        act.activation(esink[:, st % 2], m, ACT.Exp, bias=head).then_inc(s_ex, 1)

                def evac(st):
                    c = c0 + st
                    act.wait_ge(s_pt, c + 1 + cd)
                    if c >= 2:
                        act.wait_ge(s_pv, c - 1 + cd)
                    nb = 6 if mixer == "a" else 7
                    act.activation(PT[st % 2][:, 0:nb, :].rearrange("p b t -> p (b t)"), banks(0, 2)[:, 0:nb * P], ACT.Copy).then_inc(s_pte, 1)
                exps(0)
                for st in range(n):
                    if st + 1 < n:
                        exps(st + 1)
                    evac(st)
                hp = e + HP * (mixer == "b")
                act.wait_ge(s_ao, hp + 1 + dyn)
                act.activation(YH2[:, bass.ds(e + dyn, 1), :].rearrange("p a t -> p (a t)"), ZS[:], ACT.Copy).then_inc(s_yh, 1)

            def plain(n, dyn):
                act.wait_ge(s_tile, n + 1 + dyn)
                act.wait_ge(s_used, used(n - 4) + dyn)
                act.activation(Z[:, n % 4, 0:SEQ], acc(n)[:, 0:SEQ], ACT.Identity).then_inc(s_evac, 1)

            def eight(s):
                act.wait_ge(s_used, used(s - 1))
                with act.Fori(0, 2) as i:
                    for u in range(4):
                        plain(s + u, 4 * i)

            def split_x(q, counted):
                for k in range(KT):
                    act.wait_ge(*counted(k))
                    act.activation(XH2[:, k], X2[:, k], ACT.Copy).then_inc(s_xh, 1)
                act.wait_ge(s_xl, KT * (q + 1))

            def layer_norm(l):
                act.wait_ge(s_lsum, l + 1)
                act.activation(TH[:, 0:SEQ], PS[:, 6, :], ACT.Copy, scale=1.0 / D).then_inc(s_mu, 1)
                for k in range(KT):
                    act.wait_ge(s_lnd, KT * l + k + 1)
                    if k >= 4:
                        act.wait_ge(s_squ, KT * (5 + l) + k - 3)
                    act.activation(Z[:, k % 4, 0:SEQ], X2[:, k], ACT.Square).then_inc(s_sq, 1)
                act.wait_ge(s_squ, KT * (6 + l))
                rstd(TH[:, 0:SEQ], PS[:, 6, :], 1.0 / D, 1).then_inc(s_rstd, 1)
                split_x(5 + 2 * l, lambda k: (s_xn, KT * (5 + l) + k + 1))

            def ple(l):
                act.wait_ge(s_praw, 16 * (l + 1))
                act.activation(PH[:], Praw[:], ACT.Copy).then_inc(s_ph, 1)
                with act.Fori(0, 4) as i:
                    for u in range(2):
                        n = N_PLE[l] + 2 * u
                        act.wait_ge(s_tile, n + 1 + 4 * i)
                        act.wait_ge(s_used, used(n - 3) + 4 * i)
                        act.activation(Z[:, n % 4, 0:SEQ], acc(n)[:, 0:SEQ], ACT.Tanh, scale=0.5).then_inc(s_evac, 1)
                        act.wait_ge(s_tile, n + 2 + 4 * i)
                        act.activation(Z[:, (n + 1) % 4, 0:SEQ], acc(n + 1)[:, 0:SEQ], ACT.Identity).then_inc(s_evac, 1)

            act.wait_ge(s_used, used(N_A - 1))
            for k in range(KT):
                if k >= 4:
                    act.wait_ge(s_squ, KT * 4 + k - 3)
                act.activation(Z[:, k % 4, 0:SEQ], X[:, k, 0:SEQ], ACT.Square).then_inc(s_sq, 1)
            act.wait_ge(s_squ, KT * 5)
            rstd(TH[:, 0:SEQ], PS[:, 6, :], 1.0 / D).then_inc(s_rstd, 1)
            split_x(4, lambda k: (s_xn, KT * 4 + k + 1))
            for e, dyn, _ in head_pairs(act, "a"):
                n = N_A + A_TILES * e
                for t in range(6):
                    act.wait_ge(s_tile, n + t + 1 + A_TILES * dyn)
                    act.activation(QK[:, t], acc(n + t)[:, 0:SEQ], ACT.Identity).then_inc(s_evac, 1)
                swap(QS, QK, n + 6, A_TILES * dyn)
                for t in range(6, 9):
                    act.wait_ge(s_tile, n + t + 1 + A_TILES * dyn)
                    if t == 6:
                        act.wait_ge(s_used, used(n - 1) + dyn)
                        act.wait_ge(s_tre, 20 + 3 * e + 3 * dyn)
                    act.activation(Z[:, (n + t) % 4, 0:SEQ], acc(n + t)[:, 0:SEQ], ACT.Identity).then_inc(s_evac, 1)
                z_tile(n + 9, A_TILES * dyn, dyn)
                attention("a", e, dyn)
            eight(N_AOUT)
            layer_norm(0)
            ple(0)
            act.wait_ge(s_tile, N_B)
            split_x(6, lambda k: (s_used, used(N_PLE[0] + 2 * k + 1)))
            act.wait_ge(s_bm, 16)
            for t in range(2):
                act.wait_ge(s_tile, N_B + t + 1)
                act.activation(KB[:, t], acc(N_B + t)[:, 0:SEQ], ACT.Identity).then_inc(s_evac, 1)
            swap(QS[:, 0:2], KB, N_B + 2, 0)
            act.wait_ge(s_tile, N_B + 3)
            act.activation(Z[:, (N_B + 2) % 4, 0:SEQ], acc(N_B + 2)[:, 0:SEQ], ACT.Identity).then_inc(s_evac, 1)
            act.wait_ge(s_tre, 20 + 3 * HP + 1)
            for e, dyn, kv in head_pairs(act, "b"):
                n = N_BQZ + 2 * e
                act.wait_ge(s_tile, n + 1 + 2 * dyn)
                act.activation(QK[:, 0], acc(n)[:, 0:SEQ], ACT.Identity).then_inc(s_evac, 1)
                swap(QS[:, 2], QK[:, 0], n + 1, 2 * dyn)
                z_tile(n + 1, 2 * dyn, dyn)
                attention("b", e, dyn)
            eight(N_BOUT)
            layer_norm(1)
            ple(1)

        def second_dve(dve, link, linked_loop):
            def lower(q, k):
                dve.wait_ge(s_xh, KT * q + k + 1)
                dve.tensor_tensor(XL2[:, k], X2[:, k], XH2[:, k].bitcast(FP32), ALU.subtract).then_inc(s_xl, 1)

            def rope(x, xs, n, link_in, count):
                dve.wait_ge(s_swp, count)
                cos, sin = (ropet[:, i:i + 1].to_broadcast([P, n, SEQ]) for i in range(2))
                dve.tensor_tensor(x, x, cos, ALU.mult)
                link_in(dve.tensor_tensor(xs, xs, sin, ALU.mult))
                dve.tensor_tensor(x, x, xs, ALU.add).then_inc(s_rope, 1)

            def attention(mixer, e, dyn, link_in):
                n = steps_of(mixer)
                c0, cd = step0(mixer, e), n * dyn

                def mask(st):
                    c = c0 + st
                    dve.wait_ge(s_sc, c + 1 + cd)
                    if c >= 2:
                        dve.wait_ge(s_pt, c - 1 + cd)
                    dve.tensor_tensor(word[:, 1:2], ones[:, 0:1], ones[:, 0:1], ALU.mult)
                    m = smax[:, st % 2]
                    if mixer == "a":
                        link_in(dve.tensor_tensor_reduce(out=SM[st % 2][:, 0:768], in0=sc_banks(st)[:, 0:768], in1=amask[:, st % NX, :],
                                                         scale=A_SCALE, scalar=NEG, op0=ALU.add, op1=ALU.max, accum_out=m[:, 0:1]))
                        dve.tensor_scalar(m[:, 1:2], m[:, 0:1], -1.0, 0.0, ALU.mult, ALU.add).then_inc(s_sm, 1)
                    else:
                        for b in range(NX):
                            a, z = max(2 * b - 1, 0) * P, (2 * b + 1) * P
                            last = dve.tensor_tensor_reduce(out=SM[st % 2][:, a:z], in0=sc_banks(st)[:, a + P:z + P], in1=bmask[:, a:z],
                                                            scale=A_SCALE, scalar=NEG, op0=ALU.add, op1=ALU.max, accum_out=m[:, b:b + 1])
                        link_in(last)
                        head = sink[:, bass.ds(2 * e + st + 2 * dyn, 1)]
                        dve.tensor_scalar(m, m, head, -1.0, ALU.max, ALU.mult).then_inc(s_sm, 1)

                def normalise(st):
                    c = c0 + st
                    dve.wait_ge(s_ex, c + 1 + cd)
                    s = ssum[:, st % 2]
                    if mixer == "a":
                        link_in(dve.reciprocal(s[:, 1:2], s[:, 0:1]))
                        dve.tensor_scalar(SM[st % 2][:, 0:768], SM[st % 2][:, 0:768], s[:, 1:2], None, ALU.mult).then_inc(s_pn, 1)
                    else:
                        link_in(dve.tensor_tensor(s, s, esink[:, st % 2], ALU.add))
                        link_in(dve.reciprocal(s, s))
                        for b in range(NX):
                            a, z = max(2 * b - 1, 0) * P, (2 * b + 1) * P
                            last = dve.tensor_scalar(SM[st % 2][:, a:z], SM[st % 2][:, a:z], s[:, b:b + 1], None, ALU.mult)
                        last.then_inc(s_pn, 1)
                mask(0)
                for st in range(n):
                    if st + 1 < n:
                        mask(st + 1)
                    normalise(st)
                hp = e + HP * (mixer == "b")
                dve.wait_ge(s_pv, c0 + n + cd)
                dve.scalar_tensor_tensor(out=ZS[:], in0=PS[:, 2, :], scalar=0.5, in1=ZS[:], op0=ALU.mult, op1=ALU.mult).then_inc(s_ao, 1)
                dve.wait_ge(s_yh, 16 + hp + 1 + dyn)
                at = bass.ds(e + dyn, 1)
                dve.tensor_tensor(YL2[:, at, :].rearrange("p a t -> p (a t)"), ZS[:],
                                  YH2[:, at, :].rearrange("p a t -> p (a t)").bitcast(FP32), ALU.subtract).then_inc(s_y, 1)
                return hp

            def z_gate(n, ndyn, hp, dyn):
                dve.wait_ge(s_evac, n + 1 + ndyn)
                dve.wait_ge(s_y, 16 + hp + dyn)
                dve.scalar_tensor_tensor(out=ZS[:], in0=TH[:, 0:SEQ], scalar=1.0, in1=Z[:, n % 4, 0:SEQ],
                                         op0=ALU.add, op1=ALU.mult).then_inc(s_used, 1)
                dve.wait_ge(s_used, used(n) + dyn)

            def pair_loop(mixer, per, body):
                for kv in range(2 if mixer == "b" else 1):
                    linked_loop(HP // 4 if mixer == "b" else HP // 2, 2 * per,
                                lambda i, link_in: [body(4 * kv + e, 2 * i, link_in) for e in range(2)])

            def eight(s):
                with dve.Fori(0, 2) as i:
                    for u in range(4):
                        dve.wait_ge(s_evac, s + u + 1 + 4 * i)
                        x = X2[:, bass.ds(u + 4 * i, 1), :].rearrange("p a t -> p (a t)")
                        dve.scalar_tensor_tensor(out=x, in0=x, scalar=ALPHA, in1=Z[:, (s + u) % 4, 0:SEQ],
                                                 op0=ALU.mult, op1=ALU.add).then_inc(s_used, 1)

            def layer_norm(l):
                dve.wait_ge(s_mu, l + 1)
                for k in range(KT):
                    dve.tensor_tensor(X2[:, k], X2[:, k], TH[:, 0:SEQ], ALU.subtract).then_inc(s_lnd, 1)
                dve.wait_ge(s_rstd, 6 + l)

                def upper(k):
                    link(dve.tensor_tensor(X2[:, k], X2[:, k], TH[:, 0:SEQ], ALU.mult))
                    dve.tensor_scalar(X2[:, k], X2[:, k], lnp[:, l, 0, k:k + 1], lnp[:, l, 1, k:k + 1], ALU.mult, ALU.add).then_inc(s_xn, 1)
                upper(0)
                for k in range(1, KT):
                    upper(k)
                    lower(5 + 2 * l, k - 1)
                lower(5 + 2 * l, KT - 1)

            def ple(l):
                dve.wait_ge(s_ph, l + 1)
                dve.tensor_tensor(PL[:], Praw[:], PH[:].bitcast(FP32), ALU.subtract).then_inc(s_pl, 1)

                def body(i, link_in):
                    for u in range(2):
                        n = N_PLE[l] + 2 * u
                        g, v = Z[:, n % 4, 0:SEQ], Z[:, (n + 1) % 4, 0:SEQ]
                        dve.wait_ge(s_evac, n + 2 + 4 * i)
                        link_in(dve.scalar_tensor_tensor(out=g, in0=g, scalar=1.0, in1=v, op0=ALU.add, op1=ALU.mult))
                        x = X2[:, bass.ds(u + 2 * i, 1), :].rearrange("p a t -> p (a t)")
                        dve.scalar_tensor_tensor(out=x, in0=g, scalar=0.5, in1=x, op0=ALU.mult, op1=ALU.add).then_inc(s_used, 2)
                linked_loop(4, 2, body)

            dve.wait_ge(s_rstd, 5)

            def upper(k):
                if k >= 4:
                    dve.wait_ge(s_xn, KT * 4 + k - 3)
                z = Z[:, k % 4, 0:SEQ]
                link(dve.tensor_tensor(z, X[:, k, 0:SEQ], TH[:, 0:SEQ], ALU.mult))
                dve.tensor_scalar(X2[:, k], z, fin_g[:, k:k + 1], None, ALU.mult).then_inc(s_xn, 1)
            upper(0)
            for k in range(1, KT):
                upper(k)
                lower(4, k - 1)
            lower(4, KT - 1)
            dve.wait_ge(s_b2, 16)

            def pair_a(e, dyn, link_in):
                n = N_A + A_TILES * e
                rope(QK[:], QS[:], 6, link_in, 64 * (e + 1) + 64 * dyn)
                for g in range(3):
                    dve.wait_ge(s_tr, 20 + 3 * e + g + 1 + 3 * dyn)
                    dve.tensor_copy(VT[:, g].rearrange("p j d -> p (j d)"), PS[:, 4, :]).then_inc(s_tre, 1)
                z_gate(n + 9, A_TILES * dyn, e, dyn)
                attention("a", e, dyn, link_in)

            def pair_b(e, dyn, link_in):
                n = N_BQZ + 2 * e
                rope(QK[:, 0:1], QS[:, 2:3], 1, link_in, 64 * (HP + 1 + e + 1) + 64 * dyn)
                z_gate(n + 1, 2 * dyn, HP + e, dyn)
                attention("b", e, dyn, link_in)
            pair_loop("a", 1 + 8 * 2, pair_a)
            eight(N_AOUT)
            layer_norm(0)
            ple(0)
            for k in range(KT):
                lower(6, k)
            dve.wait_ge(s_bm, 16)
            rope(KB[:], QS[:, 0:2], 2, link, 64 * (HP + 1))
            dve.wait_ge(s_tr, 20 + 3 * HP + 1)
            dve.tensor_copy(VT[:, 0].rearrange("p j d -> p (j d)"), PS[:, 4, :]).then_inc(s_tre, 1)
            pair_loop("b", 1 + 2 * 3, pair_b)
            eight(N_BOUT)
            layer_norm(1)
            ple(1)

        block = stack.enter_context(nc.Block())

        @block.sync
        def _(sp):
            sp.dma_start(cact[:], cT).then_inc(s_const, 16)
            sp.dma_start(ident[:], consts_d[:, 0:P]).then_inc(s_const, 16)
            sp.dma_start(tri[:].rearrange("p a b -> p (a b)"), consts_d[:, P:3 * P]).then_inc(s_const, 16)
            sp.dma_start(mskd[:].rearrange("p a b -> p (a b)"), consts_d[:, 3 * P:5 * P]).then_inc(s_const, 16)
            sp.dma_start(dsel[:], consts_d[0:8, 5 * P:5 * P + 2]).then_inc(s_const, 16)
            sp.dma_start(pc[:], pc_d).then_inc(s_const, 16)
            sp.dma_start(fin_g[:], fin_d).then_inc(s_const, 16)
            sp.dma_start(X[:], xT).then_inc(s_const, 16)

            def load(s, src, dyn=0, cols=KT * P):
                if s >= RING:
                    sp.wait_ge(s_split, s - RING + 1 + dyn)
                sp.dma_start(raw[s % RING][:, 0:cols], src).then_inc(s_raw[s % RING], 16)

            def tile_of(w, i):
                return w[bass.ds(i, 1)].rearrange("a p n -> (a p) n")

            for l in range(DEPTH):
                n0 = l * LAYER_TILES
                if l:
                    sp.wait_ge(s_tile, n0)
                    sp.wait_ge(s_used, used(n0 - 1))
                sp.dma_start(srow[:], srow_d[l]).then_inc(s_par, 16)
                sp.dma_start(sgw[:], sguw_d[l]).then_inc(s_par, 16)
                sp.dma_start(wg[:], wg_d[l]).then_inc(s_par, 16)
                for u in range(8):
                    sp.dma_start(modw[u][:].rearrange("p a k c -> p (a k c)"), wmod_d[l, u]).then_inc(s_modw[u], 16)
                with sp.Fori(1, 3) as i:
                    for u in range(8):
                        sp.wait_ge(s_modd, 24 * l + 8 * i)
                        sp.dma_start(modw[u][:].rearrange("p a k c -> p (a k c)"),
                                     tile_of(wmod_d[l], 8 * i + u)).then_inc(s_modw[u], 16)
                for n in range(N_IN):
                    load(n0 + n, win_d[l, n])
                with sp.Fori(0, 2) as i:
                    for u in range(4):
                        load(n0 + N_IN + u, tile_of(wout_d[l], 4 * i + u), 4 * i)
                for p, (h0, hn) in enumerate(PARTS):
                    s = part_start(l, p)
                    with sp.Fori(0, 2 * hn // 4) as i:
                        for u in range(4):
                            load(s + u, tile_of(wgu_d[l], 4 * i + 2 * h0 + u), 4 * i)
                    with sp.Fori(0, 2) as i:
                        for u in range(4):
                            load(s + 2 * hn + u, tile_of(wdn_d[l, :, :, h0 * P:(h0 + hn) * P], 4 * i + u), 4 * i, hn * P)
            second_sp(sp, load, tile_of)

        @block.gpsimd
        def _(pool):
            pool.memset(ones[:], 1.0).then_inc(s_one, 1)
            pool.memset(eps_c[:, 0:1], EPS).then_inc(s_one, 1)
            pool.memset(eps_c[:, 1:2], LN_EPS).then_inc(s_one, 1)
            pool.wait_ge(s_one, 3)
            for l in range(DEPTH):
                n0 = l * LAYER_TILES
                for n in range(N_IN):
                    split_weights(pool, n0 + n)
                for t, (d, j, first, gives) in enumerate(mlstm_steps(l)):
                    c = 2 * NJ * l + t
                    o = outputs_before(l, t)
                    if gives and not first:
                        pool.wait_ge(s_wie, c + 1)
                        if o:
                            pool.wait_ge(s_nd, o)
                        pool.tensor_tensor(Qw[:], qfm[:, :, j * P:(j + 1) * P], WIs[:], ALU.mult).then_inc(s_qw, 1)
                    pool.wait_ge(s_e, c + 1)
                    if c:
                        pool.wait_ge(s_u, c)
                    tl = P - 1 if d == 0 else 0
                    pool.tensor_tensor(Ks[:], ktm[:, j, :, :], Ee[:, :, tl:tl + 1].to_broadcast([P, HEADS, P]),
                                       ALU.mult).then_inc(s_ks, 1)
                with pool.Fori(0, 2) as i:
                    for u in range(4):
                        split_weights(pool, n0 + N_IN + u, 4 * i)
                for p, (h0, hn) in enumerate(PARTS):
                    s = part_start(l, p)
                    with pool.Fori(0, 2 * hn // 4) as i:
                        for u in range(4):
                            split_weights(pool, s + u, 4 * i)
                    with pool.Fori(0, 2) as i:
                        for u in range(4):
                            split_weights(pool, s + 2 * hn + u, 4 * i, hn)
            second_pool(pool)

        @block.tensor
        def _(pe):
            def norm(q, w):
                for k in range(KT):
                    pe.wait_ge(s_sq, KT * q + k + 1)
                    for a, b in ranges(w):
                        last = pe.matmul(banks(6, 8)[:, a:b], ones[:], Z[:, k % 4, a:b], start=k == 0, stop=k == KT - 1)
                    last.then_inc(s_squ, 1)

            def transpose_tile(l, e, src, nj):
                if 10 * l + e:
                    pe.wait_ge(s_tre, 10 * l + e)
                for j in range(nj):
                    last = pe.transpose(banks(4, 6)[:, j * P:(j + 1) * P], src[:, j * P:(j + 1) * P], ident[:])
                last.then_inc(s_tr, 1)

            def sgu_mix(l, f):
                pe.wait_ge(s_svt, l + 1)
                if 2 * l + f:
                    pe.wait_ge(s_mixu, 2 * l + f)
                for j in range(width(l) // P):
                    for g in range(2):
                        c = f * P + g * 64
                        last = pe.matmul(banks(6, 8)[64 * g:64 * g + 64, j * P:(j + 1) * P], SVT[:, j, c:c + 64],
                                         sgw[:, 2 * f + g, :], start=True, stop=True)
                last.then_inc(s_mix, 1)

            def mlstm(l):
                n_end = l * LAYER_TILES + N_IN
                pe.wait_ge(s_wgl, l + 1)
                pe.wait_ge(s_tre, 10 * (l + 1))
                for j in range(NJ):
                    for k in range(KT):
                        xh, xl = XH[:, k, j * P:(j + 1) * P], XL[:, k, j * P:(j + 1) * P]
                        out = banks(4, 5)[:, 16 * j:16 * j + 16]
                        pe.matmul(out, xh, wgh[:, k, :], start=k == 0, stop=False)
                        pe.matmul(out, xh, wgl[:, k, :], start=False, stop=False)
                        last = pe.matmul(out, xl, wgh[:, k, :], start=False, stop=k == KT - 1)
                last.then_inc(s_gate, 1)
                pe.wait_ge(s_lf, l + 1)
                for d in range(2):
                    out = banks(5, 6)[:, 0:NJ * 8].rearrange("p (j e) -> p j e", e=8)[:, :, 4 * d:4 * d + 4]
                    last = pe.matmul(out, tri[:, d, :], lf[:, 2, :, 4 * d:4 * d + 4], start=True, stop=True)
                last.then_inc(s_bt, 1)
                pe.wait_ge(s_btm, l + 1)
                pe.wait_ge(s_evac, n_end)
                for i, src in enumerate((lf[:, 1], lf[:, 2], btm[:])):
                    for j in range(NJ):
                        c = i * T + j * P
                        last = pe.transpose(banks(0, 5)[0:8, c:c + P], src[:, j, :], ident[:])
                last.then_inc(s_rows, 1)
                pe.wait_ge(s_rowl, 3 * (l + 1))

                def spread(bank, i, d, j):
                    for h in range(HEADS):
                        r = 4 * d + h
                        out = PS[:, bank, h * P:(h + 1) * P]
                        pe.matmul(out, selh[:, r, :], rhl[i][0][:, j * P:(j + 1) * P], start=True, stop=False)
                        last = pe.matmul(out, selh[:, r, :], rhl[i][1][:, j * P:(j + 1) * P], start=False, stop=True)
                    return last

                for t, (d, j, first, gives) in enumerate(mlstm_steps(l)):
                    c = 2 * NJ * l + t
                    o = outputs_before(l, t)
                    js = slice(j * P, (j + 1) * P)
                    if c:
                        pe.wait_ge(s_w1, c)
                    spread(0, 0, d, j).then_inc(s_nm, 1)
                    if c:
                        pe.wait_ge(s_wie, c)
                    last = spread(1, 1, d, j)
                    if gives:
                        last = spread(2, 2, d, j)
                    last.then_inc(s_wi, 1)
                    if gives:
                        if o:
                            pe.wait_ge(s_p, o)
                        for h in range(HEADS):
                            last = pe.matmul(PS[:, 3, h * P:(h + 1) * P], kfm[:, h, js], qfm[:, h, js], start=True, stop=True)
                        last.then_inc(s_s, 1)
                        pe.wait_ge(s_p, o + 1)
                        if o:
                            pe.wait_ge(s_nde, o)
                        if not first:
                            pe.wait_ge(s_qw, weighted_before(l, t) + 1)
                            pe.wait_ge(s_st, c - 1)
                        for h in range(HEADS):
                            last = pe.matmul(PS[:, 4, h * P:(h + 1) * P], vtm[:, j, h, :], Pp[:, h, :], start=True, stop=first)
                            if not first:
                                last = pe.matmul(PS[:, 4, h * P:(h + 1) * P], ST[d][:, h, 0, :], Qw[:, h, :], start=False, stop=True)
                        for h in range(HEADS):
                            last = pe.matmul(PS[:, 5, h * P:(h + 1) * P], ones[:], Pp[:, h, :], start=True, stop=first)
                            if not first:
                                last = pe.matmul(PS[:, 5, h * P:(h + 1) * P], ST[d][:, h, 1, :], Qw[:, h, :], start=False, stop=True)
                        last.then_inc(s_nd, 1)
                    pe.wait_ge(s_ks, c + 1)
                    if c:
                        pe.wait_ge(s_st, c)
                    for h in range(HEADS):
                        out = banks(6, 8)[:, 2 * h * P:2 * (h + 1) * P]
                        pe.matmul(out[:, 0:P], Ks[:, h, :], vtm[:, j, h, :], start=True, stop=True)
                        last = pe.matmul(out[:, P:2 * P], Ks[:, h, :], ones[:], start=True, stop=True)
                    last.then_inc(s_u, 1)

            def mixer_stats(l):
                w = width(l)
                for h in range(HEADS):
                    pe.wait_ge(s_hsq, 4 * l + h + 1)
                    for a, b in ranges(w):
                        last = pe.matmul(banks(2 * h, 2 * h + 2)[:, a:b], ones[:], Z[:, h, a:b], start=True, stop=True)
                    last.then_inc(s_hss, 1)
                pe.wait_ge(s_hr, l + 1)
                for f in range(2):
                    for a, b in ranges(w):
                        last = pe.matmul(banks(0, 2)[:, a:b], ones[:], AC[:, f, a:b], start=f == 0, stop=f == 1)
                last.then_inc(s_csum, 1)
                pe.wait_ge(s_csq, l + 1)
                for f in range(2):
                    for a, b in ranges(w):
                        last = pe.matmul(banks(2, 4)[:, a:b], ones[:], Z[:, f, a:b], start=f == 0, stop=f == 1)
                last.then_inc(s_cvar, 1)

            pe.wait_ge(s_one, 3)
            pe.wait_ge(s_const, 16 * 8)
            for l in range(DEPTH):
                n0 = l * LAYER_TILES
                pe.wait_ge(s_cact, 1)
                with pe.Fori(0, 3) as i:
                    for u in range(8):
                        pe.wait_ge(s_modw[u], 48 * l + 16 + 16 * i)
                        for a in range(2):
                            for k in range(KT):
                                last = pe.matmul(PS[:, 5, bass.ds(32 * i + 4 * u + 2 * a, 2)], modw[u][:, a, k, :],
                                                 cact[:, k, :], start=k == 0, stop=k == KT - 1)
                        last.then_inc(s_modd, 1)
                norm(2 * l, T)
                pe.wait_ge(s_xl, KT * (2 * l + 1))
                for t in range(N_IN):
                    gemm_tile(pe, n0 + t, XH, XL, width(l, t))
                    if t in (9, 10):
                        pe.wait_ge(s_gel, 2 * l + t - 8)
                        transpose_tile(l, t - 9, Z[:, t - 9 + 2], width(l) // P)
                    if 11 <= t < 15:
                        pe.wait_ge(s_evac, n0 + t - 2)
                        transpose_tile(l, t - 9, kfm[:, t - 11], NJ)
                    if 15 <= t < 19:
                        pe.wait_ge(s_evac, n0 + t - 2)
                        transpose_tile(l, t - 9, Z[:, t - 15], NJ)
                    if t in (19, 21):
                        sgu_mix(l, (t - 19) // 2)
                mlstm(l)
                mixer_stats(l)
                pe.wait_ge(s_y, KT * (l + 1))
                with pe.Fori(0, 2) as i:
                    for u in range(4):
                        gemm_tile(pe, n0 + N_IN + u, XH, XL, width(l), 4 * i)
                norm(2 * l + 1, width(l))
                pe.wait_ge(s_xl, KT * (2 * l + 2))
                for p, (h0, hn) in enumerate(PARTS):
                    s = part_start(l, p)
                    with pe.Fori(0, 2 * hn // 4) as i:
                        for u in range(4):
                            gemm_tile(pe, s + u, XH, XL, width(l), 4 * i)
                    pe.wait_ge(s_used, used(s + 2 * hn - 1))
                    with pe.Fori(0, 2) as i:
                        for u in range(4):
                            gemm_tile(pe, s + 2 * hn + u, HH, HL, width(l), 4 * i, hn)
            norm(2 * DEPTH, SEQ)
            second_pe(pe, norm)

        @block.scalar
        def _(act):
            links = [0]

            def link(ins):
                links[0] += 1
                ins.then_inc(s_ach, 1)
                act.wait_ge(s_ach, links[0])

            def rstd(dst, src, scale, eps=0):
                link(act.activation(dst, src, ACT.Ln, bias=eps_c[:, eps:eps + 1], scale=scale))
                return act.activation(dst, dst, ACT.Exp, scale=-0.5)

            def norm(q, w, need_used):
                if need_used:
                    act.wait_ge(s_used, need_used)
                rs = MT if q in (0, 2) else TH
                for k in range(KT):
                    if k >= 4:
                        act.wait_ge(s_squ, KT * q + k - 3)
                    act.activation(Z[:, k % 4, 0:w], X[:, k, 0:w], ACT.Square).then_inc(s_sq, 1)
                act.wait_ge(s_squ, KT * (q + 1))
                rstd(rs[:, 0:w], banks(6, 8)[:, 0:w], 1.0 / D).then_inc(s_rstd, 1)
                for k in range(KT):
                    act.wait_ge(s_xn, KT * q + k + 1)
                    act.activation(XH[:, k, 0:w], Z[:, k % 4, 0:w], ACT.Copy).then_inc(s_xh, 1)
                act.wait_ge(s_xl, KT * (q + 1))

            def evacuate(s, out, func=ACT.Identity, bias=0.0, scale=1.0, w=T, dyn=0, need=None, signal=True):
                act.wait_ge(s_tile, s + 1 + dyn)
                if need is not None:
                    act.wait_ge(s_used, need)
                ins = act.activation(out, acc(s)[:, 0:w], func, bias=bias, scale=scale)
                return ins.then_inc(s_evac, 1) if signal else ins

            def residual_tiles(s0, gate, dyn, w, u):
                s = s0 + u
                act.wait_ge(s_tile, s + 1 + dyn)
                act.wait_ge(s_used, used(s - 4) + dyn)
                for n, (a, b) in enumerate(ranges(w)):
                    last = act.activation(Z[:, s % 4, a:b], acc(s)[:, a:b], ACT.Identity,
                                          scale=mod[:, bass.ds(gate + u + dyn, 1), n:n + 1].rearrange("p a b -> p (a b)"))
                last.then_inc(s_evac, 1)

            act.wait_ge(s_const, 16 * 8)
            act.wait_ge(s_one, 3)
            act.activation(cth[:], cact[:], ACT.Tanh, scale=0.5).then_inc(s_cth, 1)
            for l in range(DEPTH):
                n0 = l * LAYER_TILES
                w = width(l)
                act.wait_ge(s_par, 48 * (l + 1))
                act.activation(wgh[:], wg[:], ACT.Copy).then_inc(s_wgh, 1)
                norm(2 * l, T, used(n0 - 1))
                act.wait_ge(s_mod, l + 1)
                for t in range(N_IN):
                    n = n0 + t
                    b = bcol[:, t:t + 1]
                    slot = Z[:, n % 4, 0:w]
                    if t in (0, 2):
                        evacuate(n, slot, ACT.Tanh, b, 0.5, w)
                    elif t < K_T:
                        evacuate(n, slot, ACT.Identity, b, 1.0, w, need=used(n - 4) if t >= 4 else None)
                    elif t < V_T:
                        evacuate(n, kfm[:, t - K_T], ACT.Identity, b, K_SCALE)
                    elif t < Q_T:
                        act.wait_ge(s_tre, 10 * l + 2)
                        act.wait_ge(s_used, used(n0 + U_T + 1))
                        evacuate(n, Z[:, n % 4], ACT.Identity, b, 1.0)
                    elif t < O_T:
                        act.wait_ge(s_gel, 2 * (l + 1))
                        evacuate(n, qfm[:, t - Q_T, 0:w], ACT.Identity, b, 1.0, w)
                    else:
                        evacuate(n, tho[:, t - O_T, 0:w], ACT.Tanh, b, 0.5, w)
                    if 6 <= t < 10:
                        act.wait_ge(s_gin, 4 * l + t - 5)
                        g = GT[:, t - 6, 0:w]
                        act.activation(g, g, ACT.Tanh, scale=GELU_C).then_inc(s_gth, 1)
                    if t == 11:
                        act.wait_ge(s_svv, l + 1)
                        rstd(bmv[:, 0:w // P, 1:2], bmv[:, 0:w // P, 1:2], 1.0).then_inc(s_svr, 1)
                act.wait_ge(s_gtm, l + 1)
                sp = lf[:, 0].rearrange("p j (d h) -> p j d h", d=2)
                for j in range(NJ):
                    last = act.activation(sp[:, j], gt[:, j, :, 1, :], ACT.Abs)
                link(last)
                link(act.activation(lf[:, 0], lf[:, 0], ACT.Exp, scale=-1.0))
                act.activation(lf[:, 0], lf[:, 0], ACT.Ln, bias=1.0).then_inc(s_lfa, 1)
                act.wait_ge(s_row, l + 1)
                for i, r in enumerate((ri, rb, rf)):
                    act.activation(rhl[i][0][:], r[:], ACT.Copy).then_inc(s_rowh, 1)
                for t, (d, j, first, gives) in enumerate(mlstm_steps(l)):
                    c = 2 * NJ * l + t
                    o = outputs_before(l, t)
                    act.wait_ge(s_wi, c + 1)
                    if c:
                        act.wait_ge(s_st, c)
                    if weighted_before(l, t):
                        act.wait_ge(s_qw, weighted_before(l, t))
                    last = act.activation(WIs[:], PS[:, 1, :].rearrange("p (h t) -> p h t", h=HEADS), ACT.Exp)
                    if gives:
                        if o:
                            act.wait_ge(s_h, o)
                        last = act.activation(EMs[:], PS[:, 2, :].rearrange("p (h t) -> p h t", h=HEADS), ACT.Exp)
                    last.then_inc(s_wie, 1)
                    act.wait_ge(s_w1, c + 1)
                    if c:
                        act.wait_ge(s_ks, c)
                    if o:
                        act.wait_ge(s_p, o)
                    act.activation(Ee[:], W1[:], ACT.Exp).then_inc(s_e, 1)
                    if gives:
                        act.wait_ge(s_nd, o + 1)
                        act.activation(AD[:], PS[:, 5, :].rearrange("p (h t) -> p h t", h=HEADS), ACT.Abs)
                        act.activation(HN[:], PS[:, 4, :].rearrange("p (h t) -> p h t", h=HEADS), ACT.Copy).then_inc(s_nde, 1)
                act.wait_ge(s_h, outputs_before(l + 1, 0))
                act.wait_ge(s_st, 2 * NJ * (l + 1))
                for h in range(HEADS):
                    act.activation(Z[:, h, 0:w], H[:, h, 0:w], ACT.Square).then_inc(s_hsq, 1)
                for h in range(HEADS):
                    act.wait_ge(s_hss, 4 * l + h + 1)
                    last = act.activation(RH[:, h, 0:w], banks(2 * h, 2 * h + 2)[:, 0:w], ACT.Ln, bias=eps_c[:, 0:1], scale=1.0 / HD)
                link(last)
                act.activation(RH[:, :, 0:w], RH[:, :, 0:w], ACT.Exp, scale=-0.5).then_inc(s_hr, 1)
                act.wait_ge(s_csum, l + 1)
                act.activation(MU[:, 0:w], banks(0, 2)[:, 0:w], ACT.Copy, scale=1.0 / 256).then_inc(s_cmu, 1)
                act.wait_ge(s_cd, l + 1)
                act.activation(Z[:, 0:2, 0:w], AC[:, :, 0:w], ACT.Square).then_inc(s_csq, 1)
                act.wait_ge(s_cvar, l + 1)
                rstd(MU[:, 0:w], banks(2, 4)[:, 0:w], 1.0 / 256).then_inc(s_crs, 1)
                act.wait_ge(s_cl, l + 1)
                act.activation(Z[:, 0:2, 0:w], AC[:, :, 0:w], ACT.Tanh, scale=0.5).then_inc(s_cta, 1)
                for i in range(KT):
                    act.wait_ge(s_yf, KT * l + i + 1)
                    src = H[:, i] if i < 4 else Ug[:, i - 4] if i < 6 else AC[:, i - 6]
                    act.activation(XH[:, i, 0:w], src[:, 0:w], ACT.Copy).then_inc(s_yh, 1)
                act.wait_ge(s_y, KT * (l + 1))
                with act.Fori(0, 2) as i:
                    for u in range(4):
                        residual_tiles(n0 + N_IN, 16, 4 * i, w, u)
                norm(2 * l + 1, w, used(n0 + N_IN + KT - 1))
                for p, (h0, hn) in enumerate(PARTS):
                    s = part_start(l, p)
                    with act.Fori(0, 2 * hn // 4) as i:
                        for e in range(2):
                            n = s + 2 * e
                            pair = FT * l + h0 + e
                            act.wait_ge(s_tile, n + 1 + 4 * i)
                            act.wait_ge(s_used, used(n - 4) + 4 * i)
                            if pair:
                                act.wait_ge(s_hf, pair + 2 * i)
                            act.activation(Z[:, n % 4, 0:w], acc(n)[:, 0:w], ACT.Identity)
                            act.activation(TH[:, 0:w], acc(n)[:, 0:w], ACT.Tanh, scale=0.5).then_inc(s_evac, 1)
                            evacuate(n + 1, Z[:, (n + 1) % 4, 0:w], w=w, dyn=4 * i, need=used(n - 3) + 4 * i)
                            act.wait_ge(s_hf, pair + 1 + 2 * i)
                            act.activation(HH[:, bass.ds(2 * i + e, 1), 0:w].rearrange("p a t -> p (a t)"), Z[:, (n + 1) % 4, 0:w],
                                           ACT.Copy).then_inc(s_hh, 1)
                    with act.Fori(0, 2) as i:
                        for u in range(4):
                            residual_tiles(s + 2 * hn, 40, 4 * i, w, u)
            second_act(act, link, rstd, evacuate)

        @block.vector
        def _(dve):
            links = [0]

            def link(ins):
                links[0] += 1
                ins.then_inc(s_dch, 1)
                dve.wait_ge(s_dch, links[0])

            def linked_loop(n, per, body):
                start = links[0]
                with dve.Fori(0, n) as i:
                    count = [0]

                    def link_in(ins):
                        count[0] += 1
                        ins.then_inc(s_dch, 1)
                        dve.wait_ge(s_dch, start + count[0] + per * i)
                    body(i, link_in)
                    assert count[0] == per, count
                links[0] = start + n * per

            def col(l, name, i=0):
                return pc[:, l, PC[name] + i:PC[name] + i + 1]

            def norm(q, l, w):
                rs = MT if q in (0, 2) else TH
                second = q % 2
                dve.wait_ge(s_rstd, q + 1)

                def upper(k):
                    if k >= 4:
                        dve.wait_ge(s_xl, KT * q + k - 3)
                    z = Z[:, k % 4]
                    link(dve.tensor_tensor(z[:, 0:w], X[:, k, 0:w], rs[:, 0:w], ALU.mult))
                    for n, (a, b) in enumerate(ranges(w)):
                        last = dve.tensor_scalar(z[:, a:b], z[:, a:b], nsc[:, second, k, n:n + 1],
                                                 mod[:, 24 * second + k, n:n + 1], ALU.mult, ALU.add)
                    last.then_inc(s_xn, 1)

                def lower(k):
                    dve.wait_ge(s_xh, KT * q + k + 1)
                    dve.tensor_tensor(XL[:, k, 0:w], Z[:, k % 4, 0:w], XH[:, k, 0:w].bitcast(FP32), ALU.subtract).then_inc(s_xl, 1)
                upper(0)
                for k in range(1, KT):
                    upper(k)
                    lower(k - 1)
                lower(KT - 1)

            def convolve(l, f, c, src, dst):
                tap = lambda k: col(l, "cw", f * CONV_K + k)
                link(dve.tensor_scalar(dst, src, tap(CONV_K // 2), col(l, "cb", f), ALU.mult, ALU.add))
                if c == "rows":
                    s3, d3 = (v.rearrange("p (r c) -> p r c", c=GRID) for v in (src, dst))
                    cut, n, step, reach = (lambda v, a, b: v[:, :, a:b]), GRID, 1, CONV_K // 2
                    src, dst = s3, d3
                elif c == "columns":
                    cut, n, step, reach = (lambda v, a, b: v[:, a:b]), SEQ, GRID, SEQ // GRID - 1
                else:
                    cut, n, step, reach = (lambda v, a, b: v[:, a:b]), CTX, 1, CONV_K // 2
                for o in range(-reach, reach + 1):
                    if o:
                        a, b = max(0, -o * step), n - max(0, o * step)
                        link(dve.scalar_tensor_tensor(out=cut(dst, a, b), in0=cut(src, a + o * step, b + o * step),
                                                      scalar=tap(CONV_K // 2 + o), in1=cut(dst, a, b), op0=ALU.mult, op1=ALU.add))

            def add_residual(s0, u, dyn, w):
                s = s0 + u
                dve.wait_ge(s_evac, s + 1 + dyn)
                x = X[:, bass.ds(u + dyn, 1), 0:w].rearrange("p a t -> p (a t)")
                dve.tensor_tensor(x, x, Z[:, s % 4, 0:w], ALU.add).then_inc(s_used, 1)

            dve.wait_ge(s_const, 16 * 8)
            dve.wait_ge(s_cth, 1)
            link(dve.scalar_tensor_tensor(out=cth[:], in0=cth[:], scalar=1.0, in1=cact[:], op0=ALU.add, op1=ALU.mult))
            dve.tensor_scalar(cact[:], cth[:], 0.5, None, ALU.mult).then_inc(s_cact, 1)
            for l in range(DEPTH):
                n0 = l * LAYER_TILES
                w = width(l)
                nj = w // P
                dve.wait_ge(s_wgh, l + 1)
                dve.tensor_tensor(wgl[:], wg[:], wgh[:].bitcast(FP32), ALU.subtract).then_inc(s_wgl, 1)
                dve.wait_ge(s_modd, 24 * (l + 1))
                mb = pc[:, l, PC["b_mod"]:PC["b_mod"] + 48].rearrange("p (m o) -> p m o", o=1).to_broadcast([P, 48, 2])
                link(dve.tensor_tensor(mod[:], PS[:, 5, 0:96].rearrange("p (m o) -> p m o", o=2), mb, ALU.add))
                for i, name in enumerate(("norm1", "norm2")):
                    g = pc[:, l, PC[name]:PC[name] + KT].rearrange("p (m o) -> p m o", o=1).to_broadcast([P, KT, 2])
                    at = 8 + 24 * i
                    link(dve.scalar_tensor_tensor(out=nsc[:, i], in0=mod[:, at:at + KT, :], scalar=1.0, in1=g, op0=ALU.add, op1=ALU.mult))
                link(dve.tensor_copy(bcol[:], pc[:, l, PC["b_in"]:PC["b_in"] + N_IN]))
                dve.tensor_scalar(bcol[:, 0:1], bcol[:, 0:1], 0.5, None, ALU.mult)
                dve.tensor_scalar(bcol[:, 2:3], bcol[:, 2:3], 0.5, None, ALU.mult)
                dve.tensor_scalar(bcol[:, O_T:N_IN], bcol[:, O_T:N_IN], 0.5, None, ALU.mult)
                dve.tensor_scalar(bcol[:, K_T:V_T], bcol[:, K_T:V_T], K_SCALE, None, ALU.mult).then_inc(s_mod, 1)
                dve.wait_ge(s_mod, l + 1)
                norm(2 * l, l, T)
                for f in range(2):
                    dve.wait_ge(s_evac, n0 + 2 * f + 2)
                    g = Z[:, 2 * f, 0:w]
                    link(dve.tensor_scalar(g, g, 1.0, 0.5, ALU.add, ALU.mult))
                    dve.tensor_tensor(YC[:, f, 0:w], g, Z[:, 2 * f + 1, 0:w], ALU.mult).then_inc(s_used, 2)
                for i in range(4):
                    dve.wait_ge(s_evac, n0 + U_T + i + 1)
                    g, z = GT[:, i, 0:w], Z[:, i, 0:w]
                    link(dve.tensor_tensor(g, z, z, ALU.mult))
                    link(dve.tensor_scalar(g, g, GELU_A, 1.0, ALU.mult, ALU.add))
                    dve.tensor_tensor(g, g, z, ALU.mult).then_inc(s_gin, 1)
                for i in range(4):
                    dve.wait_ge(s_gth, 4 * l + i + 1)
                    g, z = GT[:, i, 0:w], Z[:, i, 0:w]
                    link(dve.scalar_tensor_tensor(out=g, in0=g, scalar=1.0, in1=z, op0=ALU.add, op1=ALU.mult))
                    out = Ug[:, i, 0:w] if i < 2 else z
                    dve.tensor_scalar(out, g, 0.5, None, ALU.mult).then_inc(s_used if i < 2 else s_gel, 1)
                for e in range(2):
                    dve.wait_ge(s_tr, 10 * l + e + 1)
                    dve.tensor_copy(SVT[:, 0:nj, e * P:(e + 1) * P],
                                    banks(4, 6)[:, 0:nj * P].rearrange("p (j c) -> p j c", c=P)).then_inc(s_tre, 1)
                dve.wait_ge(s_tre, 10 * l + 2)
                dve.wait_ge(s_par, 48 * (l + 1))
                for j in range(nj):
                    last = dve.bn_stats(bst[:, j, :], SVT[:, j, :])
                link(last)
                for j in range(nj):
                    last = dve.bn_aggr(bmv[:, j, :], bst[:, j, :])
                last.then_inc(s_svv, 1)
                dve.wait_ge(s_svr, l + 1)
                for j in range(nj):
                    last = dve.tensor_scalar(SVT[:, j, :], SVT[:, j, :], bmv[:, j, 0:1], bmv[:, j, 1:2], ALU.subtract, ALU.mult)
                link(last)
                for i in range(2):
                    row = srow[:, 256 * i:256 * (i + 1)].rearrange("p (a c) -> p a c", a=1).to_broadcast([P, nj, 256])
                    last = dve.tensor_tensor(SVT[:, 0:nj, :], SVT[:, 0:nj, :], row, (ALU.mult, ALU.add)[i])
                    if i == 0:
                        link(last)
                last.then_inc(s_svt, 1)
                for e in range(2, 10):
                    dve.wait_ge(s_tr, 10 * l + e + 1)
                    dst = ktm if e < 6 else vtm
                    dve.tensor_copy(dst[:, :, (e - 2) % 4, :], banks(4, 6)[:, 0:T].rearrange("p (j c) -> p j c", c=P)).then_inc(s_tre, 1)
                for f in range(2):
                    dve.wait_ge(s_mix, 2 * l + f + 1)
                    bias = srow[:, SROW_B + f * P:SROW_B + (f + 1) * P].rearrange("p (a c) -> p a c", a=1).to_broadcast([P, nj, P])
                    z = Z[:, f, 0:w].rearrange("p (j c) -> p j c", c=P)
                    dve.tensor_tensor(z, banks(6, 8)[:, 0:w].rearrange("p (j c) -> p j c", c=P), bias, ALU.add).then_inc(s_mixu, 1)
                    dve.wait_ge(s_mixu, 2 * l + f + 1)
                    link(dve.tensor_tensor(Ug[:, f, 0:w], Ug[:, f, 0:w], Z[:, f, 0:w], ALU.mult))
                convolve(l, 0, "rows", YC[:, 0, 0:SEQ], AC[:, 0, 0:SEQ])
                convolve(l, 1, "columns", YC[:, 1, 0:SEQ], AC[:, 1, 0:SEQ])
                if w == T:
                    for f in range(2):
                        convolve(l, f, "line", YC[:, f, SEQ:T], AC[:, f, SEQ:T])
                dve.wait_ge(s_gate, l + 1)
                gb = srow[:, SROW_G:SROW_G + 16].rearrange("p (a c) -> p a c", a=1).to_broadcast([P, NJ, 16])
                dve.tensor_tensor(gt[:].rearrange("p j d i h -> p j (d i h)"), PS[:, 4, 0:16 * NJ].rearrange("p (j c) -> p j c", c=16),
                                  gb, ALU.add).then_inc(s_gtm, 1)
                dve.wait_ge(s_lfa, l + 1)
                lfv = lf[:].rearrange("p n j (d h) -> p n j d h", d=2)
                for d in range(2):
                    last = dve.tensor_scalar(lfv[:, 1, :, d, :], gt[:, :, d, 1, :], 0.0, None, ALU.min)
                link(last)
                link(dve.tensor_tensor(lf[:, 2], lf[:, 1], lf[:, 0], ALU.subtract))
                for d in range(2):
                    last = dve.tensor_copy(lfv[:, 1, :, d, :], gt[:, :, d, 0, :])
                last.then_inc(s_lf, 1)
                dve.wait_ge(s_lf, l + 1)
                dve.wait_ge(s_bt, l + 1)
                dve.tensor_copy(btm[:].rearrange("p j e -> p (j e)"), PS[:, 5, 0:NJ * 8]).then_inc(s_btm, 1)
                dve.wait_ge(s_btm, l + 1)
                link(dve.tensor_tensor(gcol[:], lf[:, 1], btm[:], ALU.subtract))
                dve.wait_ge(s_rows, l + 1)
                for i, r in enumerate((ri, rf, rb)):
                    last = dve.tensor_copy(r[:], banks(0, 5)[0:8, i * T:(i + 1) * T])
                link(last)
                scan = lambda o, f, i, m0: link(dve.tensor_tensor_scan(o, f, i, m0, ALU.add, ALU.max))
                cs, ss = slice(SEQ, T), slice(0, SEQ)
                scan(rm[:, cs], rf[:, cs], ri[:, cs], 0.0)
                scan(rm[:, ss], rf[:, ss], ri[:, ss], rm[:, T - 1:T])
                scan(r2[:, cs][:, ::-1], rf[:, cs][:, ::-1], ri[:, cs][:, ::-1], 0.0)
                scan(r2[:, ss][:, ::-1], rf[:, ss][:, ::-1], ri[:, ss][:, ::-1], r2[:, SEQ:SEQ + 1])
                link(dve.memset(mprev[:], 0.0))
                dve.tensor_copy(mprev[:, 0, NJ - 1:NJ], rm[:, T - P - 1:T - P])
                dve.tensor_copy(mprev[:, 0, 0:1], rm[:, T - 1:T])
                dve.tensor_copy(mprev[:, 0, 1:NX], rm[:, P - 1:SEQ - P:P])
                link(dve.tensor_copy(mprev[:, 1, 0:NJ - 1], r2[:, P:T:P]))
                for one, two in ((rm[:], r2[:]), (mprev[:, 0], mprev[:, 1])):
                    link(dve.tensor_scalar(one, one, dsel[:, 0:1], None, ALU.mult))
                    link(dve.scalar_tensor_tensor(out=one, in0=two, scalar=dsel[:, 1:2], in1=one, op0=ALU.mult, op1=ALU.add))
                link(dve.tensor_copy(selh[:], ident[0:8, 0:8].rearrange("p (r c) -> p r c", c=1).to_broadcast([8, 8, P])))
                link(dve.tensor_tensor(ri[:], rb[:], rm[:], ALU.subtract))
                mp = mprev[:, 0].rearrange("p (j o) -> p j o", o=1).to_broadcast([8, NJ, P])
                dve.tensor_tensor(rb[:].rearrange("p (j t) -> p j t", t=P), ri[:].rearrange("p (j t) -> p j t", t=P), mp, ALU.add)
                dve.tensor_scalar(rf[:], rm[:], -1.0, None, ALU.mult).then_inc(s_row, 1)
                for i, r in enumerate((ri, rb, rf)):
                    dve.wait_ge(s_rowh, 3 * l + i + 1)
                    dve.tensor_tensor(rhl[i][1][:], r[:], rhl[i][0][:].bitcast(FP32), ALU.subtract).then_inc(s_rowl, 1)
                written = set()
                for t, (d, j, first, gives) in enumerate(mlstm_steps(l)):
                    c = 2 * NJ * l + t
                    o = outputs_before(l, t)
                    dve.wait_ge(s_nm, c + 1)
                    if c:
                        dve.wait_ge(s_e, c)
                    for h in range(HEADS):
                        last = dve.scalar_tensor_tensor(out=W1[:, h, :], in0=PS[:, 0, h * P:(h + 1) * P],
                                                        scalar=gcol[:, j, 4 * d + h:4 * d + h + 1], in1=mskd[:, d, :],
                                                        op0=ALU.add, op1=ALU.min)
                    last.then_inc(s_w1, 1)
                    if gives:
                        dve.wait_ge(s_e, c + 1)
                        dve.wait_ge(s_s, o + 1)
                        if o:
                            dve.wait_ge(s_nd, o)
                        dve.tensor_tensor(Pp[:], PS[:, 3, :].rearrange("p (h t) -> p h t", h=HEADS), Ee[:], ALU.mult).then_inc(s_p, 1)
                    dve.wait_ge(s_u, c + 1)
                    dve.wait_ge(s_wie, c + 1)
                    tl = P - 1 if d == 0 else 0
                    for h in range(HEADS):
                        st = ST[d][:, h].rearrange("p a c -> p (a c)")
                        up = banks(6, 8)[:, 2 * h * P:2 * (h + 1) * P]
                        if first:
                            last = dve.tensor_copy(st, up)
                        else:
                            last = dve.scalar_tensor_tensor(out=st, in0=st, scalar=WIs[:, h, tl:tl + 1], in1=up, op0=ALU.mult, op1=ALU.add)
                    last.then_inc(s_st, 1)
                    dve.wait_ge(s_st, c + 1)
                    if gives:
                        dve.wait_ge(s_nde, o + 1)
                        link(dve.tensor_tensor(AD[:], AD[:], EMs[:], ALU.max))
                        link(dve.reciprocal(AD[:], AD[:]))
                        hj = H[:, :, j * P:(j + 1) * P]
                        if j in written:
                            link(dve.tensor_tensor(HN[:], HN[:], AD[:], ALU.mult))
                            dve.tensor_tensor(hj, hj, HN[:], ALU.add).then_inc(s_h, 1)
                        else:
                            dve.tensor_tensor(hj, HN[:], AD[:], ALU.mult).then_inc(s_h, 1)
                        written.add(j)
                dve.wait_ge(s_h, outputs_before(l + 1, 0))
                dve.wait_ge(s_hr, l + 1)
                link(dve.tensor_scalar(tho[:, :, 0:w], tho[:, :, 0:w], 1.0, 0.5, ALU.add, ALU.mult))
                link(dve.tensor_tensor(H[:, :, 0:w], H[:, :, 0:w], RH[:, :, 0:w], ALU.mult))
                for h in range(HEADS):
                    dve.scalar_tensor_tensor(out=H[:, h, 0:w], in0=H[:, h, 0:w], scalar=col(l, "mg", h), in1=tho[:, h, 0:w],
                                             op0=ALU.mult, op1=ALU.mult).then_inc(s_yf, 1)

                def lower(i, src):
                    dve.wait_ge(s_yh, KT * l + i + 1)
                    dve.tensor_tensor(XL[:, i, 0:w], src[:, 0:w], XH[:, i, 0:w].bitcast(FP32), ALU.subtract).then_inc(s_y, 1)
                dve.wait_ge(s_cmu, l + 1)
                for f in range(2):
                    last = dve.tensor_tensor(AC[:, f, 0:w], AC[:, f, 0:w], MU[:, 0:w], ALU.subtract)
                last.then_inc(s_cd, 1)
                dve.wait_ge(s_crs, l + 1)
                for f in range(2):
                    last = dve.tensor_tensor(AC[:, f, 0:w], AC[:, f, 0:w], MU[:, 0:w], ALU.mult)
                link(last)
                for f in range(2):
                    last = dve.tensor_scalar(AC[:, f, 0:w], AC[:, f, 0:w], col(l, "cg", f), col(l, "clb", f), ALU.mult, ALU.add)
                last.then_inc(s_cl, 1)
                dve.wait_ge(s_cta, l + 1)
                link(dve.scalar_tensor_tensor(out=AC[:, :, 0:w], in0=Z[:, 0:2, 0:w], scalar=1.0, in1=AC[:, :, 0:w], op0=ALU.add, op1=ALU.mult))
                dve.tensor_scalar(AC[:, :, 0:w], AC[:, :, 0:w], 0.5, None, ALU.mult).then_inc(s_yf, 4)
                for i in range(KT):
                    if i == 4:
                        dve.wait_ge(s_y, KT * l + 4)
                    lower(i, H[:, i] if i < 4 else Ug[:, i - 4] if i < 6 else AC[:, i - 6])
                with dve.Fori(0, 2) as i:
                    for u in range(4):
                        add_residual(n0 + N_IN, u, 4 * i, w)
                norm(2 * l + 1, l, w)
                for p, (h0, hn) in enumerate(PARTS):
                    s = part_start(l, p)

                    def hidden(i, link_in):
                        for e in range(2):
                            n = s + 2 * e
                            pair = FT * l + h0 + e
                            g, v = Z[:, n % 4, 0:w], Z[:, (n + 1) % 4, 0:w]
                            dve.wait_ge(s_evac, n + 2 + 4 * i)
                            link_in(dve.scalar_tensor_tensor(out=g, in0=TH[:, 0:w], scalar=1.0, in1=g, op0=ALU.add, op1=ALU.mult))
                            dve.scalar_tensor_tensor(out=v, in0=g, scalar=0.5, in1=v, op0=ALU.mult, op1=ALU.mult).then_inc(s_hf, 1)
                            dve.wait_ge(s_hh, pair + 1 + 2 * i)
                            at = bass.ds(2 * i + e, 1)
                            hh = HH[:, at, 0:w].rearrange("p a t -> p (a t)").bitcast(FP32)
                            dve.tensor_tensor(HL[:, at, 0:w].rearrange("p a t -> p (a t)"), v, hh, ALU.subtract).then_inc(s_used, 2)
                    linked_loop(2 * hn // 4, 2, hidden)
                    with dve.Fori(0, 2) as i:
                        for u in range(4):
                            add_residual(s + 2 * hn, u, 4 * i, w)
            second_dve(dve, link, linked_loop)

def tiles_of(w):
    k, n = w.shape[-2] // P, w.shape[-1] // P
    v = w.reshape(w.shape[:-2] + (k, P, n, P))
    m = v.ndim
    v = np.transpose(v, tuple(range(m - 4)) + (m - 2, m - 3, m - 4, m - 1))
    return np.ascontiguousarray(v.reshape(w.shape[:-2] + (n, P, k * P)))


def columns_of(v):
    v = v.reshape(v.shape[:-1] + (-1, P))
    return np.ascontiguousarray(np.moveaxis(v, -1, 0))


def kernel(**inputs):
    import concourse.bacc as _bacc
    from concourse.bass_utils import run_bass_kernel_spmd as _run
    a = {k: np.asarray(v) for k, v in inputs.items()}
    f = np.float32
    q, k, v, o, gate, sgu, conv = 0, 512, 1024, 1536, 2048, 2064, 2576
    order = [conv + 256, conv, conv + 384, conv + 128] + [sgu + i * P for i in range(4)]
    for base in (k, v, q, o):
        order += [base + i * P for i in range(4)]
    cols = np.concatenate([np.arange(c, c + P) for c in order])
    gcols = np.arange(gate, gate + 16)
    ts = np.arange(P)
    tri = (ts[:, None] <= ts[None, :]).astype(f)
    consts = np.zeros((P, N_CONST), f)
    consts[:, 0:P] = np.eye(P, dtype=f)
    consts[:, P:2 * P], consts[:, 2 * P:3 * P] = tri, tri.T
    consts[:, 3 * P:4 * P], consts[:, 4 * P:5 * P] = np.where(tri > 0, 0, NEG), np.where(tri.T > 0, 0, NEG)
    consts[0:4, 5 * P] = 1
    consts[4:8, 5 * P + 1] = 1
    par = []
    for l in range(DEPTH):
        cw = a["conv_w"][l].T.reshape(2, P, CONV_K)
        par.append(np.concatenate([columns_of(a["norm1_g"][l]), columns_of(a["norm2_g"][l]), columns_of(a["b_in"][l][cols]),
                                   columns_of(a["mlstm_g"][l]), cw[0], cw[1], columns_of(a["conv_b"][l]),
                                   columns_of(a["conv_ln_g"][l]), columns_of(a["conv_ln_b"][l]), columns_of(a["b_mod"][l])], axis=1))
    rows = []
    for l in range(DEPTH):
        sb = a["sgu_b"][l].reshape(2, 2, 1, P)
        sb = np.broadcast_to(sb, (2, 2, 64, P)).reshape(2, P, P)
        wide = lambda r: np.broadcast_to(r[None], (P, r.shape[0]))
        rows.append(np.concatenate([wide(a["sgu_ln_g"][l]), wide(a["sgu_ln_b"][l]), sb[0], sb[1], wide(a["b_in"][l][gcols])], axis=1))
    w_gu = a["w_gu"].reshape(DEPTH, D, 2, FT, P).transpose(0, 1, 3, 2, 4).reshape(DEPTH, D, 2 * FFN)
    wg = a["w_in"][:, :, gcols].reshape(DEPTH, KT, P, 16).transpose(0, 2, 1, 3)
    wmod = tiles_of(a["w_mod"]).reshape(DEPTH, 24, 2, P, KT * P).transpose(0, 1, 3, 2, 4).reshape(DEPTH, 24, P, 2 * KT * P)
    tokens = np.concatenate([a["x"][0], a["ctx"][0]], axis=0)
    feats = lambda m: np.ascontiguousarray(m.T.reshape(-1, P, m.shape[0]).transpose(1, 0, 2))
    arrays = {
        "xT": feats(tokens), "cT": feats(np.stack([a["c"][0], a["c_ctx"]])),
        "pc": np.stack(par, axis=1), "fin": columns_of(a["final_g"]), "srow": np.stack(rows), "consts": consts,
        "sguw": a["sgu_w"].transpose(0, 3, 1, 2), "wg": wg, "wmod": wmod, "win": tiles_of(a["w_in"][:, :, cols]),
        "wout": tiles_of(a["w_out"]), "wgu": tiles_of(w_gu), "wdn": tiles_of(a["w_down"]),
    }
    aw = a["a_w_in_2"][0]
    per = []
    for hp in range(HP):
        c = np.arange(hp * P, hp * P + P)
        at = [(3 * g + i) * D for g in range(3) for i in range(2)] + [(3 * g + 2) * D for g in range(3)] + [9 * D]
        per += [c + b for b in at]
    arrays["wa"] = tiles_of(aw[:, np.concatenate(per)])
    arrays["wao"] = tiles_of(a["a_w_out_2"][0])
    arrays["pleg"] = tiles_of(a["ple_w_gate_2"])
    arrays["plep"] = tiles_of(a["ple_w_proj_2"])
    bw = a["b_w_in_2"][0]
    kc = np.arange(D, D + 64)
    arrays["wbk"] = tiles_of(bw[:, np.concatenate([kc, kc, kc + 64, kc + 64, np.arange(D + P, D + 2 * P)])])
    zc = D + 2 * P
    arrays["wbqz"] = tiles_of(bw[:, np.concatenate([np.concatenate([np.arange(h * P, h * P + P), np.arange(zc + h * P, zc + h * P + P)]) for h in range(HP)])])
    arrays["wbo"] = tiles_of(a["b_w_out_2"][0])
    arrays["p"] = np.stack([feats(a["p_2"][i, 0]) for i in range(DEPTH)])
    inv = (1.0 / (10000.0 ** (np.arange(0, ADIM, 2, dtype=f) / f(ADIM)))).astype(f)
    ang = np.arange(SEQ, dtype=f)[:, None] * inv[None, :]
    cos, sin = np.cos(ang).astype(f).T, np.sin(ang).astype(f).T
    rope = np.stack([np.tile(cos, (4, 1)), np.concatenate([-sin, sin, -sin, sin])], axis=1)
    am = np.full((P, 4, 768), NEG, f)
    for r in range(4):
        dist = (4 * ts[:, None] + r) - np.arange(SEQ)[None, :]
        am[:, r, 0:SEQ][(dist >= 0) & (dist <= P)] = 0
        back = ts[:, None] - ts[None, :]
        am[:, r, SEQ:SEQ + P][back >= 0] = 0
        am[:, r, SEQ + P:768][(back >= 0) & (back % 4 == 0)] = 0
    bm = np.full((P, 896), NEG, f)
    bm[:, 0:P][ts[:, None] >= ts[None, :]] = 0
    for b in range(3):
        dist = ts[:, None] + P - np.arange(2 * P)[None, :]
        bm[:, P + 2 * P * b:P + 2 * P * (b + 1)][(dist >= 0) & (dist <= P - 1)] = 0
    lnp = np.stack([columns_of(a["ln_g_2"]), columns_of(a["ln_b_2"])], axis=2).reshape(P, -1)
    sink = np.broadcast_to(a["b_sinks_2"][0][None], (P, AH))
    arrays["b2"] = np.concatenate([am.reshape(P, -1), rope.reshape(P, -1), lnp, sink], axis=1)
    arrays["bmask"] = bm
    nc = _bacc.Bacc("TRN2", target_bir_lowering=False, num_devices=1)
    names = ["xT", "cT", "pc", "fin", "srow", "consts", "sguw", "wg", "wmod", "win", "wout", "wgu", "wdn",
             "b2", "bmask", "p", "wa", "wao", "pleg", "plep", "wbk", "wbqz", "wbo"]
    arrays = {n: np.ascontiguousarray(arrays[n]) for n in names}
    args = [nc.dram_tensor("in_" + n, arrays[n].shape, mybir.dt.from_np(arrays[n].dtype), kind="ExternalInput").ap() for n in names]
    out = nc.dram_tensor("out_0_dram", (P, KT, SEQ), FP32, kind="ExternalOutput").ap()
    build_program(nc, *args, out)
    r = _run(nc, [{"in_" + n: arrays[n] for n in names}], core_ids=[0])
    got = np.asarray(r.results[0]["out_0_dram"])
    return np.ascontiguousarray(got.transpose(2, 1, 0).reshape(1, SEQ, D))
```

```python
import numpy as np
import concourse.bass as bass
from concourse import mybir
from contextlib import ExitStack

FP32 = mybir.dt.float32
FP32R = mybir.dt.float32r
ALU = mybir.AluOpType
ACT = mybir.ActivationFunctionType

P = 128
D = 1024
KT = D // P
SEQ, CTX = 512, 256
T = SEQ + CTX
NJ, NX = T // P, SEQ // P
DEPTH = 2
HEADS, HD = 4, 128
FFN = 2816
FT = FFN // P
PARTS = ((0, 8), (8, 8), (16, 6))
GRID = 64
CONV_K = 31
EPS, LN_EPS = 1e-6, 1e-5
K_SCALE = HD ** -0.5
ALPHA = float((2 * DEPTH) ** 0.25)
AH, ADIM = 16, 64
A_SCALE = ADIM ** -0.5
NEG = -1e30
GELU_C, GELU_A = 0.7978845608028654, 0.044715
RING = 4
MODS = 6 * KT
MOD_V = 28
MOD_P = 8

GA_T, U_T, SV_T, K_T, V_T, Q_T, O_T = 0, 4, 6, 8, 12, 16, 20
N_IN = 24
LAYER_TILES = N_IN + KT + 2 * FT + len(PARTS) * KT
HP = AH // 2
A_TILES = 10
N_A = DEPTH * LAYER_TILES
N_AOUT = N_A + A_TILES * HP
N_PLE = (N_AOUT + KT, N_AOUT + KT + 2 * KT + 3 + 2 * HP + KT)
N_B = N_PLE[0] + 2 * KT
N_BQZ = N_B + 3
N_BOUT = N_BQZ + 2 * HP
N_ALL = N_PLE[1] + 2 * KT


def part_start(l, p):
    return l * LAYER_TILES + N_IN + KT + sum(2 * PARTS[q][1] + KT for q in range(p))


def staged(n):
    if n < N_A:
        return not U_T + 2 <= n % LAYER_TILES < N_IN
    if n < N_AOUT:
        return (n - N_A) % A_TILES == 9
    if n < N_B:
        return True
    if n < N_BQZ:
        return False
    if n < N_BOUT:
        return (n - N_BQZ) % 2 == 1
    return True


USED = [0]
for _n in range(N_ALL):
    USED.append(USED[-1] + staged(_n))


def used(n):
    return USED[max(n + 1, 0)]


PC = {}
NPC = 0
for _name, _w in (("norm1", 8), ("norm2", 8), ("b_in", 24), ("mg", 4), ("cw", 2 * CONV_K), ("cb", 2),
                  ("cg", 2), ("clb", 2), ("b_mod", 48)):
    PC[_name] = NPC
    NPC += _w
SROW_B = 512
SROW_G = SROW_B + 2 * P
N_SROW = SROW_G + 16
N_CONST = 5 * P + 2


def mlstm_steps(l):
    order = ([4, 5, 0, 1, 2, 3], [5, 4, 3, 2, 1, 0])
    return [(d, order[d][i], i == 0, l == 0 or order[d][i] < NX) for i in range(NJ) for d in range(2)] if l < DEPTH else []


def outputs_before(l, t):
    return sum(s[3] for m in range(l) for s in mlstm_steps(m)) + sum(s[3] for s in mlstm_steps(l)[:t])


def outputs_of_slot(l, t):
    return outputs_before(l, max(t - 1, 0))


def weighted_before(l, t):
    return (sum(s[3] and not s[2] for m in range(l) for s in mlstm_steps(m))
            + sum(s[3] and not s[2] for s in mlstm_steps(l)[:t]))


def width(l, t=None):
    return T if l == 0 or (t is not None and K_T <= t < Q_T) else SEQ


def ranges(w):
    return [(0, SEQ), (SEQ, T)] if w == T else [(0, SEQ)]


def build_program(nc, xT, cT, cb_d, pc_d, fin_d, srow_d, consts_d, sguw_d, wg_d, wmod_d, win_d, wout_d, wgu_d, wdn_d,
                  b2_d, bmask_d, p_d, wa_d, wao_d, pleg_d, plep_d, wbk_d, wbqz_d, wbo_d, out_d):
    cursor = [nc.sbuf_base + (-nc.sbuf_base) % 64]
    addr_of = {}

    def place(name, shape, dt=FP32, addr=None):
        size = 4
        for s in shape[1:]:
            size *= s
        if addr is None:
            addr = cursor[0]
            cursor[0] += size + (-size) % 32
        assert addr + size <= nc.sbuf_usable_end, (name, addr + size, nc.sbuf_usable_end)
        addr_of[name] = addr
        return nc.alloc_sbuf_tensor_at(name, shape, dt, offset=addr)

    stack = ExitStack()
    with stack:
        def sem(name):
            return stack.enter_context(nc.semaphore(name))

        raw = [place(f"raw{i}", [P, KT * P]) for i in range(RING)]
        w_hi = [place(f"w_hi{i}", [P, KT, P], FP32R) for i in range(2)]
        w_lo = [place(f"w_lo{i}", [P, KT, P], FP32R) for i in range(2)]
        Z = place("Z", [P, 4, T])
        TH = place("TH", [P, N_SROW])
        ident = place("ident", [P, P])
        ones = place("ones", [P, P])
        word = place("word", [P, 8])
        eps_c = place("eps_c", [P, 2])
        X = place("X", [P, KT, T])
        XH = place("XH", [P, KT, T], FP32R)
        XL = place("XL", [P, KT, T], FP32R)
        tri = place("tri", [P, 2, P])
        mskd = place("mskd", [P, 2, P])
        dsel = place("dsel", [8, 2])
        pc = place("pc", [P, DEPTH, NPC])
        fin_g = place("fin_g", [P, KT])
        bcol = place("bcol", [P, N_IN])
        mods = [place(f"mod{l}", [P, MODS, 2]) for l in range(DEPTH)]
        macc = place("macc", [P, 4, 2])
        nsc = place("nsc", [P, 2, KT, 2])
        cact = place("cact", [P, KT, 2])
        cth = place("cth", [P, KT, 2])
        sgw = place("sgw", [P, 4, P])
        wg = place("wg", [P, KT, 16])
        wgh = place("wgh", [P, KT, 16], FP32R)
        wgl = place("wgl", [P, KT, 16], FP32R)
        gt = place("gt", [P, NJ, 2, 2, HEADS])
        lf = place("lf", [P, 3, NJ, 8])
        gcol = place("gcol", [P, NJ, 8])
        btm = place("btm", [P, NJ, 8])
        bst = place("bst", [P, NJ, 6])
        bmv = place("bmv", [P, NJ, 2])
        mprev = place("mprev", [8, 2, NJ])
        work = cursor[0]
        kfm = place("kfm", [P, HEADS, T])
        qfm = place("qfm", [P, HEADS, T])
        tho = place("tho", [P, HEADS, T])
        ktm = place("ktm", [P, NJ, HEADS, P])
        vtm = place("vtm", [P, NJ, HEADS, P])
        YC = place("YC", [P, 2, T])
        AC = place("AC", [P, 2, T])
        Ug = place("Ug", [P, 2, T])
        srow = place("srow", [P, N_SROW], addr=addr_of["TH"])
        SVT = place("SVT", [P, NJ, 256], addr=addr_of["tho"])
        GT = place("GT", [P, HEADS, T], addr=addr_of["qfm"])
        cb = place("cb", [P, 2, D], addr=addr_of["vtm"])
        cprod = place("cprod", [P, D], addr=addr_of["vtm"] + 8 * D)
        modv = [place(f"modv{i}", [P, D], addr=(work + (MOD_P + i) * 4 * D if i < 4 else addr_of["vtm"] + (4 * i - 4) * D))
                for i in range(8)]
        cbt = place("cbt", [P, 2, D], addr=addr_of["vtm"] + 20 * D)
        modp = [place(f"modp{i}", [P, KT, P], addr=work + i * 4 * D) for i in range(MOD_P)]
        MT = place("MT", [P, T], addr=work)
        SQ = [[place(f"SQ{q}{i}", [P, T], addr=(addr_of["Z"], addr_of["vtm"])[q] + i * T * 4) for i in range(2)] for q in range(2)]
        SS = [place(f"SS{q}", [P, T], addr=(addr_of["Z"] + 2 * T * 4, addr_of["vtm"] + 2 * T * 4)[q]) for q in range(2)]
        MU = place("MU", [P, T], addr=addr_of["kfm"])
        ri, rf, rb, rm = (place(f"row{i}", [8, T], addr=addr_of["XH"] + i * T * 4) for i in range(4))
        rhl = [[place(f"rhl{i}{j}", [8, T], FP32R, addr=addr_of["XH"] + (4 + 2 * i + j) * T * 4) for j in range(2)]
               for i in range(3)]
        r2 = place("row4", [8, T], addr=addr_of["XH"] + 10 * T * 4)
        selh = place("selh", [8, 8, P], FP32R, addr=addr_of["row4"])
        H = place("H", [P, HEADS, T], addr=addr_of["XL"] + 4 * T * 4)
        Ee, Pp, Qw, WIs, EMs, Ks = ([place(f"mw{i}{e}", [P, HEADS, P], addr=addr_of[("Z", "raw0")[e]] + i * 2048) for e in range(2)]
                                    for i in range(6))
        ST = [place(f"ST{d}", [P, HEADS, 2, P], addr=addr_of[("YC", "row0")[d]]) for d in range(2)]
        W1 = place("W1", [P, HEADS, P], addr=addr_of["YC"] + 4096)
        AD = place("AD", [P, HEADS, P], addr=addr_of["TH"])
        HN = place("HN", [P, HEADS, P], addr=addr_of["row2"])
        grow = place("grow", [16, T], addr=addr_of["Z"] + 3 * T * 4)
        RH = place("RH", [P, HEADS, T], addr=addr_of["ktm"])
        HH = place("HH", [P, 8, T], FP32R, addr=work)
        HL = place("HL", [P, 8, T], FP32R, addr=work + 8 * T * 4)
        PS = stack.enter_context(nc.psum_tensor("PS", [P, 8, 512], FP32))

        def banks(a, b):
            return PS[:, a:b, :].rearrange("p a b -> p (a b)")

        def acc(n):
            return banks(2 * (n % 2), 2 * (n % 2) + 2)

        s_const = sem("constants_loaded")
        s_x = sem("x_loaded")
        s_par = sem("layer_parameters_loaded")
        s_raw = [sem(f"raw_weights_loaded{i}") for i in range(RING)]
        s_hi = sem("weights_upper_made")
        s_split = sem("weights_split")
        s_tile = sem("gemm_tile_done")
        s_evac = sem("gemm_tile_evacuated")
        s_used = sem("staged_tile_used")
        s_modw = [sem(f"mod_weights_loaded{i}") for i in range(MOD_P)]
        s_mvw = [sem(f"mod_weights_loaded_for_dve{i}") for i in range(8)]
        s_mvd = sem("mod_tile_summed")
        s_cb = sem("c_spread")
        s_cbt = sem("c_spread_tanh_made")
        s_cba = sem("c_spread_activated")
        s_modd = sem("mod_chunk_done")
        s_mod = sem("modulation_ready")
        s_cact = sem("c_activated")
        s_cth = sem("c_tanh_made")
        s_one = sem("on_chip_constants_made")
        s_sq = sem("squares_made")
        s_acc = sem("squares_accumulated")
        s_squ = sem("squares_summed")
        s_lsq = sem("ln_squares_summed")
        s_rstd = sem("rstd_made")
        s_xn = sem("normed_made")
        s_xh = sem("operand_upper_made")
        s_xl = sem("operand_split")
        s_dch = sem("dve_chain")
        s_ach = sem("act_chain")
        s_gin = sem("gelu_argument_made")
        s_gth = sem("gelu_tanh_made")
        s_gel = sem("gelu_made")
        s_tr = sem("transposed")
        s_tre = sem("transposed_evacuated")
        s_svv = sem("sgu_variance_made")
        s_svr = sem("sgu_rstd_made")
        s_svt = sem("sgu_v_normed")
        s_mix = sem("sgu_mixed")
        s_mixu = sem("sgu_mixed_used")
        s_wgh = sem("gate_weights_upper_made")
        s_wgl = sem("gate_weights_split")
        s_gate = sem("gates_done")
        s_grow = sem("gate_rows_done")
        s_growe = sem("gate_rows_evacuated")
        s_gtm = sem("gates_made")
        s_lfa = sem("log_forget_softplus_made")
        s_lf = sem("log_forget_made")
        s_bt = sem("forget_sums_done")
        s_btm = sem("forget_sums_evacuated")
        s_rows = sem("rows_done")
        s_row = sem("rows_made")
        s_rowh = sem("rows_upper_made")
        s_rowl = sem("rows_split")
        s_nm = sem("neg_max_spread")
        s_wi = sem("inter_weights_spread")
        s_wie = sem("inter_weights_made")
        s_w1 = sem("log_weights_made")
        s_e = sem("weights_made")
        s_s = sem("scores_done")
        s_p = sem("weighted_scores_made")
        s_qw = sem("weighted_q_made")
        s_ks = sem("weighted_k_made")
        s_nd = sem("num_den_done")
        s_nde = sem("num_den_evacuated")
        s_u = sem("state_update_done")
        s_st = sem("state_made")
        s_h = sem("h_made")
        s_hsq = sem("h_squares_made")
        s_hss = sem("h_squares_summed")
        s_hr = sem("h_rstd_made")
        s_csum = sem("conv_sum_done")
        s_cmu = sem("conv_mean_made")
        s_cd = sem("conv_centred")
        s_csq = sem("conv_squares_made")
        s_cvar = sem("conv_var_done")
        s_crs = sem("conv_rstd_made")
        s_cl = sem("conv_normed")
        s_cta = sem("conv_tanh_made")
        s_yf = sem("mixer_output_made")
        s_yh = sem("mixer_output_upper_made")
        s_y = sem("mixer_output_split")
        s_hf = sem("hidden_made")
        s_hh = sem("hidden_upper_made")
        s_out = sem("output_stored")

        def split_weights(pool, s, dyn=0, k=KT):
            pool.wait_ge(s_raw[s % RING], 16 * (s // RING + 1) + 4 * dyn)
            if s >= 2:
                pool.wait_ge(s_tile, s - 1 + dyn)
            pool.tensor_tensor(word[:, 0:1], ones[:, 0:1], ones[:, 0:1], ALU.mult)
            src = raw[s % RING][:, 0:k * P].rearrange("p (k c) -> p k c", c=P)
            hi, lo = w_hi[s % 2][:, 0:k, :], w_lo[s % 2][:, 0:k, :]
            pool.tensor_scalar(hi, src, 1.0, 0.0, ALU.mult, ALU.add).then_inc(s_hi, 1)
            pool.wait_ge(s_hi, s + 1 + dyn)
            pool.tensor_tensor(lo, src, hi.bitcast(FP32), ALU.subtract).then_inc(s_split, 1)

        def gemm_step(pe, s, i, rh, rl, w, k):
            hi, lo = w_hi[s % 2][:, i, :], w_lo[s % 2][:, i, :]
            for a, b in ranges(w):
                pe.matmul(acc(s)[:, a:b], hi, rh[:, i, a:b], start=i == 0, stop=False)
                pe.matmul(acc(s)[:, a:b], hi, rl[:, i, a:b], start=False, stop=False)
            for a, b in ranges(w):
                last = pe.matmul(acc(s)[:, a:b], lo, rh[:, i, a:b], start=False, stop=i == k - 1)
            if i == k - 1:
                last.then_inc(s_tile, 1)

        def gemm_tile(pe, s, rh, rl, w, dyn=0, k=KT, ready=None):
            pe.wait_ge(s_split, s + 1 + dyn)
            if s >= 2:
                pe.wait_ge(s_evac, s - 1 + dyn)
            for i in range(k):
                if ready:
                    ready(i)
                gemm_step(pe, s, i, rh, rl, w, k)

        def first_tiles(pe, s, rh, rl, w, done):
            pe.wait_ge(s_split, s + 2)
            if s >= 2:
                pe.wait_ge(s_evac, s)
            for i in range(KT):
                pe.wait_ge(s_xl, done + i + 1)
                for e in range(2):
                    gemm_step(pe, s + e, i, rh, rl, w, KT)


        b2_at = addr_of["tri"]
        cursor[0] = b2_at
        B2 = place("B2", [P, 4 * 768 + 2 * SEQ + 4 * KT + AH])
        amask = B2[:, 0:4 * 768].rearrange("p (r s) -> p r s", r=4)
        ropet = B2[:, 4 * 768:4 * 768 + 2 * SEQ].rearrange("p (a t) -> p a t", a=2)
        lnp = B2[:, 4 * 768 + 2 * SEQ:4 * 768 + 2 * SEQ + 4 * KT].rearrange("p (l a k) -> p l a k", l=DEPTH, a=2)
        sink = B2[:, 4 * 768 + 2 * SEQ + 4 * KT:]
        bmask = place("bmask", [P, 7 * P], addr=addr_of["B2"])
        KB = place("KB", [P, 2, SEQ], addr=addr_of["B2"] + 7 * P * 4)
        YH2 = place("YH2", [P, KT, SEQ], FP32R)
        YL2 = place("YL2", [P, KT, SEQ], FP32R)
        VT = place("VT", [P, 3, NX, P])
        SM = [place(f"SM{i}", [P, 7 * P]) for i in range(2)]
        PT = [place(f"PT{i}", [P, 7, P]) for i in range(2)]
        ZS = place("ZS", [P, SEQ])
        PH = place("PH", [P, 2, SEQ], FP32R)
        PL = place("PL", [P, 2, SEQ], FP32R)
        smax = place("smax", [P, 2, 4])
        ssum = place("ssum", [P, 2, 4])
        esink = place("esink", [P, 2, 4])
        X2 = place("X2", [P, KT, SEQ], addr=addr_of["XH"])
        XH2 = place("XH2", [P, KT, SEQ], FP32R, addr=addr_of["XH"] + KT * SEQ * 4)
        XL2 = place("XL2", [P, KT, SEQ], FP32R, addr=addr_of["XH"] + 2 * KT * SEQ * 4)
        QK = place("QK", [P, 6, SEQ], addr=addr_of["X"])
        QS = place("QS", [P, 6, SEQ], addr=addr_of["X"] + 6 * SEQ * 4)
        Praw = place("Praw", [P, 2, SEQ], addr=addr_of["QS"])

        s_b2 = sem("second_block_constants_loaded")
        s_bm = sem("mixer_b_mask_loaded")
        s_swp = sem("rope_halves_swapped")
        s_rope = sem("rope_applied")
        s_sc = sem("attention_scores_done")
        s_sm = sem("attention_scores_masked")
        s_ex = sem("attention_exp_made")
        s_pn = sem("attention_probabilities_made")
        s_pt = sem("attention_probabilities_transposed")
        s_pte = sem("attention_probabilities_evacuated")
        s_pv = sem("attention_values_done")
        s_ao = sem("attention_output_made")
        s_praw = sem("p_loaded")
        s_ph = sem("p_upper_made")
        s_pl = sem("p_split")
        s_lsum = sem("ln_sum_done")
        s_mu = sem("ln_mean_made")
        s_lnd = sem("ln_centred")

        def head_pairs(eng, mixer):
            if mixer == "a":
                with eng.Fori(0, HP // 2) as i:
                    for e in range(2):
                        yield e, 2 * i, None
            else:
                for kv in range(2):
                    with eng.Fori(0, HP // 4) as i:
                        for e in range(2):
                            yield 4 * kv + e, 2 * i, kv

        def steps_of(mixer):
            return 2 * NX if mixer == "a" else 2

        def step0(mixer, hp):
            return 8 * hp if mixer == "a" else 8 * HP + 2 * hp

        def sc_banks(st):
            return banks(4 + 2 * (st % 2), 6 + 2 * (st % 2))

        def second_sp(sp, load, tile_of):
            sp.wait_ge(s_xl, KT * 5)
            sp.dma_start(B2[:], b2_d).then_inc(s_b2, 16)
            with sp.Fori(0, HP // 2) as i:
                for t in range(2 * A_TILES):
                    load(N_A + t, tile_of(wa_d, 2 * A_TILES * i + t), 2 * A_TILES * i)

            def eight(s, w):
                with sp.Fori(0, 2) as i:
                    for u in range(4):
                        load(s + u, tile_of(w, 4 * i + u), 4 * i)

            def ple(l):
                sp.wait_ge(s_rope, HP * (l + 1) + l)
                sp.dma_start(Praw[:], p_d[l]).then_inc(s_praw, 16)
                with sp.Fori(0, 4) as i:
                    for u in range(2):
                        load(N_PLE[l] + 2 * u, tile_of(pleg_d[l], 2 * i + u), 4 * i)
                        load(N_PLE[l] + 2 * u + 1, tile_of(plep_d[l], 2 * i + u), 4 * i, 2 * P)
            eight(N_AOUT, wao_d)
            ple(0)
            sp.wait_ge(s_sm, 8 * HP)
            sp.dma_start(bmask[:], bmask_d).then_inc(s_bm, 16)
            for t in range(3):
                load(N_B + t, wbk_d[t])
            for kv in range(2):
                with sp.Fori(0, HP // 4) as i:
                    for u in range(4):
                        load(N_BQZ + 8 * kv + u, tile_of(wbqz_d, 4 * i + 8 * kv + u), 4 * i)
            eight(N_BOUT, wbo_d)
            ple(1)
            sp.wait_ge(s_used, used(N_ALL - 1))
            sp.dma_start(out_d, X2[:]).then_inc(s_out, 16)
            sp.wait_ge(s_out, 16)

        def second_pool(pool):
            def eight(s):
                with pool.Fori(0, 2) as i:
                    for u in range(4):
                        split_weights(pool, s + u, 4 * i)

            def ple(l):
                with pool.Fori(0, 4) as i:
                    for u in range(2):
                        split_weights(pool, N_PLE[l] + 2 * u, 4 * i)
                        split_weights(pool, N_PLE[l] + 2 * u + 1, 4 * i, 2)
            with pool.Fori(0, HP // 2) as i:
                for t in range(2 * A_TILES):
                    split_weights(pool, N_A + t, 2 * A_TILES * i)
            eight(N_AOUT)
            ple(0)
            for t in range(3):
                split_weights(pool, N_B + t)
            for kv in range(2):
                with pool.Fori(0, HP // 4) as i:
                    for u in range(4):
                        split_weights(pool, N_BQZ + 8 * kv + u, 4 * i)
            eight(N_BOUT)
            ple(1)

        def second_pe(pe):
            def transpose_v(event, dyn, src, strided):
                pe.wait_ge(s_tre, event + dyn)
                for j in range(NX):
                    part = src[:, j:SEQ:4] if strided else src[:, j * P:(j + 1) * P]
                    last = pe.transpose(PS[:, 4, j * P:(j + 1) * P], part, ident[:])
                last.then_inc(s_tr, 1)

            def attention(mixer, e, dyn, kv, tiles):
                n = steps_of(mixer)
                c0, cd = step0(mixer, e), n * dyn
                hp = e + (0 if mixer == "a" else HP)
                pe.wait_ge(s_rope, HP * (mixer == "b") + (mixer == "b") + e + 1 + dyn)
                pe.wait_ge(s_evac, tiles[0] + tiles[1])
                pe.wait_ge(s_tre, (20 + 3 * (e + 1) if mixer == "a" else 20 + 3 * HP + 1) + (3 * dyn if mixer == "a" else 0))

                def scores(st):
                    c = c0 + st
                    if c >= 2:
                        pe.wait_ge(s_sm, c - 1 + cd)
                    sc = sc_banks(st)
                    if mixer == "a":
                        h, r = 64 * (st // NX), st % NX
                        pe.matmul(sc[:, 0:SEQ], QK[h:h + 64, 0, r:SEQ:4], QK[h:h + 64, 1, :], start=True, stop=True)
                        for g in (1, 2):
                            last = pe.matmul(sc[:, SEQ + (g - 1) * P:SEQ + g * P], QK[h:h + 64, 2 * g, r:SEQ:4],
                                             QK[h:h + 64, 2 * g + 1, r:SEQ:4], start=True, stop=True)
                    else:
                        h = 64 * st
                        for b in range(NX):
                            a = max(b - 1, 0) * P
                            at = 2 * P * b + (P if b == 0 else 0)
                            last = pe.matmul(sc[:, at:2 * P * (b + 1)], QK[h:h + 64, 0, b * P:(b + 1) * P],
                                             KB[h:h + 64, kv, a:(b + 1) * P], start=True, stop=True)
                    last.then_inc(s_sc, 1)

                def values(st):
                    c = c0 + st
                    pe.wait_ge(s_pn, c + 1 + cd)
                    if c:
                        pe.wait_ge(s_pte, c + cd)
                    nb = 6 if mixer == "a" else 7
                    for b in range(nb):
                        last = pe.transpose(banks(0, 2)[:, b * P:(b + 1) * P], SM[st % 2][:, b * P:(b + 1) * P], ident[:])
                    last.then_inc(s_pt, 1)
                    pe.wait_ge(s_pte, c + 1 + cd)
                    if st == 0 and hp:
                        pe.wait_ge(s_ao, hp + dyn)
                    pt = PT[st % 2]
                    if mixer == "a":
                        h, r = 64 * (st // NX), st % NX
                        for b in range(6):
                            g, blk = (0, b) if b < NX else (b - NX + 1, r)
                            last = pe.matmul(PS[h:h + 64, 2, r:SEQ:4], VT[:, g, blk, h:h + 64], pt[:, b, :], start=b == 0, stop=b == 5)
                    else:
                        h = 64 * st
                        for b in range(NX):
                            blocks = [(2 * b - 1, b - 1), (2 * b, b)] if b else [(0, 0)]
                            for m, (src, blk) in enumerate(blocks):
                                last = pe.matmul(PS[h:h + 64, 2, b * P:(b + 1) * P], VT[:, 0, blk, 64 * kv:64 * kv + 64], pt[:, src, :],
                                                 start=m == 0, stop=m == len(blocks) - 1)
                    last.then_inc(s_pv, 1)
                scores(0)
                for st in range(n):
                    if st + 1 < n:
                        scores(st + 1)
                    values(st)
                pe.wait_ge(s_ao, hp + 1 + dyn)

            def eight(s):
                with pe.Fori(0, 2) as i:
                    for u in range(4):
                        gemm_tile(pe, s + u, YH2, YL2, SEQ, 4 * i)

            def layer_norm(l):
                pe.wait_ge(s_used, used(N_PLE[l] - 1))
                for k in range(KT):
                    last = pe.matmul(PS[:, 6, :], ones[:], X2[:, k, :], start=k == 0, stop=k == KT - 1)
                last.then_inc(s_lsum, 1)
                for k in range(KT):
                    pe.wait_ge(s_sq, KT * (5 + l) + k + 1)
                    pe.matmul(PS[:, 6, :], ones[:], Z[:, k % 4, 0:SEQ], start=k == 0, stop=k == KT - 1).then_inc(s_lsq, 1)

            def ple(l):
                pe.wait_ge(s_xl, KT * (6 + 2 * l))
                pe.wait_ge(s_pl, l + 1)
                with pe.Fori(0, 4) as i:
                    for u in range(2):
                        gemm_tile(pe, N_PLE[l] + 2 * u, XH2, XL2, SEQ, 4 * i)
                        gemm_tile(pe, N_PLE[l] + 2 * u + 1, PH, PL, SEQ, 4 * i, 2)

            pe.wait_ge(s_xl, KT * 5)
            for e, dyn, _ in head_pairs(pe, "a"):
                n = N_A + A_TILES * e
                for t in range(A_TILES):
                    gemm_tile(pe, n + t, XH2, XL2, SEQ, A_TILES * dyn)
                    if t >= 7:
                        g = t - 7
                        pe.wait_ge(s_evac, n + t + A_TILES * dyn)
                        transpose_v(20 + 3 * e + g, 3 * dyn, Z[:, (n + t - 1) % 4, 0:SEQ], g > 0)
                attention("a", e, dyn, None, (n + A_TILES, A_TILES * dyn))
            pe.wait_ge(s_y, KT * 3)
            eight(N_AOUT)
            layer_norm(0)
            ple(0)
            pe.wait_ge(s_xl, KT * 7)
            for t in range(3):
                gemm_tile(pe, N_B + t, XH2, XL2, SEQ)
            pe.wait_ge(s_evac, N_B + 3)
            transpose_v(20 + 3 * HP, 0, Z[:, (N_B + 2) % 4, 0:SEQ], False)
            for e, dyn, kv in head_pairs(pe, "b"):
                n = N_BQZ + 2 * e
                for t in range(2):
                    gemm_tile(pe, n + t, XH2, XL2, SEQ, 2 * dyn)
                attention("b", e, dyn, kv, (n + 2, 2 * dyn))
            pe.wait_ge(s_y, KT * 4)
            eight(N_BOUT)
            layer_norm(1)
            ple(1)

        def second_act(act, link, rstd, evacuate):
            def swap(dst, src, wait_tile, dyn):
                act.wait_ge(s_evac, wait_tile + dyn)
                for q in range(4):
                    act.dma_start(dst[32 * (q ^ 1):32 * (q ^ 1) + 32], src[32 * q:32 * q + 32]).then_inc(s_swp, 16)

            def z_tile(n, dyn, per):
                act.wait_ge(s_tile, n + 1 + dyn)
                act.wait_ge(s_used, used(n - 1) + per)
                act.activation(Z[:, n % 4, 0:SEQ], acc(n)[:, 0:SEQ], ACT.Identity)
                act.activation(TH[:, 0:SEQ], acc(n)[:, 0:SEQ], ACT.Tanh, scale=0.5).then_inc(s_evac, 1)

            def attention(mixer, e, dyn):
                n = steps_of(mixer)
                c0, cd = step0(mixer, e), n * dyn

                def exps(st):
                    c = c0 + st
                    act.wait_ge(s_sm, c + 1 + cd)
                    m = smax[:, st % 2]
                    if mixer == "a":
                        s = SM[st % 2][:, 0:768]
                        act.activation(s, s, ACT.Exp, bias=m[:, 1:2], accum_out=ssum[:, st % 2, 0:1]).then_inc(s_ex, 1)
                    else:
                        for b in range(NX):
                            s = SM[st % 2][:, max(2 * b - 1, 0) * P:(2 * b + 1) * P]
                            act.activation(s, s, ACT.Exp, bias=m[:, b:b + 1], accum_out=ssum[:, st % 2, b:b + 1])
                        head = sink[:, bass.ds(2 * e + st + 2 * dyn, 1)]
                        act.activation(esink[:, st % 2], m, ACT.Exp, bias=head).then_inc(s_ex, 1)

                def evac(st):
                    c = c0 + st
                    act.wait_ge(s_pt, c + 1 + cd)
                    if c >= 2:
                        act.wait_ge(s_pv, c - 1 + cd)
                    nb = 6 if mixer == "a" else 7
                    act.activation(PT[st % 2][:, 0:nb, :].rearrange("p b t -> p (b t)"), banks(0, 2)[:, 0:nb * P], ACT.Copy).then_inc(s_pte, 1)
                exps(0)
                for st in range(n):
                    if st + 1 < n:
                        exps(st + 1)
                    evac(st)
                hp = e + HP * (mixer == "b")
                act.wait_ge(s_ao, hp + 1 + dyn)
                act.activation(YH2[:, bass.ds(e + dyn, 1), :].rearrange("p a t -> p (a t)"), ZS[:], ACT.Copy).then_inc(s_yh, 1)

            def plain(n, dyn):
                act.wait_ge(s_tile, n + 1 + dyn)
                act.wait_ge(s_used, used(n - 4) + dyn)
                act.activation(Z[:, n % 4, 0:SEQ], acc(n)[:, 0:SEQ], ACT.Identity).then_inc(s_evac, 1)

            def eight(s):
                act.wait_ge(s_used, used(s - 1))
                with act.Fori(0, 2) as i:
                    for u in range(4):
                        plain(s + u, 4 * i)

            def split_x(q, counted):
                for k in range(KT):
                    act.wait_ge(*counted(k))
                    act.activation(XH2[:, k], X2[:, k], ACT.Copy).then_inc(s_xh, 1)
                act.wait_ge(s_xl, KT * (q + 1))

            def layer_norm(l):
                act.wait_ge(s_lsum, l + 1)
                act.activation(TH[:, 0:SEQ], PS[:, 6, :], ACT.Copy, scale=1.0 / D).then_inc(s_mu, 1)
                for k in range(KT):
                    act.wait_ge(s_lnd, KT * l + k + 1)
                    if k >= 4:
                        act.wait_ge(s_lsq, KT * l + k - 3)
                    act.activation(Z[:, k % 4, 0:SEQ], X2[:, k], ACT.Square).then_inc(s_sq, 1)
                act.wait_ge(s_lsq, KT * (l + 1))
                rstd(TH[:, 0:SEQ], PS[:, 6, :], 1.0 / D, 1).then_inc(s_rstd, 1)
                split_x(5 + 2 * l, lambda k: (s_xn, KT * (5 + l) + k + 1))

            def ple(l):
                act.wait_ge(s_praw, 16 * (l + 1))
                act.activation(PH[:], Praw[:], ACT.Copy).then_inc(s_ph, 1)
                with act.Fori(0, 4) as i:
                    for u in range(2):
                        n = N_PLE[l] + 2 * u
                        act.wait_ge(s_tile, n + 1 + 4 * i)
                        act.wait_ge(s_used, used(n - 3) + 4 * i)
                        act.activation(Z[:, n % 4, 0:SEQ], acc(n)[:, 0:SEQ], ACT.Tanh, scale=0.5).then_inc(s_evac, 1)
                        act.wait_ge(s_tile, n + 2 + 4 * i)
                        act.activation(Z[:, (n + 1) % 4, 0:SEQ], acc(n + 1)[:, 0:SEQ], ACT.Identity).then_inc(s_evac, 1)

            act.wait_ge(s_squ, 5)
            rstd(TH[:, 0:SEQ], PS[:, 6, :], 1.0 / D).then_inc(s_rstd, 1)
            split_x(4, lambda k: (s_xn, KT * 4 + k + 1))
            for e, dyn, _ in head_pairs(act, "a"):
                n = N_A + A_TILES * e
                for t in range(6):
                    act.wait_ge(s_tile, n + t + 1 + A_TILES * dyn)
                    act.activation(QK[:, t], acc(n + t)[:, 0:SEQ], ACT.Identity).then_inc(s_evac, 1)
                swap(QS, QK, n + 6, A_TILES * dyn)
                for t in range(6, 9):
                    act.wait_ge(s_tile, n + t + 1 + A_TILES * dyn)
                    if t == 6:
                        act.wait_ge(s_used, used(n - 1) + dyn)
                        act.wait_ge(s_tre, 20 + 3 * e + 3 * dyn)
                    act.activation(Z[:, (n + t) % 4, 0:SEQ], acc(n + t)[:, 0:SEQ], ACT.Identity).then_inc(s_evac, 1)
                z_tile(n + 9, A_TILES * dyn, dyn)
                attention("a", e, dyn)
            eight(N_AOUT)
            layer_norm(0)
            ple(0)
            act.wait_ge(s_tile, N_B)
            split_x(6, lambda k: (s_used, used(N_PLE[0] + 2 * k + 1)))
            act.wait_ge(s_bm, 16)
            for t in range(2):
                act.wait_ge(s_tile, N_B + t + 1)
                act.activation(KB[:, t], acc(N_B + t)[:, 0:SEQ], ACT.Identity).then_inc(s_evac, 1)
            swap(QS[:, 0:2], KB, N_B + 2, 0)
            act.wait_ge(s_tile, N_B + 3)
            act.activation(Z[:, (N_B + 2) % 4, 0:SEQ], acc(N_B + 2)[:, 0:SEQ], ACT.Identity).then_inc(s_evac, 1)
            act.wait_ge(s_tre, 20 + 3 * HP + 1)
            for e, dyn, kv in head_pairs(act, "b"):
                n = N_BQZ + 2 * e
                act.wait_ge(s_tile, n + 1 + 2 * dyn)
                act.activation(QK[:, 0], acc(n)[:, 0:SEQ], ACT.Identity).then_inc(s_evac, 1)
                swap(QS[:, 2], QK[:, 0], n + 1, 2 * dyn)
                z_tile(n + 1, 2 * dyn, dyn)
                attention("b", e, dyn)
            eight(N_BOUT)
            layer_norm(1)
            ple(1)

        def second_dve(dve, link, linked_loop):
            def lower(q, k):
                dve.wait_ge(s_xh, KT * q + k + 1)
                dve.tensor_tensor(XL2[:, k], X2[:, k], XH2[:, k].bitcast(FP32), ALU.subtract).then_inc(s_xl, 1)

            def rope(x, xs, n, link_in, count):
                dve.wait_ge(s_swp, count)
                cos, sin = (ropet[:, i:i + 1].to_broadcast([P, n, SEQ]) for i in range(2))
                dve.tensor_tensor(x, x, cos, ALU.mult)
                link_in(dve.tensor_tensor(xs, xs, sin, ALU.mult))
                dve.tensor_tensor(x, x, xs, ALU.add).then_inc(s_rope, 1)

            def attention(mixer, e, dyn, link_in):
                n = steps_of(mixer)
                c0, cd = step0(mixer, e), n * dyn

                def mask(st):
                    c = c0 + st
                    dve.wait_ge(s_sc, c + 1 + cd)
                    if c >= 2:
                        dve.wait_ge(s_pt, c - 1 + cd)
                    dve.tensor_tensor(word[:, 1:2], ones[:, 0:1], ones[:, 0:1], ALU.mult)
                    m = smax[:, st % 2]
                    if mixer == "a":
                        link_in(dve.tensor_tensor_reduce(out=SM[st % 2][:, 0:768], in0=sc_banks(st)[:, 0:768], in1=amask[:, st % NX, :],
                                                         scale=A_SCALE, scalar=NEG, op0=ALU.add, op1=ALU.max, accum_out=m[:, 0:1]))
                        dve.tensor_scalar(m[:, 1:2], m[:, 0:1], -1.0, 0.0, ALU.mult, ALU.add).then_inc(s_sm, 1)
                    else:
                        for b in range(NX):
                            a, z = max(2 * b - 1, 0) * P, (2 * b + 1) * P
                            last = dve.tensor_tensor_reduce(out=SM[st % 2][:, a:z], in0=sc_banks(st)[:, a + P:z + P], in1=bmask[:, a:z],
                                                            scale=A_SCALE, scalar=NEG, op0=ALU.add, op1=ALU.max, accum_out=m[:, b:b + 1])
                        link_in(last)
                        head = sink[:, bass.ds(2 * e + st + 2 * dyn, 1)]
                        dve.tensor_scalar(m, m, head, -1.0, ALU.max, ALU.mult).then_inc(s_sm, 1)

                def normalise(st):
                    c = c0 + st
                    dve.wait_ge(s_ex, c + 1 + cd)
                    s = ssum[:, st % 2]
                    if mixer == "a":
                        link_in(dve.reciprocal(s[:, 1:2], s[:, 0:1]))
                        dve.tensor_scalar(SM[st % 2][:, 0:768], SM[st % 2][:, 0:768], s[:, 1:2], None, ALU.mult).then_inc(s_pn, 1)
                    else:
                        link_in(dve.tensor_tensor(s, s, esink[:, st % 2], ALU.add))
                        link_in(dve.reciprocal(s, s))
                        for b in range(NX):
                            a, z = max(2 * b - 1, 0) * P, (2 * b + 1) * P
                            last = dve.tensor_scalar(SM[st % 2][:, a:z], SM[st % 2][:, a:z], s[:, b:b + 1], None, ALU.mult)
                        last.then_inc(s_pn, 1)
                mask(0)
                for st in range(n):
                    if st + 1 < n:
                        mask(st + 1)
                    normalise(st)
                hp = e + HP * (mixer == "b")
                dve.wait_ge(s_pv, c0 + n + cd)
                dve.scalar_tensor_tensor(out=ZS[:], in0=PS[:, 2, :], scalar=0.5, in1=ZS[:], op0=ALU.mult, op1=ALU.mult).then_inc(s_ao, 1)
                dve.wait_ge(s_yh, 16 + hp + 1 + dyn)
                at = bass.ds(e + dyn, 1)
                dve.tensor_tensor(YL2[:, at, :].rearrange("p a t -> p (a t)"), ZS[:],
                                  YH2[:, at, :].rearrange("p a t -> p (a t)").bitcast(FP32), ALU.subtract).then_inc(s_y, 1)
                return hp

            def z_gate(n, ndyn, hp, dyn):
                dve.wait_ge(s_evac, n + 1 + ndyn)
                dve.wait_ge(s_y, 16 + hp + dyn)
                dve.scalar_tensor_tensor(out=ZS[:], in0=TH[:, 0:SEQ], scalar=1.0, in1=Z[:, n % 4, 0:SEQ],
                                         op0=ALU.add, op1=ALU.mult).then_inc(s_used, 1)
                dve.wait_ge(s_used, used(n) + dyn)

            def pair_loop(mixer, per, body):
                for kv in range(2 if mixer == "b" else 1):
                    linked_loop(HP // 4 if mixer == "b" else HP // 2, 2 * per,
                                lambda i, link_in: [body(4 * kv + e, 2 * i, link_in) for e in range(2)])

            def eight(s):
                with dve.Fori(0, 2) as i:
                    for u in range(4):
                        dve.wait_ge(s_evac, s + u + 1 + 4 * i)
                        x = X2[:, bass.ds(u + 4 * i, 1), :].rearrange("p a t -> p (a t)")
                        dve.scalar_tensor_tensor(out=x, in0=x, scalar=ALPHA, in1=Z[:, (s + u) % 4, 0:SEQ],
                                                 op0=ALU.mult, op1=ALU.add).then_inc(s_used, 1)

            def layer_norm(l):
                dve.wait_ge(s_mu, l + 1)
                for k in range(KT):
                    dve.tensor_tensor(X2[:, k], X2[:, k], TH[:, 0:SEQ], ALU.subtract).then_inc(s_lnd, 1)
                dve.wait_ge(s_rstd, 6 + l)

                def upper(k):
                    link(dve.tensor_tensor(X2[:, k], X2[:, k], TH[:, 0:SEQ], ALU.mult))
                    dve.tensor_scalar(X2[:, k], X2[:, k], lnp[:, l, 0, k:k + 1], lnp[:, l, 1, k:k + 1], ALU.mult, ALU.add).then_inc(s_xn, 1)
                upper(0)
                for k in range(1, KT):
                    upper(k)
                    lower(5 + 2 * l, k - 1)
                lower(5 + 2 * l, KT - 1)

            def ple(l):
                dve.wait_ge(s_ph, l + 1)
                dve.tensor_tensor(PL[:], Praw[:], PH[:].bitcast(FP32), ALU.subtract).then_inc(s_pl, 1)

                def body(i, link_in):
                    for u in range(2):
                        n = N_PLE[l] + 2 * u
                        g, v = Z[:, n % 4, 0:SEQ], Z[:, (n + 1) % 4, 0:SEQ]
                        dve.wait_ge(s_evac, n + 2 + 4 * i)
                        link_in(dve.scalar_tensor_tensor(out=g, in0=g, scalar=1.0, in1=v, op0=ALU.add, op1=ALU.mult))
                        x = X2[:, bass.ds(u + 2 * i, 1), :].rearrange("p a t -> p (a t)")
                        dve.scalar_tensor_tensor(out=x, in0=g, scalar=0.5, in1=x, op0=ALU.mult, op1=ALU.add).then_inc(s_used, 2)
                linked_loop(4, 2, body)

            dve.wait_ge(s_rstd, 5)

            def upper(k):
                if k >= 4:
                    dve.wait_ge(s_xn, KT * 4 + k - 3)
                z = Z[:, k % 4, 0:SEQ]
                link(dve.tensor_tensor(z, X[:, k, 0:SEQ], TH[:, 0:SEQ], ALU.mult))
                dve.tensor_scalar(X2[:, k], z, fin_g[:, k:k + 1], None, ALU.mult).then_inc(s_xn, 1)
            upper(0)
            for k in range(1, KT):
                upper(k)
                lower(4, k - 1)
            lower(4, KT - 1)
            dve.wait_ge(s_b2, 16)

            def pair_a(e, dyn, link_in):
                n = N_A + A_TILES * e
                rope(QK[:], QS[:], 6, link_in, 64 * (e + 1) + 64 * dyn)
                for g in range(3):
                    dve.wait_ge(s_tr, 20 + 3 * e + g + 1 + 3 * dyn)
                    dve.tensor_copy(VT[:, g].rearrange("p j d -> p (j d)"), PS[:, 4, :]).then_inc(s_tre, 1)
                z_gate(n + 9, A_TILES * dyn, e, dyn)
                attention("a", e, dyn, link_in)

            def pair_b(e, dyn, link_in):
                n = N_BQZ + 2 * e
                rope(QK[:, 0:1], QS[:, 2:3], 1, link_in, 64 * (HP + 1 + e + 1) + 64 * dyn)
                z_gate(n + 1, 2 * dyn, HP + e, dyn)
                attention("b", e, dyn, link_in)
            pair_loop("a", 1 + 8 * 2, pair_a)
            eight(N_AOUT)
            layer_norm(0)
            ple(0)
            for k in range(KT):
                lower(6, k)
            dve.wait_ge(s_bm, 16)
            rope(KB[:], QS[:, 0:2], 2, link, 64 * (HP + 1))
            dve.wait_ge(s_tr, 20 + 3 * HP + 1)
            dve.tensor_copy(VT[:, 0].rearrange("p j d -> p (j d)"), PS[:, 4, :]).then_inc(s_tre, 1)
            pair_loop("b", 1 + 2 * 3, pair_b)
            eight(N_BOUT)
            layer_norm(1)
            ple(1)

        block = stack.enter_context(nc.Block())

        @block.sync
        def _(sp):
            sp.dma_start(cact[:], cT).then_inc(s_const, 16)
            sp.dma_start(cb[:].rearrange("p a k -> p (a k)"), cb_d).then_inc(s_cb, 16)
            sp.dma_start(ident[:], consts_d[:, 0:P]).then_inc(s_const, 16)
            sp.dma_start(tri[:].rearrange("p a b -> p (a b)"), consts_d[:, P:3 * P]).then_inc(s_const, 16)
            sp.dma_start(mskd[:].rearrange("p a b -> p (a b)"), consts_d[:, 3 * P:5 * P]).then_inc(s_const, 16)
            sp.dma_start(dsel[:], consts_d[0:8, 5 * P:5 * P + 2]).then_inc(s_const, 16)
            sp.dma_start(pc[:], pc_d).then_inc(s_const, 16)
            sp.dma_start(fin_g[:], fin_d).then_inc(s_const, 16)

            def load(s, src, dyn=0, cols=KT * P):
                if s >= RING:
                    sp.wait_ge(s_split, s - RING + 1 + dyn)
                sp.dma_start(raw[s % RING][:, 0:cols], src).then_inc(s_raw[s % RING], 16)

            def tile_of(w, i):
                return w[bass.ds(i, 1)].rearrange("a p n -> (a p) n")

            for l in range(DEPTH):
                n0 = l * LAYER_TILES
                if l:
                    sp.wait_ge(s_tile, n0)
                    sp.wait_ge(s_used, used(n0 - 1))
                sp.dma_start(srow[:], srow_d[l]).then_inc(s_par, 16)
                sp.dma_start(sgw[:], sguw_d[l]).then_inc(s_par, 16)
                sp.dma_start(wg[:], wg_d[l]).then_inc(s_par, 16)
                if l == 0:
                    v = p = 0
                    for m in range(MODS):
                        if v * (MODS - MOD_V) <= p * MOD_V and v < MOD_V:
                            slot = v % 8
                            if v == 6:
                                sp.wait_ge(s_cba, 1)
                            if v >= 8:
                                sp.wait_ge(s_mvd, v - 7)
                            sp.dma_start(modv[slot][:], wmod_d[l, v]).then_inc(s_mvw[slot], 16)
                            v += 1
                        else:
                            if p >= MOD_P:
                                sp.wait_ge(s_modd, p - MOD_P + 1)
                            sp.dma_start(modp[p % MOD_P][:].rearrange("p k c -> p (k c)"), wmod_d[l, MOD_V + p]).then_inc(s_modw[p % MOD_P], 16)
                            p += 1
                        if m == MODS // 3:
                            sp.dma_start(X[:], xT).then_inc(s_x, 16)
                for n in range(N_IN):
                    load(n0 + n, win_d[l, n])
                sp.wait_ge(s_st, 2 * NJ * (l + 1))
                sp.wait_ge(s_h, outputs_before(l + 1, 0))
                with sp.Fori(0, 2) as i:
                    for u in range(4):
                        load(n0 + N_IN + u, tile_of(wout_d[l], 4 * i + u), 4 * i)
                for p, (h0, hn) in enumerate(PARTS):
                    s = part_start(l, p)
                    with sp.Fori(0, 2 * hn // 4) as i:
                        for u in range(4):
                            load(s + u, tile_of(wgu_d[l], 4 * i + 2 * h0 + u), 4 * i)
                    with sp.Fori(0, 2) as i:
                        for u in range(4):
                            load(s + 2 * hn + u, tile_of(wdn_d[l, :, :, h0 * P:(h0 + hn) * P], 4 * i + u), 4 * i, hn * P)
            second_sp(sp, load, tile_of)

        @block.gpsimd
        def _(pool):
            pool.memset(ones[:], 1.0).then_inc(s_one, 1)
            pool.memset(eps_c[:, 0:1], EPS).then_inc(s_one, 1)
            pool.memset(eps_c[:, 1:2], LN_EPS).then_inc(s_one, 1)
            pool.wait_ge(s_one, 3)
            for k in range(KT):
                pool.wait_ge(s_sq, k + 1)
                sq, ss = SQ[0][k % 2], SS[0]
                if k:
                    pool.wait_ge(s_acc, k)
                    pool.tensor_tensor(ss[:], ss[:], sq[:], ALU.add).then_inc(s_acc, 1)
                else:
                    pool.tensor_scalar(ss[:], sq[:], 1.0, 0.0, ALU.mult, ALU.add).then_inc(s_acc, 1)
            for l in range(DEPTH):
                n0 = l * LAYER_TILES
                for n in range(N_IN):
                    split_weights(pool, n0 + n)
                for t, (d, j, first, gives) in enumerate(mlstm_steps(l)):
                    c = 2 * NJ * l + t
                    if gives and not first:
                        pool.wait_ge(s_wie, c + 1)
                        if outputs_of_slot(l, t):
                            pool.wait_ge(s_nd, outputs_of_slot(l, t))
                        pool.tensor_tensor(Qw[c % 2][:], qfm[:, :, j * P:(j + 1) * P], WIs[c % 2][:], ALU.mult).then_inc(s_qw, 1)
                    pool.wait_ge(s_e, c + 1)
                    if c >= 2:
                        pool.wait_ge(s_u, c - 1)
                    tl = P - 1 if d == 0 else 0
                    pool.tensor_tensor(Ks[c % 2][:], ktm[:, j, :, :], Ee[c % 2][:, :, tl:tl + 1].to_broadcast([P, HEADS, P]),
                                       ALU.mult).then_inc(s_ks, 1)
                with pool.Fori(0, 2) as i:
                    for u in range(4):
                        split_weights(pool, n0 + N_IN + u, 4 * i)
                for p, (h0, hn) in enumerate(PARTS):
                    s = part_start(l, p)
                    with pool.Fori(0, 2 * hn // 4) as i:
                        for u in range(4):
                            split_weights(pool, s + u, 4 * i)
                    with pool.Fori(0, 2) as i:
                        for u in range(4):
                            split_weights(pool, s + 2 * hn + u, 4 * i, hn)
            second_pool(pool)

        @block.tensor
        def _(pe):
            def norm(q, w):
                pe.wait_ge(s_acc, KT * (q + 1))
                for a, b in ranges(w):
                    last = pe.matmul(banks(6, 8)[:, a:b], ones[:], SS[q > 0][:, a:b], start=True, stop=True)
                last.then_inc(s_squ, 1)

            def transpose_tile(l, e, src, nj):
                if 10 * l + e:
                    pe.wait_ge(s_tre, 10 * l + e)
                for j in range(nj):
                    last = pe.transpose(banks(4, 6)[:, j * P:(j + 1) * P], src[:, j * P:(j + 1) * P], ident[:])
                last.then_inc(s_tr, 1)

            def sgu_mix(l, f):
                pe.wait_ge(s_svt, l + 1)
                if 2 * l + f:
                    pe.wait_ge(s_mixu, 2 * l + f)
                for j in range(width(l) // P):
                    for g in range(2):
                        c = f * P + g * 64
                        last = pe.matmul(banks(6, 8)[64 * g:64 * g + 64, j * P:(j + 1) * P], SVT[:, j, c:c + 64],
                                         sgw[:, 2 * f + g, :], start=True, stop=True)
                last.then_inc(s_mix, 1)

            def gates(l):
                pe.wait_ge(s_wgl, l + 1)
                pe.wait_ge(s_tre, 10 * (l + 1))
                for k in range(KT):
                    for a, b in ranges(T):
                        out = banks(4, 6)[0:16, a:b]
                        pe.matmul(out, wgh[:, k, :], XH[:, k, a:b], start=k == 0, stop=False)
                        pe.matmul(out, wgh[:, k, :], XL[:, k, a:b], start=False, stop=False)
                        last = pe.matmul(out, wgl[:, k, :], XH[:, k, a:b], start=False, stop=k == KT - 1)
                last.then_inc(s_grow, 1)
                pe.wait_ge(s_growe, l + 1)
                for j in range(NJ):
                    last = pe.transpose(PS[:, 4, 16 * j:16 * j + 16], grow[:, j * P:(j + 1) * P], ident[0:16, 0:16])
                last.then_inc(s_gate, 1)

            def forget_sums(l):
                pe.wait_ge(s_lf, l + 1)
                for d in range(2):
                    out = banks(5, 6)[:, 0:NJ * 8].rearrange("p (j e) -> p j e", e=8)[:, :, 4 * d:4 * d + 4]
                    last = pe.matmul(out, tri[:, d, :], lf[:, 2, :, 4 * d:4 * d + 4], start=True, stop=True)
                last.then_inc(s_bt, 1)

            def mlstm(l):
                n_end = l * LAYER_TILES + N_IN
                pe.wait_ge(s_btm, l + 1)
                pe.wait_ge(s_evac, n_end)
                for i, src in enumerate((lf[:, 1], lf[:, 2], btm[:])):
                    for j in range(NJ):
                        c = i * T + j * P
                        last = pe.transpose(banks(0, 5)[0:8, c:c + P], src[:, j, :], ident[:])
                last.then_inc(s_rows, 1)
                pe.wait_ge(s_rowl, 3 * (l + 1))

                def spread(bank, i, d, j):
                    for h in range(HEADS):
                        r = 4 * d + h
                        out = PS[:, bank, h * P:(h + 1) * P]
                        pe.matmul(out, selh[:, r, :], rhl[i][0][:, j * P:(j + 1) * P], start=True, stop=False)
                        last = pe.matmul(out, selh[:, r, :], rhl[i][1][:, j * P:(j + 1) * P], start=False, stop=True)
                    return last

                def exponents(t):
                    d, j, first, gives = mlstm_steps(l)[t]
                    c = 2 * NJ * l + t
                    o = outputs_before(l, t)
                    js = slice(j * P, (j + 1) * P)
                    if c:
                        pe.wait_ge(s_w1, c)
                    spread(0, 0, d, j).then_inc(s_nm, 1)
                    if c:
                        pe.wait_ge(s_wie, c)
                    last = spread(1, 1, d, j)
                    if gives:
                        last = spread(2, 2, d, j)
                    last.then_inc(s_wi, 1)
                    if gives:
                        if o:
                            pe.wait_ge(s_p, o)
                        for h in range(HEADS):
                            last = pe.matmul(PS[:, 3, h * P:(h + 1) * P], kfm[:, h, js], qfm[:, h, js], start=True, stop=True)
                        last.then_inc(s_s, 1)

                steps = mlstm_steps(l)
                exponents(0)
                for t, (d, j, first, gives) in enumerate(steps):
                    c = 2 * NJ * l + t
                    o = outputs_before(l, t)
                    if t + 1 < len(steps):
                        exponents(t + 1)
                    if gives:
                        pe.wait_ge(s_p, o + 1)
                        if o:
                            pe.wait_ge(s_nde, o)
                        if not first:
                            pe.wait_ge(s_qw, weighted_before(l, t) + 1)
                            pe.wait_ge(s_st, c - 1)
                        for h in range(HEADS):
                            last = pe.matmul(PS[:, 4, h * P:(h + 1) * P], vtm[:, j, h, :], Pp[c % 2][:, h, :], start=True, stop=first)
                            if not first:
                                last = pe.matmul(PS[:, 4, h * P:(h + 1) * P], ST[d][:, h, 0, :], Qw[c % 2][:, h, :], start=False, stop=True)
                        for h in range(HEADS):
                            last = pe.matmul(PS[:, 5, h * P:(h + 1) * P], ones[:], Pp[c % 2][:, h, :], start=True, stop=first)
                            if not first:
                                last = pe.matmul(PS[:, 5, h * P:(h + 1) * P], ST[d][:, h, 1, :], Qw[c % 2][:, h, :], start=False, stop=True)
                        last.then_inc(s_nd, 1)
                    pe.wait_ge(s_ks, c + 1)
                    if c:
                        pe.wait_ge(s_st, c)
                    for h in range(HEADS):
                        out = banks(6, 8)[:, 2 * h * P:2 * (h + 1) * P]
                        pe.matmul(out[:, 0:P], Ks[c % 2][:, h, :], vtm[:, j, h, :], start=True, stop=True)
                        last = pe.matmul(out[:, P:2 * P], Ks[c % 2][:, h, :], ones[:], start=True, stop=True)
                    last.then_inc(s_u, 1)

            def mixer_stats(l):
                w = width(l)
                for h in range(HEADS):
                    pe.wait_ge(s_hsq, 4 * l + h + 1)
                    for a, b in ranges(w):
                        last = pe.matmul(banks(2 * h, 2 * h + 2)[:, a:b], ones[:], Z[:, h, a:b], start=True, stop=True)
                    last.then_inc(s_hss, 1)
                pe.wait_ge(s_hr, l + 1)
                for f in range(2):
                    for a, b in ranges(w):
                        last = pe.matmul(banks(0, 2)[:, a:b], ones[:], AC[:, f, a:b], start=f == 0, stop=f == 1)
                last.then_inc(s_csum, 1)
                pe.wait_ge(s_csq, l + 1)
                for f in range(2):
                    for a, b in ranges(w):
                        last = pe.matmul(banks(2, 4)[:, a:b], ones[:], Z[:, f, a:b], start=f == 0, stop=f == 1)
                last.then_inc(s_cvar, 1)

            pe.wait_ge(s_one, 3)
            pe.wait_ge(s_const, 16 * 7)
            for l in range(DEPTH):
                n0 = l * LAYER_TILES
                if l == 0:
                    pe.wait_ge(s_cact, 1)
                    for m in range(MODS - MOD_V):
                        pe.wait_ge(s_modw[m % MOD_P], 16 * (m // MOD_P + 1))
                        for k in range(KT):
                            last = pe.matmul(PS[:, 5, 2 * m:2 * m + 2], modp[m % MOD_P][:, k, :], cact[:, k, :],
                                             start=k == 0, stop=k == KT - 1)
                        last.then_inc(s_modd, 1)
                norm(2 * l, T)
                first_tiles(pe, n0, XH, XL, width(l), 2 * KT * l)
                for t in range(2, N_IN):
                    gemm_tile(pe, n0 + t, XH, XL, width(l, t))
                    if t in (9, 10):
                        pe.wait_ge(s_gel, 2 * l + t - 8)
                        transpose_tile(l, t - 9, Z[:, t - 9 + 2], width(l) // P)
                    if 11 <= t < 15:
                        pe.wait_ge(s_evac, n0 + t - 2)
                        transpose_tile(l, t - 9, kfm[:, t - 11], NJ)
                    if 15 <= t < 19:
                        pe.wait_ge(s_evac, n0 + t - 2)
                        transpose_tile(l, t - 9, Z[:, t - 15], NJ)
                    if t in (18, 19):
                        sgu_mix(l, t - 18)
                    if t == 20:
                        gates(l)
                    if t == 22:
                        forget_sums(l)
                mlstm(l)
                mixer_stats(l)
                pe.wait_ge(s_y, KT * (l + 1))
                with pe.Fori(0, 2) as i:
                    for u in range(4):
                        gemm_tile(pe, n0 + N_IN + u, XH, XL, width(l), 4 * i)
                norm(2 * l + 1, width(l))
                for p, (h0, hn) in enumerate(PARTS):
                    s = part_start(l, p)
                    if p == 0:
                        first_tiles(pe, s, XH, XL, width(l), KT * (2 * l + 1))
                        for u in (2, 3):
                            gemm_tile(pe, s + u, XH, XL, width(l))
                    with pe.Fori(p == 0, 2 * hn // 4) as i:
                        for u in range(4):
                            gemm_tile(pe, s + u, XH, XL, width(l), 4 * i)


                    def hidden_ready(k):
                        pe.wait_ge(s_used, used(s + 2 * k + 1))
                    with pe.Fori(0, 2) as i:
                        for u in range(4):
                            gemm_tile(pe, s + 2 * hn + u, HH, HL, width(l), 4 * i, hn, hidden_ready if u == 0 else None)
            norm(2 * DEPTH, SEQ)
            second_pe(pe)

        @block.scalar
        def _(act):
            links = [0]

            def link(ins):
                links[0] += 1
                ins.then_inc(s_ach, 1)
                act.wait_ge(s_ach, links[0])

            def rstd(dst, src, scale, eps=0):
                link(act.activation(dst, src, ACT.Ln, bias=eps_c[:, eps:eps + 1], scale=scale))
                return act.activation(dst, dst, ACT.Exp, scale=-0.5)

            def norm(q, l, w):
                act.wait_ge(s_squ, q + 1)
                rs = MT if q in (0, 2) else TH
                rstd(rs[:, 0:w], banks(6, 8)[:, 0:w], 1.0 / D).then_inc(s_rstd, 1)
                for k in range(KT):
                    act.wait_ge(s_xn, KT * q + k + 1)
                    for n, (a, b) in enumerate(ranges(w)):
                        last = act.activation(XH[:, k, a:b], Z[:, k % 4, a:b], ACT.Identity, bias=mods[l][:, 24 * (q % 2) + k, n:n + 1])
                    last.then_inc(s_xh, 1)
                act.wait_ge(s_xl, KT * (q + 1))

            def load_mod(l, slot, m):
                act.dma_start(modv[4 + slot][:], m).then_inc(s_mvw[4 + slot], 16)

            def mod_tile(l, m):
                return wmod_d[l][bass.ds(m, 1)].rearrange("a p n -> (a p) n")

            def silu_c(l):
                if l:
                    act.dma_start(cb[:].rearrange("p a k -> p (a k)"), cb_d).then_inc(s_cb, 16)
                act.wait_ge(s_cb, 16 * (l + 1))
                act.activation(cbt[:], cb[:], ACT.Tanh, scale=0.5).then_inc(s_cbt, 1)

            def evacuate(s, out, func=ACT.Identity, bias=0.0, scale=1.0, w=T, dyn=0, need=None, signal=True):
                act.wait_ge(s_tile, s + 1 + dyn)
                if need is not None:
                    act.wait_ge(s_used, need)
                ins = act.activation(out, acc(s)[:, 0:w], func, bias=bias, scale=scale)
                return ins.then_inc(s_evac, 1) if signal else ins

            def residual_tiles(s0, l, gate, dyn, w, u, q=None):
                s = s0 + u
                act.wait_ge(s_tile, s + 1 + dyn)
                act.wait_ge(s_used, used(s - 4) + dyn)
                for n, (a, b) in enumerate(ranges(w)):
                    last = act.activation(Z[:, s % 4, a:b], acc(s)[:, a:b], ACT.Identity,
                                          scale=mods[l][:, bass.ds(gate + u + dyn, 1), n:n + 1].rearrange("p a b -> p (a b)"))
                last.then_inc(s_evac, 1)
                if q is not None:
                    act.wait_ge(s_used, used(s) + dyn)
                    act.wait_ge(s_acc, KT * q + u - 1 + dyn)
                    x = X[:, bass.ds(u + dyn, 1), 0:w].rearrange("p a t -> p (a t)")
                    act.activation(SQ[1][u % 2][:, 0:w], x, ACT.Square).then_inc(s_sq, 1)

            act.wait_ge(s_const, 16 * 7)
            act.wait_ge(s_one, 3)
            act.activation(cth[:], cact[:], ACT.Tanh, scale=0.5).then_inc(s_cth, 1)
            silu_c(0)
            act.wait_ge(s_x, 16)
            for k in range(KT):
                if k >= 2:
                    act.wait_ge(s_acc, k - 1)
                act.activation(SQ[0][k % 2][:], X[:, k], ACT.Square).then_inc(s_sq, 1)
            for l in range(DEPTH):
                n0 = l * LAYER_TILES
                w = width(l)
                act.wait_ge(s_par, 48 * (l + 1))
                act.activation(wgh[:], wg[:], ACT.Copy).then_inc(s_wgh, 1)
                act.wait_ge(s_mod, l + 1)
                norm(2 * l, l, T)
                for t in range(N_IN):
                    n = n0 + t
                    b = bcol[:, t:t + 1]
                    slot = Z[:, n % 4, 0:w]
                    if t in (0, 2):
                        evacuate(n, slot, ACT.Tanh, b, 0.5, w)
                    elif t < K_T:
                        evacuate(n, slot, ACT.Identity, b, 1.0, w, need=used(n - 4) if t >= 4 else None)
                    elif t < V_T:
                        evacuate(n, kfm[:, t - K_T], ACT.Identity, b, K_SCALE)
                    elif t < Q_T:
                        act.wait_ge(s_tre, 10 * l + 2)
                        act.wait_ge(s_used, used(n0 + U_T + 1))
                        evacuate(n, Z[:, n % 4], ACT.Identity, b, 1.0)
                    elif t < O_T:
                        act.wait_ge(s_gel, 2 * (l + 1))
                        evacuate(n, qfm[:, t - Q_T, 0:w], ACT.Identity, b, 1.0, w)
                    else:
                        act.wait_ge(s_mix, 2 * (l + 1))
                        evacuate(n, tho[:, t - O_T, 0:w], ACT.Tanh, b, 0.5, w)
                    if 6 <= t < 10:
                        act.wait_ge(s_gin, 4 * l + t - 5)
                        g = GT[:, t - 6, 0:w]
                        act.activation(g, g, ACT.Tanh, scale=GELU_C).then_inc(s_gth, 1)
                    if t == 11:
                        act.wait_ge(s_svv, l + 1)
                        rstd(bmv[:, 0:w // P, 1:2], bmv[:, 0:w // P, 1:2], 1.0).then_inc(s_svr, 1)
                    if t == 20:
                        act.wait_ge(s_grow, l + 1)
                        act.activation(grow[:], banks(4, 6)[0:16, 0:T], ACT.Copy).then_inc(s_growe, 1)
                    if t == 21:
                        act.wait_ge(s_gtm, l + 1)
                        sp = lf[:, 0].rearrange("p j (d h) -> p j d h", d=2)
                        for j in range(NJ):
                            last = act.activation(sp[:, j], gt[:, j, :, 1, :], ACT.Abs)
                        link(last)
                        link(act.activation(lf[:, 0], lf[:, 0], ACT.Exp, scale=-1.0))
                        act.activation(lf[:, 0], lf[:, 0], ACT.Ln, bias=1.0).then_inc(s_lfa, 1)
                act.wait_ge(s_row, l + 1)
                for i, r in enumerate((ri, rb, rf)):
                    act.activation(rhl[i][0][:], r[:], ACT.Copy).then_inc(s_rowh, 1)

                def exponentials(t):
                    gives = mlstm_steps(l)[t][3]
                    c = 2 * NJ * l + t
                    act.wait_ge(s_wi, c + 1)
                    if c >= 2:
                        act.wait_ge(s_st, c - 1)
                    if weighted_before(l, max(t - 1, 0)):
                        act.wait_ge(s_qw, weighted_before(l, max(t - 1, 0)))
                    last = act.activation(WIs[c % 2][:], PS[:, 1, :].rearrange("p (h t) -> p h t", h=HEADS), ACT.Exp)
                    if gives:
                        if outputs_of_slot(l, t):
                            act.wait_ge(s_h, outputs_of_slot(l, t))
                        last = act.activation(EMs[c % 2][:], PS[:, 2, :].rearrange("p (h t) -> p h t", h=HEADS), ACT.Exp)
                    last.then_inc(s_wie, 1)
                    act.wait_ge(s_w1, c + 1)
                    if c >= 2:
                        act.wait_ge(s_ks, c - 1)
                    if outputs_of_slot(l, t):
                        act.wait_ge(s_p, outputs_of_slot(l, t))
                    act.activation(Ee[c % 2][:], W1[:], ACT.Exp).then_inc(s_e, 1)

                steps = mlstm_steps(l)
                exponentials(0)
                for t, (d, j, first, gives) in enumerate(steps):
                    if t + 1 < len(steps):
                        exponentials(t + 1)
                    if gives:
                        o = outputs_before(l, t)
                        act.wait_ge(s_nd, o + 1)
                        if o:
                            act.wait_ge(s_h, o)
                        act.activation(AD[:], PS[:, 5, :].rearrange("p (h t) -> p h t", h=HEADS), ACT.Abs)
                        act.activation(HN[:], PS[:, 4, :].rearrange("p (h t) -> p h t", h=HEADS), ACT.Copy).then_inc(s_nde, 1)
                act.wait_ge(s_h, outputs_before(l + 1, 0))
                act.wait_ge(s_st, 2 * NJ * (l + 1))
                for h in range(HEADS):
                    act.activation(Z[:, h, 0:w], H[:, h, 0:w], ACT.Square).then_inc(s_hsq, 1)
                for h in range(HEADS):
                    act.wait_ge(s_hss, 4 * l + h + 1)
                    last = act.activation(RH[:, h, 0:w], banks(2 * h, 2 * h + 2)[:, 0:w], ACT.Ln, bias=eps_c[:, 0:1], scale=1.0 / HD)
                link(last)
                act.activation(RH[:, :, 0:w], RH[:, :, 0:w], ACT.Exp, scale=-0.5).then_inc(s_hr, 1)
                act.wait_ge(s_csum, l + 1)
                act.activation(MU[:, 0:w], banks(0, 2)[:, 0:w], ACT.Copy, scale=1.0 / 256).then_inc(s_cmu, 1)
                act.wait_ge(s_cd, l + 1)
                act.activation(Z[:, 0:2, 0:w], AC[:, :, 0:w], ACT.Square).then_inc(s_csq, 1)
                act.wait_ge(s_cvar, l + 1)
                rstd(MU[:, 0:w], banks(2, 4)[:, 0:w], 1.0 / 256).then_inc(s_crs, 1)
                act.wait_ge(s_cl, l + 1)
                act.activation(Z[:, 0:2, 0:w], AC[:, :, 0:w], ACT.Tanh, scale=0.5).then_inc(s_cta, 1)
                for i in range(KT):
                    act.wait_ge(s_yf, KT * l + i + 1)
                    src = H[:, i] if i < 4 else Ug[:, i - 4] if i < 6 else AC[:, i - 6]
                    act.activation(XH[:, i, 0:w], src[:, 0:w], ACT.Copy).then_inc(s_yh, 1)
                act.wait_ge(s_y, KT * (l + 1))
                with act.Fori(0, 2) as i:
                    for u in range(4):
                        residual_tiles(n0 + N_IN, l, 16, 4 * i, w, u, 2 * l + 1)
                norm(2 * l + 1, l, w)
                more = l + 1 < DEPTH
                if more:
                    for m in range(2):
                        load_mod(l + 1, m, wmod_d[l + 1, m])
                    silu_c(l + 1)
                    act.wait_ge(s_cba, l + 2)
                    for m in range(2, 4):
                        load_mod(l + 1, m, wmod_d[l + 1, m])
                for p, (h0, hn) in enumerate(PARTS):
                    s = part_start(l, p)
                    with act.Fori(0, 2 * hn // 4) as i:
                        for e in range(2):
                            n = s + 2 * e
                            pair = FT * l + h0 + e
                            act.wait_ge(s_tile, n + 1 + 4 * i)
                            act.wait_ge(s_used, used(n - 4) + 4 * i)
                            if pair:
                                act.wait_ge(s_hf, pair + 2 * i)
                            act.activation(Z[:, n % 4, 0:w], acc(n)[:, 0:w], ACT.Identity)
                            act.activation(TH[:, 0:w], acc(n)[:, 0:w], ACT.Tanh, scale=0.5).then_inc(s_evac, 1)
                            evacuate(n + 1, Z[:, (n + 1) % 4, 0:w], w=w, dyn=4 * i, need=used(n - 3) + 4 * i)
                            act.wait_ge(s_hf, pair + 1 + 2 * i)
                            act.activation(HH[:, bass.ds(2 * i + e, 1), 0:w].rearrange("p a t -> p (a t)"), Z[:, (n + 1) % 4, 0:w],
                                           ACT.Copy).then_inc(s_hh, 1)
                        if more:
                            for u in range(4):
                                m = 2 * h0 + u
                                act.wait_ge(s_mvd, MOD_V + m + 1 + 4 * i)
                                load_mod(l + 1, u, mod_tile(l + 1, m + 4 + 4 * i))
                    with act.Fori(0, 2) as i:
                        for u in range(4):
                            residual_tiles(s + 2 * hn, l, 40, 4 * i, w, u, 2 * l + 2 if p == len(PARTS) - 1 else None)
            second_act(act, link, rstd, evacuate)

        @block.vector
        def _(dve):
            links = [0]

            def link(ins):
                links[0] += 1
                ins.then_inc(s_dch, 1)
                dve.wait_ge(s_dch, links[0])

            def linked_loop(n, per, body):
                start = links[0]
                with dve.Fori(0, n) as i:
                    count = [0]

                    def link_in(ins):
                        count[0] += 1
                        ins.then_inc(s_dch, 1)
                        dve.wait_ge(s_dch, start + count[0] + per * i)
                    body(i, link_in)
                    assert count[0] == per, count
                links[0] = start + n * per

            def col(l, name, i=0):
                return pc[:, l, PC[name] + i:PC[name] + i + 1]

            def norm(q, l, w):
                rs = MT if q in (0, 2) else TH
                second = q % 2
                dve.wait_ge(s_rstd, q + 1)

                def scaled(k):
                    if k >= 4:
                        dve.wait_ge(s_xl, KT * q + k - 3)
                    for n, (a, b) in enumerate(ranges(w)):
                        last = dve.scalar_tensor_tensor(out=Z[:, k % 4, a:b], in0=X[:, k, a:b], scalar=nsc[:, second, k, n:n + 1],
                                                        in1=rs[:, a:b], op0=ALU.mult, op1=ALU.mult)
                    last.then_inc(s_xn, 1)

                def lower(k):
                    dve.wait_ge(s_xh, KT * q + k + 1)
                    for n, (a, b) in enumerate(ranges(w)):
                        last = dve.scalar_tensor_tensor(out=XL[:, k, a:b], in0=Z[:, k % 4, a:b], scalar=mods[l][:, 24 * second + k, n:n + 1],
                                                        in1=XH[:, k, a:b].bitcast(FP32), op0=ALU.add, op1=ALU.subtract)
                    last.then_inc(s_xl, 1)
                scaled(0)
                for k in range(1, KT):
                    scaled(k)
                    lower(k - 1)
                lower(KT - 1)

            def activate_c(l):
                dve.wait_ge(s_cbt, l + 1)
                link(dve.scalar_tensor_tensor(out=cb[:], in0=cbt[:], scalar=1.0, in1=cb[:], op0=ALU.add, op1=ALU.mult))
                dve.tensor_scalar(cb[:], cb[:], 0.5, None, ALU.mult).then_inc(s_cba, 1)
                dve.wait_ge(s_cba, l + 1)

            def mod_tiles(l, first, dyn, slots, loads, link_in):
                for u in range(4):
                    dve.wait_ge(s_mvw[slots + u], 16 * loads + 4 * dyn)
                    for n in range(2):
                        last = dve.tensor_tensor_reduce(out=cprod[:], in0=modv[slots + u][:], in1=cb[:, n, :], scale=1.0, scalar=0.0,
                                                        op0=ALU.mult, op1=ALU.add, accum_out=macc[:, u, n:n + 1])
                        if n == 0:
                            link_in(last)
                    last.then_inc(s_mvd, 1)
                    dve.wait_ge(s_mvd, (MOD_V if l else 0) + first + u + 1 + dyn)
                at = bass.ds(first + dyn, 4)
                link_in(dve.tensor_copy(mods[l][:, at, :], macc[:]))

            def convolve(l, w, part, parts):
                grid = lambda v: v.rearrange("p (r c) -> p r c", c=GRID)
                todo = [(0, GRID, 1, CONV_K // 2, grid, 0, SEQ), (1, SEQ, GRID, SEQ // GRID - 1, None, 0, SEQ)]
                if w == T:
                    todo += [(f, CTX, 1, CONV_K // 2, None, SEQ, T) for f in range(2)]
                taps = [(line, o) for line in todo for o in [0] + [o for o in range(-line[3], line[3] + 1) if o]]
                for (f, n, step, reach, shape, t0, t1), o in taps[part * len(taps) // parts:(part + 1) * len(taps) // parts]:
                    src, dst = YC[:, f, t0:t1], AC[:, f, t0:t1]
                    tap = col(l, "cw", f * CONV_K + CONV_K // 2 + o)
                    if o == 0:
                        link(dve.tensor_scalar(dst, src, tap, col(l, "cb", f), ALU.mult, ALU.add))
                        continue
                    a, b = max(0, -o * step), n - max(0, o * step)
                    if shape:
                        cut = lambda v, p, q: shape(v)[:, :, p:q]
                    else:
                        cut = lambda v, p, q: v[:, p:q]
                    link(dve.scalar_tensor_tensor(out=cut(dst, a, b), in0=cut(src, a + o * step, b + o * step),
                                                  scalar=tap, in1=cut(dst, a, b), op0=ALU.mult, op1=ALU.add))

            def add_residual(s0, u, dyn, w, q=None):
                s = s0 + u
                dve.wait_ge(s_evac, s + 1 + dyn)
                x = X[:, bass.ds(u + dyn, 1), 0:w].rearrange("p a t -> p (a t)")
                dve.tensor_tensor(x, x, Z[:, s % 4, 0:w], ALU.add).then_inc(s_used, 1)
                if q is not None:
                    dve.wait_ge(s_sq, KT * q + u + 1 + dyn)
                    dve.wait_ge(s_acc, KT * q + u + dyn)
                    dve.tensor_tensor(SS[1][:, 0:w], SS[1][:, 0:w], SQ[1][u % 2][:, 0:w], ALU.add).then_inc(s_acc, 1)

            dve.wait_ge(s_const, 16 * 7)
            dve.wait_ge(s_cth, 1)
            link(dve.scalar_tensor_tensor(out=cth[:], in0=cth[:], scalar=1.0, in1=cact[:], op0=ALU.add, op1=ALU.mult))
            dve.tensor_scalar(cact[:], cth[:], 0.5, None, ALU.mult).then_inc(s_cact, 1)
            activate_c(0)
            for g in range(MOD_V // 4):
                mod_tiles(0, 4 * g, 0, 4 * (g % 2), g // 2 + 1, link)
            for l in range(DEPTH):
                n0 = l * LAYER_TILES
                w = width(l)
                nj = w // P
                dve.wait_ge(s_wgh, l + 1)
                dve.tensor_tensor(wgl[:], wg[:], wgh[:].bitcast(FP32), ALU.subtract).then_inc(s_wgl, 1)
                mod = mods[l]
                if l == 0:
                    dve.wait_ge(s_modd, MODS - MOD_V)
                    link(dve.tensor_copy(mod[:, MOD_V:MODS, :], PS[:, 5, 0:2 * (MODS - MOD_V)].rearrange("p (m o) -> p m o", o=2)))
                mb = pc[:, l, PC["b_mod"]:PC["b_mod"] + 48].rearrange("p (m o) -> p m o", o=1).to_broadcast([P, 48, 2])
                link(dve.tensor_tensor(mod[:], mod[:], mb, ALU.add))
                for i, name in enumerate(("norm1", "norm2")):
                    g = pc[:, l, PC[name]:PC[name] + KT].rearrange("p (m o) -> p m o", o=1).to_broadcast([P, KT, 2])
                    at = 8 + 24 * i
                    link(dve.scalar_tensor_tensor(out=nsc[:, i], in0=mod[:, at:at + KT, :], scalar=1.0, in1=g, op0=ALU.add, op1=ALU.mult))
                link(dve.tensor_copy(bcol[:], pc[:, l, PC["b_in"]:PC["b_in"] + N_IN]))
                dve.tensor_scalar(bcol[:, 0:1], bcol[:, 0:1], 0.5, None, ALU.mult)
                dve.tensor_scalar(bcol[:, 2:3], bcol[:, 2:3], 0.5, None, ALU.mult)
                dve.tensor_scalar(bcol[:, O_T:N_IN], bcol[:, O_T:N_IN], 0.5, None, ALU.mult)
                dve.tensor_scalar(bcol[:, K_T:V_T], bcol[:, K_T:V_T], K_SCALE, None, ALU.mult).then_inc(s_mod, 1)
                dve.wait_ge(s_mod, l + 1)
                norm(2 * l, l, T)
                for f in range(2):
                    dve.wait_ge(s_evac, n0 + 2 * f + 2)
                    g = Z[:, 2 * f, 0:w]
                    link(dve.tensor_scalar(g, g, 1.0, 0.5, ALU.add, ALU.mult))
                    dve.tensor_tensor(YC[:, f, 0:w], g, Z[:, 2 * f + 1, 0:w], ALU.mult).then_inc(s_used, 2)
                for i in range(4):
                    dve.wait_ge(s_evac, n0 + U_T + i + 1)
                    g, z = GT[:, i, 0:w], Z[:, i, 0:w]
                    link(dve.tensor_tensor(g, z, z, ALU.mult))
                    link(dve.tensor_scalar(g, g, GELU_A, 1.0, ALU.mult, ALU.add))
                    dve.tensor_tensor(g, g, z, ALU.mult).then_inc(s_gin, 1)
                for i in range(4):
                    dve.wait_ge(s_gth, 4 * l + i + 1)
                    g, z = GT[:, i, 0:w], Z[:, i, 0:w]
                    link(dve.scalar_tensor_tensor(out=g, in0=g, scalar=1.0, in1=z, op0=ALU.add, op1=ALU.mult))
                    out = Ug[:, i, 0:w] if i < 2 else z
                    dve.tensor_scalar(out, g, 0.5, None, ALU.mult).then_inc(s_used if i < 2 else s_gel, 1)
                for e in range(2):
                    dve.wait_ge(s_tr, 10 * l + e + 1)
                    dve.tensor_copy(SVT[:, 0:nj, e * P:(e + 1) * P],
                                    banks(4, 6)[:, 0:nj * P].rearrange("p (j c) -> p j c", c=P)).then_inc(s_tre, 1)
                dve.wait_ge(s_tre, 10 * l + 2)
                dve.wait_ge(s_par, 48 * (l + 1))
                for j in range(nj):
                    last = dve.bn_stats(bst[:, j, :], SVT[:, j, :])
                link(last)
                for j in range(nj):
                    last = dve.bn_aggr(bmv[:, j, :], bst[:, j, :])
                last.then_inc(s_svv, 1)
                dve.wait_ge(s_svr, l + 1)
                for j in range(nj):
                    last = dve.tensor_scalar(SVT[:, j, :], SVT[:, j, :], bmv[:, j, 0:1], bmv[:, j, 1:2], ALU.subtract, ALU.mult)
                link(last)
                for i in range(2):
                    row = srow[:, 256 * i:256 * (i + 1)].rearrange("p (a c) -> p a c", a=1).to_broadcast([P, nj, 256])
                    last = dve.tensor_tensor(SVT[:, 0:nj, :], SVT[:, 0:nj, :], row, (ALU.mult, ALU.add)[i])
                    if i == 0:
                        link(last)
                last.then_inc(s_svt, 1)
                for e in range(2, 10):
                    dve.wait_ge(s_tr, 10 * l + e + 1)
                    dst = ktm if e < 6 else vtm
                    dve.tensor_copy(dst[:, :, (e - 2) % 4, :], banks(4, 6)[:, 0:T].rearrange("p (j c) -> p j c", c=P)).then_inc(s_tre, 1)
                    convolve(l, w, e - 2, 8)
                for f in range(2):
                    dve.wait_ge(s_mix, 2 * l + f + 1)
                    bias = srow[:, SROW_B + f * P:SROW_B + (f + 1) * P].rearrange("p (a c) -> p a c", a=1).to_broadcast([P, nj, P])
                    z = Z[:, f, 0:w].rearrange("p (j c) -> p j c", c=P)
                    dve.tensor_tensor(z, banks(6, 8)[:, 0:w].rearrange("p (j c) -> p j c", c=P), bias, ALU.add).then_inc(s_mixu, 1)
                    dve.wait_ge(s_mixu, 2 * l + f + 1)
                    link(dve.tensor_tensor(Ug[:, f, 0:w], Ug[:, f, 0:w], Z[:, f, 0:w], ALU.mult))
                dve.wait_ge(s_gate, l + 1)
                gb = srow[:, SROW_G:SROW_G + 16].rearrange("p (a c) -> p a c", a=1).to_broadcast([P, NJ, 16])
                dve.tensor_tensor(gt[:].rearrange("p j d i h -> p j (d i h)"), PS[:, 4, 0:16 * NJ].rearrange("p (j c) -> p j c", c=16),
                                  gb, ALU.add).then_inc(s_gtm, 1)
                dve.wait_ge(s_lfa, l + 1)
                lfv = lf[:].rearrange("p n j (d h) -> p n j d h", d=2)
                for d in range(2):
                    last = dve.tensor_scalar(lfv[:, 1, :, d, :], gt[:, :, d, 1, :], 0.0, None, ALU.min)
                link(last)
                link(dve.tensor_tensor(lf[:, 2], lf[:, 1], lf[:, 0], ALU.subtract))
                for d in range(2):
                    last = dve.tensor_copy(lfv[:, 1, :, d, :], gt[:, :, d, 0, :])
                last.then_inc(s_lf, 1)
                dve.wait_ge(s_lf, l + 1)
                dve.wait_ge(s_bt, l + 1)
                dve.tensor_copy(btm[:].rearrange("p j e -> p (j e)"), PS[:, 5, 0:NJ * 8]).then_inc(s_btm, 1)
                dve.wait_ge(s_btm, l + 1)
                link(dve.tensor_tensor(gcol[:], lf[:, 1], btm[:], ALU.subtract))
                dve.wait_ge(s_rows, l + 1)
                for i, r in enumerate((ri, rf, rb)):
                    last = dve.tensor_copy(r[:], banks(0, 5)[0:8, i * T:(i + 1) * T])
                link(last)
                scan = lambda o, f, i, m0: link(dve.tensor_tensor_scan(o, f, i, m0, ALU.add, ALU.max))
                cs, ss = slice(SEQ, T), slice(0, SEQ)
                scan(rm[:, cs], rf[:, cs], ri[:, cs], 0.0)
                scan(rm[:, ss], rf[:, ss], ri[:, ss], rm[:, T - 1:T])
                scan(r2[:, cs][:, ::-1], rf[:, cs][:, ::-1], ri[:, cs][:, ::-1], 0.0)
                scan(r2[:, ss][:, ::-1], rf[:, ss][:, ::-1], ri[:, ss][:, ::-1], r2[:, SEQ:SEQ + 1])
                link(dve.memset(mprev[:], 0.0))
                dve.tensor_copy(mprev[:, 0, NJ - 1:NJ], rm[:, T - P - 1:T - P])
                dve.tensor_copy(mprev[:, 0, 0:1], rm[:, T - 1:T])
                dve.tensor_copy(mprev[:, 0, 1:NX], rm[:, P - 1:SEQ - P:P])
                link(dve.tensor_copy(mprev[:, 1, 0:NJ - 1], r2[:, P:T:P]))
                for one, two in ((rm[:], r2[:]), (mprev[:, 0], mprev[:, 1])):
                    link(dve.tensor_scalar(one, one, dsel[:, 0:1], None, ALU.mult))
                    link(dve.scalar_tensor_tensor(out=one, in0=two, scalar=dsel[:, 1:2], in1=one, op0=ALU.mult, op1=ALU.add))
                link(dve.tensor_copy(selh[:], ident[0:8, 0:8].rearrange("p (r c) -> p r c", c=1).to_broadcast([8, 8, P])))
                link(dve.tensor_tensor(ri[:], rb[:], rm[:], ALU.subtract))
                mp = mprev[:, 0].rearrange("p (j o) -> p j o", o=1).to_broadcast([8, NJ, P])
                dve.tensor_tensor(rb[:].rearrange("p (j t) -> p j t", t=P), ri[:].rearrange("p (j t) -> p j t", t=P), mp, ALU.add)
                dve.tensor_scalar(rf[:], rm[:], -1.0, None, ALU.mult).then_inc(s_row, 1)
                for i, r in enumerate((ri, rb, rf)):
                    dve.wait_ge(s_rowh, 3 * l + i + 1)
                    dve.tensor_tensor(rhl[i][1][:], r[:], rhl[i][0][:].bitcast(FP32), ALU.subtract).then_inc(s_rowl, 1)
                written = set()
                steps = mlstm_steps(l)

                def log_weights(t):
                    d, j = steps[t][0:2]
                    c = 2 * NJ * l + t
                    dve.wait_ge(s_nm, c + 1)
                    if c:
                        dve.wait_ge(s_e, c)
                    for h in range(HEADS):
                        last = dve.scalar_tensor_tensor(out=W1[:, h, :], in0=PS[:, 0, h * P:(h + 1) * P],
                                                        scalar=gcol[:, j, 4 * d + h:4 * d + h + 1], in1=mskd[:, d, :],
                                                        op0=ALU.add, op1=ALU.min)
                    last.then_inc(s_w1, 1)

                def weighted_scores(t):
                    c = 2 * NJ * l + t
                    if steps[t][3]:
                        dve.wait_ge(s_e, c + 1)
                        dve.wait_ge(s_s, outputs_before(l, t) + 1)
                        if outputs_of_slot(l, t):
                            dve.wait_ge(s_nd, outputs_of_slot(l, t))
                        dve.tensor_tensor(Pp[c % 2][:], PS[:, 3, :].rearrange("p (h t) -> p h t", h=HEADS), Ee[c % 2][:],
                                          ALU.mult).then_inc(s_p, 1)
                log_weights(0)
                weighted_scores(0)
                log_weights(1)
                for t, (d, j, first, gives) in enumerate(steps):
                    c = 2 * NJ * l + t
                    o = outputs_before(l, t)
                    if t + 1 < len(steps):
                        weighted_scores(t + 1)
                    dve.wait_ge(s_u, c + 1)
                    dve.wait_ge(s_wie, c + 1)
                    tl = P - 1 if d == 0 else 0
                    for h in range(HEADS):
                        st = ST[d][:, h].rearrange("p a c -> p (a c)")
                        up = banks(6, 8)[:, 2 * h * P:2 * (h + 1) * P]
                        if first:
                            last = dve.tensor_copy(st, up)
                        else:
                            last = dve.scalar_tensor_tensor(out=st, in0=st, scalar=WIs[c % 2][:, h, tl:tl + 1], in1=up, op0=ALU.mult, op1=ALU.add)
                    last.then_inc(s_st, 1)
                    if t + 2 < len(steps):
                        log_weights(t + 2)
                    dve.wait_ge(s_st, c + 1)
                    if gives:
                        dve.wait_ge(s_nde, o + 1)
                        link(dve.tensor_tensor(AD[:], AD[:], EMs[c % 2][:], ALU.max))
                        link(dve.reciprocal(AD[:], AD[:]))
                        hj = H[:, :, j * P:(j + 1) * P]
                        if j in written:
                            link(dve.tensor_tensor(HN[:], HN[:], AD[:], ALU.mult))
                            dve.tensor_tensor(hj, hj, HN[:], ALU.add).then_inc(s_h, 1)
                        else:
                            dve.tensor_tensor(hj, HN[:], AD[:], ALU.mult).then_inc(s_h, 1)
                        written.add(j)
                dve.wait_ge(s_h, outputs_before(l + 1, 0))
                dve.wait_ge(s_hr, l + 1)
                link(dve.tensor_scalar(tho[:, :, 0:w], tho[:, :, 0:w], 1.0, 0.5, ALU.add, ALU.mult))
                link(dve.tensor_tensor(H[:, :, 0:w], H[:, :, 0:w], RH[:, :, 0:w], ALU.mult))
                for h in range(HEADS):
                    dve.scalar_tensor_tensor(out=H[:, h, 0:w], in0=H[:, h, 0:w], scalar=col(l, "mg", h), in1=tho[:, h, 0:w],
                                             op0=ALU.mult, op1=ALU.mult).then_inc(s_yf, 1)

                def lower(i, src):
                    dve.wait_ge(s_yh, KT * l + i + 1)
                    dve.tensor_tensor(XL[:, i, 0:w], src[:, 0:w], XH[:, i, 0:w].bitcast(FP32), ALU.subtract).then_inc(s_y, 1)
                dve.wait_ge(s_cmu, l + 1)
                for f in range(2):
                    last = dve.tensor_tensor(AC[:, f, 0:w], AC[:, f, 0:w], MU[:, 0:w], ALU.subtract)
                last.then_inc(s_cd, 1)
                dve.wait_ge(s_crs, l + 1)
                for f in range(2):
                    last = dve.tensor_tensor(AC[:, f, 0:w], AC[:, f, 0:w], MU[:, 0:w], ALU.mult)
                link(last)
                for f in range(2):
                    last = dve.tensor_scalar(AC[:, f, 0:w], AC[:, f, 0:w], col(l, "cg", f), col(l, "clb", f), ALU.mult, ALU.add)
                last.then_inc(s_cl, 1)
                dve.wait_ge(s_cta, l + 1)
                link(dve.scalar_tensor_tensor(out=AC[:, :, 0:w], in0=Z[:, 0:2, 0:w], scalar=1.0, in1=AC[:, :, 0:w], op0=ALU.add, op1=ALU.mult))
                dve.tensor_scalar(AC[:, :, 0:w], AC[:, :, 0:w], 0.5, None, ALU.mult).then_inc(s_yf, 4)
                for i in range(KT):
                    if i == 4:
                        dve.wait_ge(s_y, KT * l + 4)
                    lower(i, H[:, i] if i < 4 else Ug[:, i - 4] if i < 6 else AC[:, i - 6])
                link(dve.memset(SS[1][:, 0:w], 0.0))
                with dve.Fori(0, 2) as i:
                    for u in range(4):
                        add_residual(n0 + N_IN, u, 4 * i, w, 2 * l + 1)
                norm(2 * l + 1, l, w)
                more = l + 1 < DEPTH
                if more:
                    activate_c(l + 1)
                for p, (h0, hn) in enumerate(PARTS):
                    s = part_start(l, p)

                    def hidden(i, link_in):
                        if more:
                            mod_tiles(l + 1, 2 * h0, 4 * i, 4, MOD_V // 8 + h0 // 2 + 1, link_in)
                        for e in range(2):
                            n = s + 2 * e
                            pair = FT * l + h0 + e
                            g, v = Z[:, n % 4, 0:w], Z[:, (n + 1) % 4, 0:w]
                            dve.wait_ge(s_evac, n + 2 + 4 * i)
                            link_in(dve.scalar_tensor_tensor(out=g, in0=TH[:, 0:w], scalar=1.0, in1=g, op0=ALU.add, op1=ALU.mult))
                            dve.scalar_tensor_tensor(out=v, in0=g, scalar=0.5, in1=v, op0=ALU.mult, op1=ALU.mult).then_inc(s_hf, 1)
                            dve.wait_ge(s_hh, pair + 1 + 2 * i)
                            at = bass.ds(2 * i + e, 1)
                            hh = HH[:, at, 0:w].rearrange("p a t -> p (a t)").bitcast(FP32)
                            dve.tensor_tensor(HL[:, at, 0:w].rearrange("p a t -> p (a t)"), v, hh, ALU.subtract).then_inc(s_used, 2)
                    linked_loop(2 * hn // 4, 7 if more else 2, hidden)
                    q = 2 * l + 2 if p == len(PARTS) - 1 else None
                    if q is not None:
                        if more:
                            mod_tiles(l + 1, MODS - 4, 0, 4, MOD_V // 8 + MODS // 4, link)
                        link(dve.memset(SS[1][:, 0:w], 0.0))
                    with dve.Fori(0, 2) as i:
                        for u in range(4):
                            add_residual(s + 2 * hn, u, 4 * i, w, q)
            second_dve(dve, link, linked_loop)

def tiles_of(w):
    k, n = w.shape[-2] // P, w.shape[-1] // P
    v = w.reshape(w.shape[:-2] + (k, P, n, P))
    m = v.ndim
    v = np.transpose(v, tuple(range(m - 4)) + (m - 2, m - 3, m - 4, m - 1))
    return np.ascontiguousarray(v.reshape(w.shape[:-2] + (n, P, k * P)))


def columns_of(v):
    v = v.reshape(v.shape[:-1] + (-1, P))
    return np.ascontiguousarray(np.moveaxis(v, -1, 0))


def kernel(**inputs):
    import concourse.bacc as _bacc
    from concourse.bass_utils import run_bass_kernel_spmd as _run
    a = {k: np.asarray(v) for k, v in inputs.items()}
    f = np.float32
    q, k, v, o, gate, sgu, conv = 0, 512, 1024, 1536, 2048, 2064, 2576
    order = [conv + 256, conv, conv + 384, conv + 128] + [sgu + i * P for i in range(4)]
    for base in (k, v, q, o):
        order += [base + i * P for i in range(4)]
    cols = np.concatenate([np.arange(c, c + P) for c in order])
    gcols = np.arange(gate, gate + 16)
    ts = np.arange(P)
    tri = (ts[:, None] <= ts[None, :]).astype(f)
    consts = np.zeros((P, N_CONST), f)
    consts[:, 0:P] = np.eye(P, dtype=f)
    consts[:, P:2 * P], consts[:, 2 * P:3 * P] = tri, tri.T
    consts[:, 3 * P:4 * P], consts[:, 4 * P:5 * P] = np.where(tri > 0, 0, NEG), np.where(tri.T > 0, 0, NEG)
    consts[0:4, 5 * P] = 1
    consts[4:8, 5 * P + 1] = 1
    par = []
    for l in range(DEPTH):
        cw = a["conv_w"][l].T.reshape(2, P, CONV_K)
        par.append(np.concatenate([columns_of(a["norm1_g"][l]), columns_of(a["norm2_g"][l]), columns_of(a["b_in"][l][cols]),
                                   columns_of(a["mlstm_g"][l]), cw[0], cw[1], columns_of(a["conv_b"][l]),
                                   columns_of(a["conv_ln_g"][l]), columns_of(a["conv_ln_b"][l]), columns_of(a["b_mod"][l])], axis=1))
    rows = []
    for l in range(DEPTH):
        sb = a["sgu_b"][l].reshape(2, 2, 1, P)
        sb = np.broadcast_to(sb, (2, 2, 64, P)).reshape(2, P, P)
        wide = lambda r: np.broadcast_to(r[None], (P, r.shape[0]))
        rows.append(np.concatenate([wide(a["sgu_ln_g"][l]), wide(a["sgu_ln_b"][l]), sb[0], sb[1], wide(a["b_in"][l][gcols])], axis=1))
    w_gu = a["w_gu"].reshape(DEPTH, D, 2, FT, P).transpose(0, 1, 3, 2, 4).reshape(DEPTH, D, 2 * FFN)
    wg = a["w_in"][:, :, gcols].reshape(DEPTH, KT, P, 16).transpose(0, 2, 1, 3)
    rows_of = a["w_mod"].transpose(0, 2, 1).reshape(DEPTH, MODS, P, D)
    wmod = np.concatenate([rows_of[0:1, 0:MOD_V], tiles_of(a["w_mod"])[0:1, MOD_V:]], axis=1)
    wmod = np.concatenate([wmod, rows_of[1:]])
    tokens = np.concatenate([a["x"][0], a["ctx"][0]], axis=0)
    feats = lambda m: np.ascontiguousarray(m.T.reshape(-1, P, m.shape[0]).transpose(1, 0, 2))
    arrays = {
        "xT": feats(tokens), "cT": feats(np.stack([a["c"][0], a["c_ctx"]])),
        "cb": np.broadcast_to(np.concatenate([a["c"][0], a["c_ctx"]])[None], (P, 2 * D)),
        "pc": np.stack(par, axis=1), "fin": columns_of(a["final_g"]), "srow": np.stack(rows), "consts": consts,
        "sguw": a["sgu_w"].transpose(0, 3, 1, 2), "wg": wg, "wmod": wmod, "win": tiles_of(a["w_in"][:, :, cols]),
        "wout": tiles_of(a["w_out"]), "wgu": tiles_of(w_gu), "wdn": tiles_of(a["w_down"]),
    }
    aw = a["a_w_in_2"][0]
    per = []
    for hp in range(HP):
        c = np.arange(hp * P, hp * P + P)
        at = [(3 * g + i) * D for g in range(3) for i in range(2)] + [(3 * g + 2) * D for g in range(3)] + [9 * D]
        per += [c + b for b in at]
    arrays["wa"] = tiles_of(aw[:, np.concatenate(per)])
    arrays["wao"] = tiles_of(a["a_w_out_2"][0])
    arrays["pleg"] = tiles_of(a["ple_w_gate_2"])
    arrays["plep"] = tiles_of(a["ple_w_proj_2"])
    bw = a["b_w_in_2"][0]
    kc = np.arange(D, D + 64)
    arrays["wbk"] = tiles_of(bw[:, np.concatenate([kc, kc, kc + 64, kc + 64, np.arange(D + P, D + 2 * P)])])
    zc = D + 2 * P
    arrays["wbqz"] = tiles_of(bw[:, np.concatenate([np.concatenate([np.arange(h * P, h * P + P), np.arange(zc + h * P, zc + h * P + P)]) for h in range(HP)])])
    arrays["wbo"] = tiles_of(a["b_w_out_2"][0])
    arrays["p"] = np.stack([feats(a["p_2"][i, 0]) for i in range(DEPTH)])
    inv = (1.0 / (10000.0 ** (np.arange(0, ADIM, 2, dtype=f) / f(ADIM)))).astype(f)
    ang = np.arange(SEQ, dtype=f)[:, None] * inv[None, :]
    cos, sin = np.cos(ang).astype(f).T, np.sin(ang).astype(f).T
    rope = np.stack([np.tile(cos, (4, 1)), np.concatenate([-sin, sin, -sin, sin])], axis=1)
    am = np.full((P, 4, 768), NEG, f)
    for r in range(4):
        dist = (4 * ts[:, None] + r) - np.arange(SEQ)[None, :]
        am[:, r, 0:SEQ][(dist >= 0) & (dist <= P)] = 0
        back = ts[:, None] - ts[None, :]
        am[:, r, SEQ:SEQ + P][back >= 0] = 0
        am[:, r, SEQ + P:768][(back >= 0) & (back % 4 == 0)] = 0
    bm = np.full((P, 896), NEG, f)
    bm[:, 0:P][ts[:, None] >= ts[None, :]] = 0
    for b in range(3):
        dist = ts[:, None] + P - np.arange(2 * P)[None, :]
        bm[:, P + 2 * P * b:P + 2 * P * (b + 1)][(dist >= 0) & (dist <= P - 1)] = 0
    lnp = np.stack([columns_of(a["ln_g_2"]), columns_of(a["ln_b_2"])], axis=2).reshape(P, -1)
    sink = np.broadcast_to(a["b_sinks_2"][0][None], (P, AH))
    arrays["b2"] = np.concatenate([am.reshape(P, -1), rope.reshape(P, -1), lnp, sink], axis=1)
    arrays["bmask"] = bm
    nc = _bacc.Bacc("TRN2", target_bir_lowering=False, num_devices=1)
    names = ["xT", "cT", "cb", "pc", "fin", "srow", "consts", "sguw", "wg", "wmod", "win", "wout", "wgu", "wdn",
             "b2", "bmask", "p", "wa", "wao", "pleg", "plep", "wbk", "wbqz", "wbo"]
    arrays = {n: np.ascontiguousarray(arrays[n]) for n in names}
    args = [nc.dram_tensor("in_" + n, arrays[n].shape, mybir.dt.from_np(arrays[n].dtype), kind="ExternalInput").ap() for n in names]
    out = nc.dram_tensor("out_0_dram", (P, KT, SEQ), FP32, kind="ExternalOutput").ap()
    build_program(nc, *args, out)
    r = _run(nc, [{"in_" + n: arrays[n] for n in names}], core_ids=[0])
    got = np.asarray(r.results[0]["out_0_dram"])
    return np.ascontiguousarray(got.transpose(2, 1, 0).reshape(1, SEQ, D))
```

```python
import numpy as np
import concourse.bass as bass
from concourse import mybir
from contextlib import ExitStack

FP32 = mybir.dt.float32
FP32R = mybir.dt.float32r
ALU = mybir.AluOpType
ACT = mybir.ActivationFunctionType

P = 128
D = 1024
KT = D // P
SEQ, CTX = 512, 256
T = SEQ + CTX
NJ, NX = T // P, SEQ // P
DEPTH = 2
HEADS, HD = 4, 128
FFN = 2816
FT = FFN // P
PARTS = ((0, 8), (8, 8), (16, 6))
GRID = 64
CONV_K = 31
EPS, LN_EPS = 1e-6, 1e-5
K_SCALE = HD ** -0.5
ALPHA = float((2 * DEPTH) ** 0.25)
AH, ADIM = 16, 64
A_SCALE = ADIM ** -0.5
NEG = -1e30
GELU_C, GELU_A = 0.7978845608028654, 0.044715
RING = 4
MODS = 6 * KT
MOD_V = 28
MOD_P = 8

GA_T, U_T, SV_T, K_T, V_T, Q_T, O_T = 0, 4, 6, 8, 12, 16, 20
N_IN = 24
LAYER_TILES = N_IN + KT + 2 * FT + len(PARTS) * KT
HP = AH // 2
A_TILES = 10
N_A = DEPTH * LAYER_TILES
N_AOUT = N_A + A_TILES * HP
N_PLE = (N_AOUT + KT, N_AOUT + KT + 2 * KT + 3 + 2 * HP + KT)
N_B = N_PLE[0] + 2 * KT
N_BQZ = N_B + 3
N_BOUT = N_BQZ + 2 * HP
N_ALL = N_PLE[1] + 2 * KT


def part_start(l, p):
    return l * LAYER_TILES + N_IN + KT + sum(2 * PARTS[q][1] + KT for q in range(p))


def staged(n):
    if n < N_A:
        return not U_T + 2 <= n % LAYER_TILES < N_IN
    if n < N_AOUT:
        return (n - N_A) % A_TILES == 9
    if n < N_B:
        return True
    if n < N_BQZ:
        return False
    if n < N_BOUT:
        return (n - N_BQZ) % 2 == 1
    return True


USED = [0]
for _n in range(N_ALL):
    USED.append(USED[-1] + staged(_n))


def used(n):
    return USED[max(n + 1, 0)]


PC = {}
NPC = 0
for _name, _w in (("norm1", 8), ("norm2", 8), ("b_in", 24), ("mg", 4), ("cw", 2 * CONV_K), ("cb", 2),
                  ("cg", 2), ("clb", 2), ("b_mod", 48)):
    PC[_name] = NPC
    NPC += _w
SROW_B = 512
SROW_G = SROW_B + 2 * P
N_SROW = SROW_G + 16
N_CONST = 5 * P + 2


def mlstm_steps(l):
    order = ([4, 5, 0, 1, 2, 3], [5, 4, 3, 2, 1, 0])
    return [(d, order[d][i], i == 0, l == 0 or order[d][i] < NX) for i in range(NJ) for d in range(2)] if l < DEPTH else []


def outputs_before(l, t):
    return sum(s[3] for m in range(l) for s in mlstm_steps(m)) + sum(s[3] for s in mlstm_steps(l)[:t])


def outputs_of_slot(l, t):
    return outputs_before(l, max(t - 1, 0))


def weighted_before(l, t):
    return (sum(s[3] and not s[2] for m in range(l) for s in mlstm_steps(m))
            + sum(s[3] and not s[2] for s in mlstm_steps(l)[:t]))


def width(l, t=None):
    return T if l == 0 or (t is not None and K_T <= t < Q_T) else SEQ


def ranges(w):
    return [(0, SEQ), (SEQ, T)] if w == T else [(0, SEQ)]


def build_program(nc, xT, cT, cb_d, pc_d, fin_d, srow_d, consts_d, sguw_d, wg_d, wmod_d, win_d, wout_d, wgu_d, wdn_d,
                  b2_d, bmask_d, p_d, wa_d, wao_d, pleg_d, plep_d, wbk_d, wbqz_d, wbo_d, out_d):
    cursor = [nc.sbuf_base + (-nc.sbuf_base) % 64]
    addr_of = {}

    def place(name, shape, dt=FP32, addr=None):
        size = 4
        for s in shape[1:]:
            size *= s
        if addr is None:
            addr = cursor[0]
            cursor[0] += size + (-size) % 32
        assert addr + size <= nc.sbuf_usable_end, (name, addr + size, nc.sbuf_usable_end)
        addr_of[name] = addr
        return nc.alloc_sbuf_tensor_at(name, shape, dt, offset=addr)

    stack = ExitStack()
    with stack:
        def sem(name):
            return stack.enter_context(nc.semaphore(name))

        raw = [place(f"raw{i}", [P, KT * P]) for i in range(RING)]
        w_hi = [place(f"w_hi{i}", [P, KT, P], FP32R) for i in range(2)]
        w_lo = [place(f"w_lo{i}", [P, KT, P], FP32R) for i in range(2)]
        Z = place("Z", [P, 4, T])
        TH = place("TH", [P, N_SROW])
        ident = place("ident", [P, P])
        ones = place("ones", [P, P])
        word = place("word", [P, 8])
        eps_c = place("eps_c", [P, 2])
        X = place("X", [P, KT, T])
        XH = place("XH", [P, KT, T], FP32R)
        XL = place("XL", [P, KT, T], FP32R)
        tri = place("tri", [P, 2, P])
        mskd = place("mskd", [P, 2, P])
        dsel = place("dsel", [8, 2])
        pc = place("pc", [P, DEPTH, NPC])
        fin_g = place("fin_g", [P, KT])
        bcol = place("bcol", [P, N_IN])
        mods = [place(f"mod{l}", [P, MODS, 2]) for l in range(DEPTH)]
        macc = place("macc", [P, 4, 2])
        nsc = place("nsc", [P, 2, KT, 2])
        cact = place("cact", [P, KT, 2])
        cth = place("cth", [P, KT, 2])
        sgw = place("sgw", [P, 4, P])
        wg = place("wg", [P, KT, 16])
        wgh = place("wgh", [P, KT, 16], FP32R)
        wgl = place("wgl", [P, KT, 16], FP32R)
        gt = place("gt", [P, NJ, 2, 2, HEADS])
        lf = place("lf", [P, 3, NJ, 8])
        gcol = place("gcol", [P, NJ, 8])
        btm = place("btm", [P, NJ, 8])
        bst = place("bst", [P, NJ, 6])
        bmv = place("bmv", [P, NJ, 2])
        mprev = place("mprev", [8, 2, NJ])
        work = cursor[0]
        kfm = place("kfm", [P, HEADS, T])
        qfm = place("qfm", [P, HEADS, T])
        tho = place("tho", [P, HEADS, T])
        ktm = place("ktm", [P, NJ, HEADS, P])
        vtm = place("vtm", [P, NJ, HEADS, P])
        YC = place("YC", [P, 2, T])
        AC = place("AC", [P, 2, T])
        Ug = place("Ug", [P, 2, T])
        srow = place("srow", [P, N_SROW], addr=addr_of["TH"])
        SVT = place("SVT", [P, NJ, 256], addr=addr_of["tho"])
        GT = place("GT", [P, HEADS, T], addr=addr_of["qfm"])
        cb = place("cb", [P, 2, D], addr=addr_of["vtm"])
        cprod = place("cprod", [P, D], addr=addr_of["vtm"] + 8 * D)
        modv = [place(f"modv{i}", [P, D], addr=(work + (MOD_P + i) * 4 * D if i < 4 else addr_of["vtm"] + (4 * i - 4) * D))
                for i in range(8)]
        cbt = place("cbt", [P, 2, D], addr=addr_of["vtm"] + 20 * D)
        modp = [place(f"modp{i}", [P, KT, P], addr=work + i * 4 * D) for i in range(MOD_P)]
        MT = place("MT", [P, T], addr=work)
        SQ = [[place(f"SQ{q}{i}", [P, T], addr=(addr_of["Z"], addr_of["vtm"])[q] + i * T * 4) for i in range(2)] for q in range(2)]
        SS = [place(f"SS{q}", [P, T], addr=(addr_of["Z"] + 2 * T * 4, addr_of["vtm"] + 2 * T * 4)[q]) for q in range(2)]
        MU = place("MU", [P, T], addr=addr_of["Z"] + 2 * T * 4)
        ri, rf, rb, rm = (place(f"row{i}", [8, T], addr=addr_of["XH"] + i * T * 4) for i in range(4))
        rhl = [[place(f"rhl{i}{j}", [8, T], FP32R, addr=addr_of["XH"] + (4 + 2 * i + j) * T * 4) for j in range(2)]
               for i in range(3)]
        r2 = place("row4", [8, T], addr=addr_of["XH"] + 10 * T * 4)
        selh = place("selh", [8, 8, P], FP32R, addr=addr_of["row4"])
        H = place("H", [P, HEADS, T], addr=addr_of["XL"] + 4 * T * 4)
        Ee, Pp, Qw, WIs, EMs, Ks = ([place(f"mw{i}{e}", [P, HEADS, P], addr=addr_of[("Z", "raw0")[e]] + i * 2048) for e in range(2)]
                                    for i in range(6))
        ST = [place(f"ST{d}", [P, HEADS, 2, P], addr=addr_of[("YC", "row0")[d]]) for d in range(2)]
        W1 = place("W1", [P, HEADS, P], addr=addr_of["YC"] + 4096)
        AD = place("AD", [P, HEADS, P], addr=addr_of["TH"])
        HN = place("HN", [P, HEADS, P], addr=addr_of["row2"])
        grow = place("grow", [16, T], addr=addr_of["Z"] + 3 * T * 4)
        RH = place("RH", [P, HEADS, T], addr=addr_of["ktm"])
        HH = place("HH", [P, 8, T], FP32R, addr=work)
        HL = place("HL", [P, 8, T], FP32R, addr=work + 8 * T * 4)
        PS = stack.enter_context(nc.psum_tensor("PS", [P, 8, 512], FP32))

        def banks(a, b):
            return PS[:, a:b, :].rearrange("p a b -> p (a b)")

        def acc(n):
            return banks(2 * (n % 2), 2 * (n % 2) + 2)

        s_const = sem("constants_loaded")
        s_x = sem("x_loaded")
        s_par = sem("layer_parameters_loaded")
        s_raw = [sem(f"raw_weights_loaded{i}") for i in range(RING)]
        s_hi = sem("weights_upper_made")
        s_split = sem("weights_split")
        s_tile = sem("gemm_tile_done")
        s_evac = sem("gemm_tile_evacuated")
        s_used = sem("staged_tile_used")
        s_modw = [sem(f"mod_weights_loaded{i}") for i in range(MOD_P)]
        s_mvw = [sem(f"mod_weights_loaded_for_dve{i}") for i in range(8)]
        s_mvd = sem("mod_tile_summed")
        s_cb = sem("c_spread")
        s_cbt = sem("c_spread_tanh_made")
        s_cba = sem("c_spread_activated")
        s_modd = sem("mod_chunk_done")
        s_mod = sem("modulation_ready")
        s_cact = sem("c_activated")
        s_cth = sem("c_tanh_made")
        s_one = sem("on_chip_constants_made")
        s_sq = sem("squares_made")
        s_acc = sem("squares_accumulated")
        s_squ = sem("squares_summed")
        s_lsq = sem("ln_squares_summed")
        s_rstd = sem("rstd_made")
        s_xn = sem("normed_made")
        s_xh = sem("operand_upper_made")
        s_xl = sem("operand_split")
        s_dch = sem("dve_chain")
        s_ach = sem("act_chain")
        s_gin = sem("gelu_argument_made")
        s_gth = sem("gelu_tanh_made")
        s_gel = sem("gelu_made")
        s_tr = sem("transposed")
        s_tre = sem("transposed_evacuated")
        s_svv = sem("sgu_variance_made")
        s_svr = sem("sgu_rstd_made")
        s_svt = sem("sgu_v_normed")
        s_mix = sem("sgu_mixed")
        s_mixu = sem("sgu_mixed_used")
        s_wgh = sem("gate_weights_upper_made")
        s_wgl = sem("gate_weights_split")
        s_gate = sem("gates_done")
        s_grow = sem("gate_rows_done")
        s_growe = sem("gate_rows_evacuated")
        s_gtm = sem("gates_made")
        s_lfa = sem("log_forget_softplus_made")
        s_lf = sem("log_forget_made")
        s_bt = sem("forget_sums_done")
        s_btm = sem("forget_sums_evacuated")
        s_rows = sem("rows_done")
        s_row = sem("rows_made")
        s_rowh = sem("rows_upper_made")
        s_rowl = sem("rows_split")
        s_nm = sem("neg_max_spread")
        s_wi = sem("inter_weights_spread")
        s_wie = sem("inter_weights_made")
        s_w1 = sem("log_weights_made")
        s_e = sem("weights_made")
        s_s = sem("scores_done")
        s_p = sem("weighted_scores_made")
        s_qw = sem("weighted_q_made")
        s_ks = sem("weighted_k_made")
        s_nd = sem("num_den_done")
        s_nde = sem("num_den_evacuated")
        s_u = sem("state_update_done")
        s_st = sem("state_made")
        s_h = sem("h_made")
        s_hsq = sem("h_squares_made")
        s_hss = sem("h_squares_summed")
        s_hln = sem("h_sums_left_the_tiles_banks")
        s_hr = sem("h_rstd_made")
        s_tho = sem("output_gate_made")
        s_csum = sem("conv_sum_done")
        s_cmu = sem("conv_mean_made")
        s_cd = sem("conv_centred")
        s_csq = sem("conv_squares_made")
        s_cvar = sem("conv_var_done")
        s_crs = sem("conv_rstd_made")
        s_cl = sem("conv_normed")
        s_cta = sem("conv_tanh_made")
        s_yf = sem("mixer_output_made")
        s_yh = sem("mixer_output_upper_made")
        s_y = sem("mixer_output_split")
        s_hf = sem("hidden_made")
        s_hh = sem("hidden_upper_made")
        s_out = sem("output_stored")

        def split_weights(pool, s, dyn=0, k=KT):
            pool.wait_ge(s_raw[s % RING], 16 * (s // RING + 1) + 4 * dyn)
            if s >= 2:
                pool.wait_ge(s_tile, s - 1 + dyn)
            pool.tensor_tensor(word[:, 0:1], ones[:, 0:1], ones[:, 0:1], ALU.mult)
            src = raw[s % RING][:, 0:k * P].rearrange("p (k c) -> p k c", c=P)
            hi, lo = w_hi[s % 2][:, 0:k, :], w_lo[s % 2][:, 0:k, :]
            pool.tensor_scalar(hi, src, 1.0, 0.0, ALU.mult, ALU.add).then_inc(s_hi, 1)
            pool.wait_ge(s_hi, s + 1 + dyn)
            pool.tensor_tensor(lo, src, hi.bitcast(FP32), ALU.subtract).then_inc(s_split, 1)

        def gemm_step(pe, s, i, rh, rl, w, k):
            hi, lo = w_hi[s % 2][:, i, :], w_lo[s % 2][:, i, :]
            for a, b in ranges(w):
                pe.matmul(acc(s)[:, a:b], hi, rh[:, i, a:b], start=i == 0, stop=False)
                pe.matmul(acc(s)[:, a:b], hi, rl[:, i, a:b], start=False, stop=False)
            for a, b in ranges(w):
                last = pe.matmul(acc(s)[:, a:b], lo, rh[:, i, a:b], start=False, stop=i == k - 1)
            if i == k - 1:
                last.then_inc(s_tile, 1)

        def gemm_tile(pe, s, rh, rl, w, dyn=0, k=KT, ready=None):
            pe.wait_ge(s_split, s + 1 + dyn)
            if s >= 2:
                pe.wait_ge(s_evac, s - 1 + dyn)
            for i in range(k):
                if ready:
                    ready(i)
                gemm_step(pe, s, i, rh, rl, w, k)

        def first_tiles(pe, s, rh, rl, w, sem, done):
            pe.wait_ge(s_split, s + 2)
            if s >= 2:
                pe.wait_ge(s_evac, s)
            for i in range(KT):
                pe.wait_ge(sem, done + i + 1)
                for e in range(2):
                    gemm_step(pe, s + e, i, rh, rl, w, KT)


        b2_at = addr_of["tri"]
        cursor[0] = b2_at
        B2 = place("B2", [P, 4 * 768 + 2 * SEQ + 4 * KT + AH])
        amask = B2[:, 0:4 * 768].rearrange("p (r s) -> p r s", r=4)
        ropet = B2[:, 4 * 768:4 * 768 + 2 * SEQ].rearrange("p (a t) -> p a t", a=2)
        lnp = B2[:, 4 * 768 + 2 * SEQ:4 * 768 + 2 * SEQ + 4 * KT].rearrange("p (l a k) -> p l a k", l=DEPTH, a=2)
        sink = B2[:, 4 * 768 + 2 * SEQ + 4 * KT:]
        bmask = place("bmask", [P, 7 * P], addr=addr_of["B2"])
        KB = place("KB", [P, 2, SEQ], addr=addr_of["B2"] + 7 * P * 4)
        YH2 = place("YH2", [P, KT, SEQ], FP32R)
        YL2 = place("YL2", [P, KT, SEQ], FP32R)
        V0h, V0l = (place(f"V0{i}", [P, NX, P], FP32R) for i in range(2))
        VT = place("VT", [P, 2, NX, P])
        SM = [place(f"SM{i}", [P, 7 * P]) for i in range(2)]
        PO = place("PO", [P, 4, 2, P])
        PB = [place(f"PB{i}", [P, 7, P], addr=addr_of["PO"] + i * 7 * P * 4) for i in range(2)]
        cursor[0] = addr_of["PO"] + 14 * P * 4
        ZS = place("ZS", [P, SEQ])
        QS = place("QS", [P, 2, SEQ])
        P0l = place("P0l", [P, NX, P, 4], FP32R)
        PH = place("PH", [P, 2, SEQ], FP32R, addr=addr_of["QS"])
        PL = place("PL", [P, 2, SEQ], FP32R, addr=addr_of["QS"] + 2 * SEQ * 4)
        smax = place("smax", [P, 2, 4])
        ssum = place("ssum", [P, 2, 4])
        esink = place("esink", [P, 2, 4])
        X2 = place("X2", [P, KT, SEQ], addr=addr_of["XH"])
        XH2 = place("XH2", [P, KT, SEQ], FP32R, addr=addr_of["XH"] + KT * SEQ * 4)
        XL2 = place("XL2", [P, KT, SEQ], FP32R, addr=addr_of["XH"] + 2 * KT * SEQ * 4)
        QKh, QKl = (place(f"QK{i}", [P, 2, SEQ], FP32R, addr=addr_of["X"] + i * 2 * SEQ * 4) for i in range(2))
        QK = place("QK", [P, 4, SEQ], addr=addr_of["X"] + 4 * SEQ * 4)
        P0h = place("P0h", [P, NX, P, 4], FP32R, addr=addr_of["X"] + 8 * SEQ * 4)
        Praw = place("Praw", [P, 2, SEQ], addr=addr_of["X"])

        s_b2 = sem("second_block_constants_loaded")
        s_bm = sem("mixer_b_mask_loaded")
        s_swp = sem("rope_halves_swapped")
        s_rope = sem("rope_applied")
        s_sc = sem("attention_scores_done")
        s_sm = sem("attention_scores_masked")
        s_ex = sem("attention_exp_made")
        s_pn = sem("attention_probabilities_made")
        s_pt = sem("attention_probabilities_transposed")
        s_pth = sem("attention_probabilities_upper_made")
        s_ptl = sem("attention_probabilities_split")
        s_qkh = sem("q_k_upper_made")
        s_qkl = sem("q_k_split")
        s_vh = sem("v_upper_made")
        s_pv = sem("attention_values_done")
        s_ao = sem("attention_output_made")
        s_praw = sem("p_loaded")
        s_ph = sem("p_upper_made")
        s_pl = sem("p_split")
        s_lsum = sem("ln_sum_done")
        s_mu = sem("ln_mean_made")
        s_lnd = sem("ln_centred")
        s_lacc = sem("ln_sums_accumulated")
        s_xb = sem("ln_bias_added")

        def head_pairs(eng, mixer):
            last = 6 if mixer == "a" else 4
            with eng.Fori(0, last // 2) as i:
                for e in range(2):
                    yield e, 2 * i, 0, True
            for e in range(last, HP):
                yield e, 0, 1, e + 1 < HP

        def steps_of(mixer):
            return 2 * NX if mixer == "a" else 2

        def step0(mixer, hp):
            return 8 * hp if mixer == "a" else 8 * HP + 2 * hp

        def score_banks(st):
            return banks(4 + 2 * (st % 2), 6 + 2 * (st % 2))

        def score_block(mixer, st, b):
            if mixer == "a":
                return score_banks(st)[:, (0, SEQ, SEQ + P)[b]:(SEQ, SEQ + P, 768)[b]]
            return score_banks(st)[:, 2 * P * b:2 * P * (b + 1)]

        def transposed_parts(nb):
            return [(PS[:, 3, :], 0, NX), (PS[:, 1, 0:(nb - NX) * P], NX, nb)]

        def second_sp(sp, load, tile_of):
            with sp.Fori(0, HP // 2) as i:
                for t in range(2 * A_TILES):
                    load(N_A + t, tile_of(wa_d, 2 * A_TILES * i + t), 2 * A_TILES * i)

            def eight(s, w):
                with sp.Fori(0, 2) as i:
                    for u in range(4):
                        load(s + u, tile_of(w, 4 * i + u), 4 * i)

            def ple(l):
                sp.wait_ge(s_ao, 2 * HP * (l + 1))
                sp.dma_start(Praw[:], p_d[l]).then_inc(s_praw, 16)
                with sp.Fori(0, 4) as i:
                    for u in range(2):
                        load(N_PLE[l] + 2 * u, tile_of(pleg_d[l], 2 * i + u), 4 * i)
                        load(N_PLE[l] + 2 * u + 1, tile_of(plep_d[l], 2 * i + u), 4 * i, 2 * P)
            eight(N_AOUT, wao_d)
            ple(0)
            sp.wait_ge(s_sm, 8 * HP)
            sp.dma_start(bmask[:], bmask_d).then_inc(s_bm, 16)
            for t in range(3):
                load(N_B + t, wbk_d[t])
            for kv in range(2):
                with sp.Fori(0, HP // 4) as i:
                    for u in range(4):
                        load(N_BQZ + 8 * kv + u, tile_of(wbqz_d, 4 * i + 8 * kv + u), 4 * i)
            eight(N_BOUT, wbo_d)
            ple(1)
            sp.wait_ge(s_used, used(N_ALL - 1))
            sp.dma_start(out_d, X2[:]).then_inc(s_out, 16)
            sp.wait_ge(s_out, 16)

        def second_pool(pool):
            def eight(s):
                with pool.Fori(0, 2) as i:
                    for u in range(4):
                        split_weights(pool, s + u, 4 * i)

            def ple(l):
                with pool.Fori(0, 4) as i:
                    for u in range(2):
                        split_weights(pool, N_PLE[l] + 2 * u, 4 * i)
                        split_weights(pool, N_PLE[l] + 2 * u + 1, 4 * i, 2)
            with pool.Fori(0, HP // 2) as i:
                for t in range(2 * A_TILES):
                    split_weights(pool, N_A + t, 2 * A_TILES * i)
            eight(N_AOUT)
            ple(0)
            for t in range(3):
                split_weights(pool, N_B + t)
            for kv in range(2):
                with pool.Fori(0, HP // 4) as i:
                    for u in range(4):
                        split_weights(pool, N_BQZ + 8 * kv + u, 4 * i)
            eight(N_BOUT)
            ple(1)

        def second_pe(pe):
            def transpose_v(event, dyn, src, strided):
                pe.wait_ge(s_tre, event + dyn)
                for j in range(NX):
                    part = src[:, j:SEQ:4] if strided else src[:, j * P:(j + 1) * P]
                    last = pe.transpose(PS[:, 3, j * P:(j + 1) * P], part, ident[:])
                last.then_inc(s_tr, 1)

            def three(out, lh, ll, rh, rl, start=True, stop=True):
                pe.matmul(out, lh, rh, start=start, stop=False)
                pe.matmul(out, lh, rl, start=False, stop=False)
                return pe.matmul(out, ll, rh, start=False, stop=stop)

            def attention(mixer, e, dyn, kv, follows):
                n = steps_of(mixer)
                c0, cd = step0(mixer, e), n * dyn
                hp = e + (0 if mixer == "a" else HP)
                if mixer == "a":
                    pe.wait_ge(s_qkl, e + 1 + dyn)
                    pe.wait_ge(s_rope, 3 * e + 3 + 3 * dyn)
                else:
                    pe.wait_ge(s_rope, 3 * HP + 2 + e + dyn)

                def scores(st):
                    c = c0 + st
                    if c >= 2:
                        pe.wait_ge(s_sm, c - 1 + cd)
                    if mixer == "a":
                        h, r = slice(64 * (st // NX), 64 * (st // NX) + 64), st % NX
                        three(score_block(mixer, st, 0), QKh[h, 0, r:SEQ:4], QKl[h, 0, r:SEQ:4], QKh[h, 1, :], QKl[h, 1, :])
                        for g in (1, 2):
                            last = pe.matmul(score_block(mixer, st, g), QK[h, 2 * g - 2, r:SEQ:4], QK[h, 2 * g - 1, r:SEQ:4],
                                             start=True, stop=True)
                    else:
                        h = slice(64 * st, 64 * st + 64)
                        for b in range(NX):
                            last = pe.matmul(score_block(mixer, st, b)[:, 0 if b else P:2 * P], QK[h, 0, b * P:(b + 1) * P],
                                             KB[h, kv, max(b - 1, 0) * P:(b + 1) * P], start=True, stop=True)
                    last.then_inc(s_sc, 1)

                def transposes(st):
                    c = c0 + st
                    pe.wait_ge(s_pn, c + 1 + cd)
                    if c:
                        pe.wait_ge(s_ptl if mixer == "a" else s_pth, c + cd)
                    for dst, b0, b1 in transposed_parts(6 if mixer == "a" else 7):
                        for b in range(b0, b1):
                            last = pe.transpose(dst[:, (b - b0) * P:(b - b0 + 1) * P], SM[st % 2][:, b * P:(b + 1) * P], ident[:])
                    last.then_inc(s_pt, 1)

                def values(head):
                    pe.wait_ge(s_ptl if mixer == "a" else s_pth, c0 + (head + 1) * n // 2 + cd)
                    if mixer == "a":
                        pe.wait_ge(s_evac, N_A + A_TILES * (e + 1) + (2 * head + 2 if follows else 0) + A_TILES * dyn)
                    else:
                        pe.wait_ge(s_evac, N_BQZ + 2 * (e + 1) + (1 if follows else 0) + 2 * dyn)
                    if head:
                        pe.wait_ge(s_ao, 2 * hp + 1 + 2 * dyn)
                    else:
                        pe.wait_ge(s_tre, 20 + (3 * (e + 1) + 3 * dyn if mixer == "a" else 3 * HP + 1))
                    h = slice(64 * head, 64 * head + 64)
                    if mixer == "a":
                        for b in range(NX):
                            if b == NX - 1:
                                for r in range(4):
                                    for g in (0, 1):
                                        pe.matmul(PS[h, 2, r:SEQ:4], VT[:, g, r, h], PO[:, r, g, :], start=False, stop=False)
                            last = three(PS[:, 2, :], V0h[:, b, :], V0l[:, b, :], P0h[:, b].rearrange("p i r -> p (i r)"),
                                         P0l[:, b].rearrange("p i r -> p (i r)"), b == 0, b == NX - 1)
                    else:
                        for b in range(NX):
                            blocks = [(2 * b - 1, b - 1), (2 * b, b)] if b else [(0, 0)]
                            for m, (src, blk) in enumerate(blocks):
                                last = pe.matmul(PS[h, 2, b * P:(b + 1) * P], VT[:, 0, blk, 64 * kv:64 * kv + 64], PB[head][:, src, :],
                                                 start=m == 0, stop=m == len(blocks) - 1)
                    last.then_inc(s_pv, 1)
                scores(0)
                scores(1)
                for st in range(n):
                    transposes(st)
                    if st + 2 < n:
                        scores(st + 2)
                    if follows and mixer == "b":
                        if st == 0:
                            pe.wait_ge(s_y, 3 * KT + e + dyn)
                        gemm_tile(pe, N_BQZ + 2 * (e + 1) + st, XH2, XL2, SEQ, 2 * dyn)
                    if follows and mixer == "a" and st % 2 == 0:
                        if st == 2:
                            pe.wait_ge(s_y, 2 * KT + e + dyn)
                        if st == 6:
                            pe.wait_ge(s_ao, 2 * hp + 1 + 2 * dyn)
                        gemm_tile(pe, N_A + A_TILES * (e + 1) + st // 2, XH2, XL2, SEQ, A_TILES * dyn)
                    if (st + 1) % (n // 2) == 0:
                        values(st // (n // 2))

            def eight(s):
                with pe.Fori(0, 2) as i:
                    for u in range(4):
                        gemm_tile(pe, s + u, YH2, YL2, SEQ, 4 * i)

            def layer_norm(l):
                pe.wait_ge(s_lacc, (KT + 1) * (l + 1))
                pe.matmul(PS[:, 6, :], ones[:], TH[:, 0:SEQ], start=True, stop=True).then_inc(s_lsum, 1)
                for k in range(KT):
                    pe.wait_ge(s_sq, KT * (5 + l) + k + 1)
                    pe.matmul(PS[:, 6, :], ones[:], Z[:, k % 4, 0:SEQ], start=k == 0, stop=k == KT - 1).then_inc(s_lsq, 1)

            def ple(l):
                def operand_ready(k):
                    pe.wait_ge(s_xl, KT * (5 + 2 * l) + k + 1)
                with pe.Fori(0, 4) as i:
                    for u in range(2):
                        gemm_tile(pe, N_PLE[l] + 2 * u, XH2, XL2, SEQ, 4 * i, ready=operand_ready if u == 0 else None)
                        pe.wait_ge(s_pl, l + 1)
                        gemm_tile(pe, N_PLE[l] + 2 * u + 1, PH, PL, SEQ, 4 * i, 2)

            first_tiles(pe, N_A, XH2, XL2, SEQ, s_xl, KT * 4)
            for t in range(2, 4):
                gemm_tile(pe, N_A + t, XH2, XL2, SEQ)
            for e, dyn, _, follows in head_pairs(pe, "a"):
                n = N_A + A_TILES * e
                for t in range(4, A_TILES):
                    if t == 5:
                        pe.wait_ge(s_y, 2 * KT + e + dyn)
                    gemm_tile(pe, n + t, XH2, XL2, SEQ, A_TILES * dyn)
                    if t >= 7:
                        g = t - 7
                        pe.wait_ge(s_evac, n + t + A_TILES * dyn)
                        transpose_v(20 + 3 * e + g, 3 * dyn, Z[:, (n + t - 1) % 4, 0:SEQ], g > 0)
                attention("a", e, dyn, None, follows)
            pe.wait_ge(s_y, KT * 3)
            eight(N_AOUT)
            layer_norm(0)
            ple(0)
            first_tiles(pe, N_B, XH2, XL2, SEQ, s_xl, KT * 6)
            gemm_tile(pe, N_B + 2, XH2, XL2, SEQ)
            pe.wait_ge(s_evac, N_B + 3)
            transpose_v(20 + 3 * HP, 0, Z[:, (N_B + 2) % 4, 0:SEQ], False)
            for t in range(2):
                gemm_tile(pe, N_BQZ + t, XH2, XL2, SEQ)
            for e, dyn, kv, follows in head_pairs(pe, "b"):
                attention("b", e, dyn, kv, follows)
            pe.wait_ge(s_y, KT * 4)
            eight(N_BOUT)
            layer_norm(1)
            ple(1)

        def second_act(act, link, rstd, evacuate):
            def swap(k, src, wait_tile, dyn, ropes=None):
                act.wait_ge(s_evac, wait_tile + dyn)
                if ropes is not None:
                    act.wait_ge(s_rope, ropes)
                for q in range(4):
                    act.dma_start(QS[32 * (q ^ 1):32 * (q ^ 1) + 32, 0:k], src[32 * q:32 * q + 32]).then_inc(s_swp, 16)

            def upper(dst, src, ropes):
                act.wait_ge(s_rope, ropes)
                act.activation(dst, src, ACT.Copy).then_inc(s_qkh, 1)

            def z_tile(n, dyn, per):
                act.wait_ge(s_tile, n + 1 + dyn)
                act.wait_ge(s_used, used(n - 1) + per)
                act.activation(Z[:, n % 4, 0:SEQ], acc(n)[:, 0:SEQ], ACT.Identity)
                act.activation(TH[:, 0:SEQ], acc(n)[:, 0:SEQ], ACT.Tanh, scale=0.5).then_inc(s_evac, 1)

            def a_tile(e, dyn, t):
                n = N_A + A_TILES * e
                act.wait_ge(s_tile, n + t + 1 + A_TILES * dyn)
                if t == 0:
                    act.wait_ge(s_tre, 20 + 3 * e + 3 * dyn)
                if t == 3:
                    act.wait_ge(s_used, used(n - 1) + dyn)
                if t == 4:
                    act.wait_ge(s_qkl, e + 1 + dyn)
                if t in (6, 8):
                    act.wait_ge(s_rope, 3 * e + t // 2 - 1 + 3 * dyn)
                act.activation(Z[:, (n + t) % 4, 0:SEQ], acc(n + t)[:, 0:SEQ], ACT.Identity).then_inc(s_evac, 1)

            def a_swap(e, dyn, g):
                n = N_A + A_TILES * e + 2 * g
                swap(2, Z[:, n % 4:n % 4 + 2, 0:SEQ], n + 2, A_TILES * dyn, 3 * e + g + 3 * dyn if 3 * e + g else None)

            def a_upper(e, dyn):
                slot = (N_A + A_TILES * e) % 4
                upper(QKh[:], Z[:, slot:slot + 2, 0:SEQ], 3 * e + 1 + 3 * dyn)

            def b_tile(e, dyn, t):
                n = N_BQZ + 2 * e
                if t:
                    z_tile(n + 1, 2 * dyn, dyn)
                else:
                    act.wait_ge(s_tile, n + 1 + 2 * dyn)
                    act.activation(Z[:, n % 4, 0:SEQ], acc(n)[:, 0:SEQ], ACT.Identity).then_inc(s_evac, 1)
                    swap(1, Z[:, n % 4:n % 4 + 1, 0:SEQ], n + 1, 2 * dyn, 3 * HP + 1 + e + dyn)

            def attention(mixer, e, dyn, follows):
                n = steps_of(mixer)
                c0, cd = step0(mixer, e), n * dyn

                hp = e + HP * (mixer == "b")

                def exps(st):
                    c = c0 + st
                    act.wait_ge(s_sm, c + 1 + cd)
                    m = smax[:, st % 2]
                    if mixer == "a":
                        s = SM[st % 2][:, 0:768]
                        act.activation(s, s, ACT.Exp, bias=m[:, 1:2], accum_out=ssum[:, st % 2, 0:1]).then_inc(s_ex, 1)
                    else:
                        for b in range(NX):
                            s = SM[st % 2][:, max(2 * b - 1, 0) * P:(2 * b + 1) * P]
                            act.activation(s, s, ACT.Exp, bias=m[:, b:b + 1], accum_out=ssum[:, st % 2, b:b + 1])
                        head = sink[:, bass.ds(2 * e + st + 2 * dyn, 1)]
                        act.activation(esink[:, st % 2], m, ACT.Exp, bias=head).then_inc(s_ex, 1)

                def probabilities_upper(st):
                    c = c0 + st
                    act.wait_ge(s_pt, c + 1 + cd)
                    if mixer == "a":
                        if st == NX:
                            act.wait_ge(s_pv, 2 * hp + 1 + 2 * dyn)
                        act.activation(P0h[:, :, :, st % NX], PS[:, 3, :].rearrange("p (b i) -> p b i", b=NX), ACT.Copy)
                        dst = PO[:, st % NX].rearrange("p g t -> p (g t)")
                        last = act.activation(dst, PS[:, 1, 0:2 * P], ACT.Copy)
                    else:
                        for src, b0, b1 in transposed_parts(7):
                            last = act.activation(PB[st][:, b0:b1, :].rearrange("p b t -> p (b t)"), src, ACT.Copy)
                    last.then_inc(s_pth, 1)
                exps(0)
                exps(1)
                for st in range(n):
                    probabilities_upper(st)
                    if st + 2 < n:
                        exps(st + 2)
                    if follows and mixer == "b":
                        b_tile(e + 1, dyn, st)
                    if follows and mixer == "a":
                        if st % 2 == 0:
                            a_tile(e + 1, dyn, st // 2)
                        if st == 2:
                            a_swap(e + 1, dyn, 0)
                        if st == n - 1:
                            a_upper(e + 1, dyn)
                            a_swap(e + 1, dyn, 1)
                act.wait_ge(s_ao, 2 * hp + 2 + 2 * dyn)
                act.activation(YH2[:, bass.ds(e + dyn, 1), :].rearrange("p a t -> p (a t)"), ZS[:], ACT.Copy).then_inc(s_yh, 1)

            def plain(n, dyn):
                act.wait_ge(s_tile, n + 1 + dyn)
                act.wait_ge(s_used, used(n - 4) + dyn)
                act.activation(Z[:, n % 4, 0:SEQ], acc(n)[:, 0:SEQ], ACT.Identity).then_inc(s_evac, 1)

            def eight(s):
                act.wait_ge(s_used, used(s - 1))
                with act.Fori(0, 2) as i:
                    for u in range(4):
                        plain(s + u, 4 * i)

            def split_x(q, counted):
                for k in range(KT):
                    act.wait_ge(*counted(k))
                    act.activation(XH2[:, k], X2[:, k], ACT.Copy).then_inc(s_xh, 1)
                act.wait_ge(s_xl, KT * (q + 1))

            def layer_norm(l):
                act.wait_ge(s_praw, 16 * (l + 1))
                act.activation(PH[:], Praw[:], ACT.Copy).then_inc(s_ph, 1)
                act.wait_ge(s_lsum, l + 1)
                act.activation(TH[:, 0:SEQ], PS[:, 6, :], ACT.Copy, scale=1.0 / D).then_inc(s_mu, 1)
                for k in range(KT):
                    act.wait_ge(s_lnd, KT * l + k + 1)
                    if k >= 4:
                        act.wait_ge(s_lsq, KT * l + k - 3)
                    act.activation(Z[:, k % 4, 0:SEQ], X2[:, k], ACT.Square).then_inc(s_sq, 1)
                act.wait_ge(s_lsq, KT * (l + 1))
                rstd(TH[:, 0:SEQ], PS[:, 6, :], 1.0 / D, 1).then_inc(s_rstd, 1)

                def biased(k):
                    act.wait_ge(s_xl, KT * (5 + 2 * l) + k + 1)
                    act.activation(X2[:, k], X2[:, k], ACT.Identity, bias=lnp[:, l, 1, k:k + 1]).then_inc(s_xb, 1)
                for k in range(KT):
                    act.wait_ge(s_xn, KT * (5 + l) + k + 1)
                    act.activation(XH2[:, k], X2[:, k], ACT.Identity, bias=lnp[:, l, 1, k:k + 1]).then_inc(s_xh, 1)
                    if k:
                        biased(k - 1)
                biased(KT - 1)

            def ple(l):
                with act.Fori(0, 4) as i:
                    for u in range(2):
                        n = N_PLE[l] + 2 * u
                        act.wait_ge(s_tile, n + 1 + 4 * i)
                        act.wait_ge(s_used, used(n - 3) + 4 * i)
                        act.activation(Z[:, n % 4, 0:SEQ], acc(n)[:, 0:SEQ], ACT.Tanh, scale=0.5).then_inc(s_evac, 1)
                        act.wait_ge(s_tile, n + 2 + 4 * i)
                        act.activation(Z[:, (n + 1) % 4, 0:SEQ], acc(n + 1)[:, 0:SEQ], ACT.Identity).then_inc(s_evac, 1)

            act.wait_ge(s_squ, 5)
            rstd(TH[:, 0:SEQ], PS[:, 6, :], 1.0 / D).then_inc(s_rstd, 1)
            split_x(4, lambda k: (s_xn, KT * 4 + k + 1))
            act.dma_start(B2[:], b2_d).then_inc(s_b2, 16)
            for t in range(4):
                a_tile(0, 0, t)
                if t == 1:
                    a_swap(0, 0, 0)
            a_upper(0, 0)
            a_swap(0, 0, 1)
            for e, dyn, _, follows in head_pairs(act, "a"):
                n = N_A + A_TILES * e
                for t in range(4, 9):
                    a_tile(e, dyn, t)
                    if t == 5:
                        a_swap(e, dyn, 2)
                    if t == 7:
                        act.wait_ge(s_tr, 20 + 3 * e + 1 + 3 * dyn)
                        act.activation(V0h[:].rearrange("p j d -> p (j d)"), PS[:, 3, :], ACT.Copy).then_inc(s_vh, 1)
                z_tile(n + 9, A_TILES * dyn, dyn)
                attention("a", e, dyn, follows)
            eight(N_AOUT)
            layer_norm(0)
            ple(0)
            act.wait_ge(s_tile, N_B)
            split_x(6, lambda k: (s_used, used(N_PLE[0] + 2 * k + 1)))
            act.wait_ge(s_bm, 16)
            for t in range(3):
                act.wait_ge(s_tile, N_B + t + 1)
                act.activation(Z[:, (N_B + t) % 4, 0:SEQ], acc(N_B + t)[:, 0:SEQ], ACT.Identity).then_inc(s_evac, 1)
                if t == 1:
                    swap(2, Z[:, N_B % 4:N_B % 4 + 2, 0:SEQ], N_B + 2, 0)
            act.wait_ge(s_tre, 20 + 3 * HP + 1)
            for t in range(2):
                b_tile(0, 0, t)
            for e, dyn, _, follows in head_pairs(act, "b"):
                attention("b", e, dyn, follows)
            eight(N_BOUT)
            layer_norm(1)
            ple(1)

        def second_dve(dve, link, linked_loop):
            def lower(q, k):
                dve.wait_ge(s_xh, KT * q + k + 1)
                dve.tensor_tensor(XL2[:, k], X2[:, k], XH2[:, k].bitcast(FP32), ALU.subtract).then_inc(s_xl, 1)

            def rope(x, k, link_in, swaps, out):
                dve.wait_ge(s_swp, swaps)
                xs = QS[:, 0:k]
                cos, sin = (ropet[:, i:i + 1].to_broadcast([P, k, SEQ]) for i in range(2))
                dve.tensor_tensor(x, x, cos, ALU.mult)
                link_in(dve.tensor_tensor(xs, xs, sin, ALU.mult))
                dve.tensor_tensor(out, x, xs, ALU.add).then_inc(s_rope, 1)

            def a_rope(e, dyn, g, link_in):
                slot = (N_A + A_TILES * e + 2 * g) % 4
                x = Z[:, slot:slot + 2, 0:SEQ]
                rope(x, 2, link_in, 64 * (3 * e + g + 1) + 192 * dyn, QK[:, 2 * g - 2:2 * g] if g else x)

            def b_rope(e, dyn, link_in):
                slot = (N_BQZ + 2 * e) % 4
                rope(Z[:, slot:slot + 1, 0:SEQ], 1, link_in, 64 * (3 * HP + 1 + e + 1) + 64 * dyn, QK[:, 0:1])

            def a_lower(e, dyn):
                slot = (N_A + A_TILES * e) % 4
                dve.wait_ge(s_qkh, e + 1 + dyn)
                dve.tensor_tensor(QKl[:], Z[:, slot:slot + 2, 0:SEQ], QKh[:].bitcast(FP32), ALU.subtract).then_inc(s_qkl, 1)

            def attention(mixer, e, dyn, link_in, follows):
                n = steps_of(mixer)
                c0, cd = step0(mixer, e), n * dyn

                def mask(st):
                    c = c0 + st
                    dve.wait_ge(s_sc, c + 1 + cd)
                    if c >= 2:
                        dve.wait_ge(s_pt, c - 1 + cd)
                    dve.tensor_tensor(word[:, 1:2], ones[:, 0:1], ones[:, 0:1], ALU.mult)
                    m = smax[:, st % 2]
                    if mixer == "a":
                        link_in(dve.tensor_tensor_reduce(out=SM[st % 2][:, 0:768], in0=score_banks(st)[:, 0:768], in1=amask[:, st % NX, :],
                                                         scale=A_SCALE, scalar=NEG, op0=ALU.add, op1=ALU.max, accum_out=m[:, 0:1]))
                        dve.tensor_scalar(m[:, 1:2], m[:, 0:1], -1.0, 0.0, ALU.mult, ALU.add).then_inc(s_sm, 1)
                    else:
                        for b in range(NX):
                            a, z = max(2 * b - 1, 0) * P, (2 * b + 1) * P
                            last = dve.tensor_tensor_reduce(out=SM[st % 2][:, a:z], in0=score_block(mixer, st, b)[:, 0 if b else P:2 * P], in1=bmask[:, a:z],
                                                            scale=A_SCALE, scalar=NEG, op0=ALU.add, op1=ALU.max, accum_out=m[:, b:b + 1])
                        link_in(last)
                        head = sink[:, bass.ds(2 * e + st + 2 * dyn, 1)]
                        dve.tensor_scalar(m, m, head, -1.0, ALU.max, ALU.mult).then_inc(s_sm, 1)

                def normalise(st):
                    c = c0 + st
                    dve.wait_ge(s_ex, c + 1 + cd)
                    s = ssum[:, st % 2]
                    if mixer == "a":
                        link_in(dve.reciprocal(s[:, 1:2], s[:, 0:1]))
                        dve.tensor_scalar(SM[st % 2][:, 0:768], SM[st % 2][:, 0:768], s[:, 1:2], None, ALU.mult).then_inc(s_pn, 1)
                    else:
                        link_in(dve.tensor_tensor(s, s, esink[:, st % 2], ALU.add))
                        link_in(dve.reciprocal(s, s))
                        for b in range(NX):
                            a, z = max(2 * b - 1, 0) * P, (2 * b + 1) * P
                            last = dve.tensor_scalar(SM[st % 2][:, a:z], SM[st % 2][:, a:z], s[:, b:b + 1], None, ALU.mult)
                        last.then_inc(s_pn, 1)
                hp = e + HP * (mixer == "b")

                def probabilities_lower(st):
                    c = c0 + st
                    dve.wait_ge(s_pth, c + 1 + cd)
                    upper, lower = P0h[:, :, :, st % NX], P0l[:, :, :, st % NX]
                    dve.tensor_tensor(lower, PS[:, 3, :].rearrange("p (b i) -> p b i", b=NX), upper.bitcast(FP32),
                                      ALU.subtract).then_inc(s_ptl, 1)

                def output(head):
                    dve.wait_ge(s_pv, 2 * hp + head + 1 + 2 * dyn)
                    h = slice(64 * head, 64 * head + 64)
                    dve.scalar_tensor_tensor(out=ZS[h], in0=PS[h, 2, :], scalar=0.5, in1=ZS[h], op0=ALU.mult, op1=ALU.mult).then_inc(s_ao, 1)
                mask(0)
                mask(1)
                normalise(0)
                for st in range(n):
                    if st + 1 < n:
                        normalise(st + 1)
                    if st == n // 2:
                        output(0)
                        if mixer == "b" and follows:
                            b_rope(e + 1, dyn, link_in)
                    if mixer == "a":
                        probabilities_lower(st)
                    if st + 2 < n:
                        mask(st + 2)
                    if mixer == "a" and follows:
                        if st == n - 2:
                            a_rope(e + 1, dyn, 0, link_in)
                        if st == n - 1:
                            a_lower(e + 1, dyn)
                output(1)
                dve.wait_ge(s_yh, 16 + hp + 1 + dyn)
                at = bass.ds(e + dyn, 1)
                dve.tensor_tensor(YL2[:, at, :].rearrange("p a t -> p (a t)"), ZS[:],
                                  YH2[:, at, :].rearrange("p a t -> p (a t)").bitcast(FP32), ALU.subtract).then_inc(s_y, 1)
                return hp

            def z_gate(n, ndyn, hp, dyn):
                dve.wait_ge(s_evac, n + 1 + ndyn)
                dve.wait_ge(s_y, 16 + hp + dyn)
                dve.scalar_tensor_tensor(out=ZS[:], in0=TH[:, 0:SEQ], scalar=1.0, in1=Z[:, n % 4, 0:SEQ],
                                         op0=ALU.add, op1=ALU.mult).then_inc(s_used, 1)
                dve.wait_ge(s_used, used(n) + dyn)

            def pair_loop(mixer, per, body):
                last = 6 if mixer == "a" else 4
                linked_loop(last // 2, 2 * per, lambda i, link_in: [body(e, 2 * i, link_in, True) for e in range(2)])
                for e in range(last, HP):
                    body(e, 0, link, e + 1 < HP)

            def eight(s, l):
                dve.memset(TH[:, 0:SEQ], 0.0).then_inc(s_lacc, 1)
                with dve.Fori(0, 2) as i:
                    for u in range(4):
                        dve.wait_ge(s_evac, s + u + 1 + 4 * i)
                        x = X2[:, bass.ds(u + 4 * i, 1), :].rearrange("p a t -> p (a t)")
                        dve.scalar_tensor_tensor(out=x, in0=x, scalar=ALPHA, in1=Z[:, (s + u) % 4, 0:SEQ],
                                                 op0=ALU.mult, op1=ALU.add).then_inc(s_used, 1)
                        dve.wait_ge(s_used, used(s + u) + 4 * i)
                        dve.wait_ge(s_lacc, (KT + 1) * l + 1 + u + 4 * i)
                        dve.tensor_tensor(TH[:, 0:SEQ], TH[:, 0:SEQ], x, ALU.add).then_inc(s_lacc, 1)

            def layer_norm(l):
                dve.wait_ge(s_ph, l + 1)
                dve.tensor_tensor(PL[:], Praw[:], PH[:].bitcast(FP32), ALU.subtract).then_inc(s_pl, 1)
                dve.wait_ge(s_mu, l + 1)
                for k in range(KT):
                    dve.tensor_tensor(X2[:, k], X2[:, k], TH[:, 0:SEQ], ALU.subtract).then_inc(s_lnd, 1)
                dve.wait_ge(s_rstd, 6 + l)

                def upper(k):
                    dve.scalar_tensor_tensor(out=X2[:, k], in0=X2[:, k], scalar=lnp[:, l, 0, k:k + 1], in1=TH[:, 0:SEQ],
                                             op0=ALU.mult, op1=ALU.mult).then_inc(s_xn, 1)

                def biased_lower(k):
                    dve.wait_ge(s_xh, KT * (5 + 2 * l) + k + 1)
                    dve.scalar_tensor_tensor(out=XL2[:, k], in0=X2[:, k], scalar=lnp[:, l, 1, k:k + 1], in1=XH2[:, k].bitcast(FP32),
                                             op0=ALU.add, op1=ALU.subtract).then_inc(s_xl, 1)
                upper(0)
                for k in range(1, KT):
                    upper(k)
                    biased_lower(k - 1)
                biased_lower(KT - 1)

            def ple(l):
                dve.wait_ge(s_xb, KT * (l + 1))

                def body(i, link_in):
                    for u in range(2):
                        n = N_PLE[l] + 2 * u
                        g, v = Z[:, n % 4, 0:SEQ], Z[:, (n + 1) % 4, 0:SEQ]
                        dve.wait_ge(s_evac, n + 2 + 4 * i)
                        link_in(dve.scalar_tensor_tensor(out=g, in0=g, scalar=1.0, in1=v, op0=ALU.add, op1=ALU.mult))
                        x = X2[:, bass.ds(u + 2 * i, 1), :].rearrange("p a t -> p (a t)")
                        dve.scalar_tensor_tensor(out=x, in0=g, scalar=0.5, in1=x, op0=ALU.mult, op1=ALU.add).then_inc(s_used, 2)
                linked_loop(4, 2, body)

            dve.wait_ge(s_rstd, 5)

            def upper(k):
                dve.scalar_tensor_tensor(out=X2[:, k], in0=X[:, k, 0:SEQ], scalar=fin_g[:, k:k + 1], in1=TH[:, 0:SEQ],
                                         op0=ALU.mult, op1=ALU.mult).then_inc(s_xn, 1)
            upper(0)
            for k in range(1, KT):
                upper(k)
                lower(4, k - 1)
            lower(4, KT - 1)
            dve.wait_ge(s_b2, 16)

            def pair_a(e, dyn, link_in, follows):
                n = N_A + A_TILES * e
                for g in (1, 2):
                    a_rope(e, dyn, g, link_in)
                dve.wait_ge(s_vh, e + 1 + dyn)
                dve.tensor_tensor(V0l[:].rearrange("p j d -> p (j d)"), PS[:, 3, :], V0h[:].rearrange("p j d -> p (j d)").bitcast(FP32),
                                  ALU.subtract).then_inc(s_tre, 1)
                for g in (1, 2):
                    dve.wait_ge(s_tr, 20 + 3 * e + g + 1 + 3 * dyn)
                    dve.tensor_copy(VT[:, g - 1].rearrange("p j d -> p (j d)"), PS[:, 3, :]).then_inc(s_tre, 1)
                z_gate(n + 9, A_TILES * dyn, e, dyn)
                attention("a", e, dyn, link_in, follows)

            def pair_b(e, dyn, link_in, follows):
                n = N_BQZ + 2 * e
                z_gate(n + 1, 2 * dyn, HP + e, dyn)
                attention("b", e, dyn, link_in, follows)
            a_rope(0, 0, 0, link)
            a_lower(0, 0)
            pair_loop("a", 3 + 8 * 2, pair_a)
            eight(N_AOUT, 0)
            layer_norm(0)
            ple(0)
            for k in range(KT):
                lower(6, k)
            dve.wait_ge(s_bm, 16)
            rope(Z[:, N_B % 4:N_B % 4 + 2, 0:SEQ], 2, link, 64 * (3 * HP + 1), KB[:])
            dve.wait_ge(s_tr, 20 + 3 * HP + 1)
            dve.tensor_copy(VT[:, 0].rearrange("p j d -> p (j d)"), PS[:, 3, :]).then_inc(s_tre, 1)
            b_rope(0, 0, link)
            pair_loop("b", 1 + 2 * 3, pair_b)
            eight(N_BOUT, 1)
            layer_norm(1)
            ple(1)

        block = stack.enter_context(nc.Block())

        @block.sync
        def _(sp):
            sp.dma_start(cact[:], cT).then_inc(s_const, 16)
            sp.dma_start(cb[:].rearrange("p a k -> p (a k)"), cb_d).then_inc(s_cb, 16)
            sp.dma_start(ident[:], consts_d[:, 0:P]).then_inc(s_const, 16)
            sp.dma_start(tri[:].rearrange("p a b -> p (a b)"), consts_d[:, P:3 * P]).then_inc(s_const, 16)
            sp.dma_start(mskd[:].rearrange("p a b -> p (a b)"), consts_d[:, 3 * P:5 * P]).then_inc(s_const, 16)
            sp.dma_start(dsel[:], consts_d[0:8, 5 * P:5 * P + 2]).then_inc(s_const, 16)
            sp.dma_start(pc[:], pc_d).then_inc(s_const, 16)
            sp.dma_start(fin_g[:], fin_d).then_inc(s_const, 16)

            def load(s, src, dyn=0, cols=KT * P):
                if s >= RING:
                    sp.wait_ge(s_split, s - RING + 1 + dyn)
                sp.dma_start(raw[s % RING][:, 0:cols], src).then_inc(s_raw[s % RING], 16)

            def tile_of(w, i):
                return w[bass.ds(i, 1)].rearrange("a p n -> (a p) n")

            for l in range(DEPTH):
                n0 = l * LAYER_TILES
                if l:
                    sp.wait_ge(s_tile, n0)
                    sp.wait_ge(s_used, used(n0 - 1))
                sp.dma_start(srow[:], srow_d[l]).then_inc(s_par, 16)
                sp.dma_start(sgw[:], sguw_d[l]).then_inc(s_par, 16)
                sp.dma_start(wg[:], wg_d[l]).then_inc(s_par, 16)
                if l == 0:
                    v = p = 0
                    for m in range(MODS):
                        if v * (MODS - MOD_V) <= p * MOD_V and v < MOD_V:
                            slot = v % 8
                            if v == 6:
                                sp.wait_ge(s_cba, 1)
                            if v >= 8:
                                sp.wait_ge(s_mvd, v - 7)
                            sp.dma_start(modv[slot][:], wmod_d[l, v]).then_inc(s_mvw[slot], 16)
                            v += 1
                        else:
                            if p >= MOD_P:
                                sp.wait_ge(s_modd, p - MOD_P + 1)
                            sp.dma_start(modp[p % MOD_P][:].rearrange("p k c -> p (k c)"), wmod_d[l, MOD_V + p]).then_inc(s_modw[p % MOD_P], 16)
                            p += 1
                        if m == MODS // 3:
                            sp.dma_start(X[:], xT).then_inc(s_x, 16)
                for n in range(N_IN):
                    load(n0 + n, win_d[l, n])
                sp.wait_ge(s_st, 2 * NJ * (l + 1))
                sp.wait_ge(s_h, outputs_before(l + 1, 0))
                with sp.Fori(0, 2) as i:
                    for u in range(4):
                        load(n0 + N_IN + u, tile_of(wout_d[l], 4 * i + u), 4 * i)
                for p, (h0, hn) in enumerate(PARTS):
                    s = part_start(l, p)
                    with sp.Fori(0, 2 * hn // 4) as i:
                        for u in range(4):
                            load(s + u, tile_of(wgu_d[l], 4 * i + 2 * h0 + u), 4 * i)
                    with sp.Fori(0, 2) as i:
                        for u in range(4):
                            load(s + 2 * hn + u, tile_of(wdn_d[l, :, :, h0 * P:(h0 + hn) * P], 4 * i + u), 4 * i, hn * P)
            second_sp(sp, load, tile_of)

        @block.gpsimd
        def _(pool):
            pool.memset(ones[:], 1.0).then_inc(s_one, 1)
            pool.memset(eps_c[:, 0:1], EPS).then_inc(s_one, 1)
            pool.memset(eps_c[:, 1:2], LN_EPS).then_inc(s_one, 1)
            pool.wait_ge(s_one, 3)
            for k in range(KT):
                pool.wait_ge(s_sq, k + 1)
                sq, ss = SQ[0][k % 2], SS[0]
                if k:
                    pool.wait_ge(s_acc, k)
                    pool.tensor_tensor(ss[:], ss[:], sq[:], ALU.add).then_inc(s_acc, 1)
                else:
                    pool.tensor_scalar(ss[:], sq[:], 1.0, 0.0, ALU.mult, ALU.add).then_inc(s_acc, 1)
            for l in range(DEPTH):
                n0 = l * LAYER_TILES
                for n in range(N_IN):
                    split_weights(pool, n0 + n)
                pool.wait_ge(s_evac, n0 + N_IN)
                pool.tensor_scalar(tho[:, :, 0:width(l)], tho[:, :, 0:width(l)], 1.0, 0.5, ALU.add, ALU.mult).then_inc(s_tho, 1)
                for t, (d, j, first, gives) in enumerate(mlstm_steps(l)):
                    c = 2 * NJ * l + t
                    if gives and not first:
                        pool.wait_ge(s_wie, c + 1)
                        if outputs_of_slot(l, t):
                            pool.wait_ge(s_nd, outputs_of_slot(l, t))
                        pool.tensor_tensor(Qw[c % 2][:], qfm[:, :, j * P:(j + 1) * P], WIs[c % 2][:], ALU.mult).then_inc(s_qw, 1)
                    pool.wait_ge(s_e, c + 1)
                    if c >= 2:
                        pool.wait_ge(s_u, c - 1)
                    tl = P - 1 if d == 0 else 0
                    pool.tensor_tensor(Ks[c % 2][:], ktm[:, j, :, :], Ee[c % 2][:, :, tl:tl + 1].to_broadcast([P, HEADS, P]),
                                       ALU.mult).then_inc(s_ks, 1)
                with pool.Fori(0, 2) as i:
                    for u in range(4):
                        split_weights(pool, n0 + N_IN + u, 4 * i)
                for p, (h0, hn) in enumerate(PARTS):
                    s = part_start(l, p)
                    with pool.Fori(0, 2 * hn // 4) as i:
                        for u in range(4):
                            split_weights(pool, s + u, 4 * i)
                    with pool.Fori(0, 2) as i:
                        for u in range(4):
                            split_weights(pool, s + 2 * hn + u, 4 * i, hn)
            second_pool(pool)

        @block.tensor
        def _(pe):
            def norm(q, w):
                pe.wait_ge(s_acc, KT * (q + 1))
                for a, b in ranges(w):
                    last = pe.matmul(banks(6, 8)[:, a:b], ones[:], SS[q > 0][:, a:b], start=True, stop=True)
                last.then_inc(s_squ, 1)

            def transpose_tile(l, e, src, nj):
                if 10 * l + e:
                    pe.wait_ge(s_tre, 10 * l + e)
                for j in range(nj):
                    last = pe.transpose(banks(4, 6)[:, j * P:(j + 1) * P], src[:, j * P:(j + 1) * P], ident[:])
                last.then_inc(s_tr, 1)

            def sgu_mix(l, f):
                pe.wait_ge(s_svt, l + 1)
                if 2 * l + f:
                    pe.wait_ge(s_mixu, 2 * l + f)
                for j in range(width(l) // P):
                    for g in range(2):
                        c = f * P + g * 64
                        last = pe.matmul(banks(6, 8)[64 * g:64 * g + 64, j * P:(j + 1) * P], SVT[:, j, c:c + 64],
                                         sgw[:, 2 * f + g, :], start=True, stop=True)
                last.then_inc(s_mix, 1)

            def gates(l):
                pe.wait_ge(s_wgl, l + 1)
                pe.wait_ge(s_tre, 10 * (l + 1))
                for k in range(KT):
                    for a, b in ranges(T):
                        out = banks(4, 6)[0:16, a:b]
                        pe.matmul(out, wgh[:, k, :], XH[:, k, a:b], start=k == 0, stop=False)
                        pe.matmul(out, wgh[:, k, :], XL[:, k, a:b], start=False, stop=False)
                        last = pe.matmul(out, wgl[:, k, :], XH[:, k, a:b], start=False, stop=k == KT - 1)
                last.then_inc(s_grow, 1)
                pe.wait_ge(s_growe, l + 1)
                for j in range(NJ):
                    last = pe.transpose(PS[:, 4, 16 * j:16 * j + 16], grow[:, j * P:(j + 1) * P], ident[0:16, 0:16])
                last.then_inc(s_gate, 1)

            def forget_sums(l):
                pe.wait_ge(s_lf, l + 1)
                for d in range(2):
                    out = banks(5, 6)[:, 0:NJ * 8].rearrange("p (j e) -> p j e", e=8)[:, :, 4 * d:4 * d + 4]
                    last = pe.matmul(out, tri[:, d, :], lf[:, 2, :, 4 * d:4 * d + 4], start=True, stop=True)
                last.then_inc(s_bt, 1)

            def mlstm(l):
                n_end = l * LAYER_TILES + N_IN
                pe.wait_ge(s_btm, l + 1)
                pe.wait_ge(s_evac, n_end)
                for i, src in enumerate((lf[:, 1], lf[:, 2], btm[:])):
                    for j in range(NJ):
                        c = i * T + j * P
                        last = pe.transpose(banks(0, 5)[0:8, c:c + P], src[:, j, :], ident[:])
                last.then_inc(s_rows, 1)
                pe.wait_ge(s_rowl, 3 * (l + 1))

                def spread(bank, i, d, j):
                    for h in range(HEADS):
                        r = 4 * d + h
                        out = PS[:, bank, h * P:(h + 1) * P]
                        pe.matmul(out, selh[:, r, :], rhl[i][0][:, j * P:(j + 1) * P], start=True, stop=False)
                        last = pe.matmul(out, selh[:, r, :], rhl[i][1][:, j * P:(j + 1) * P], start=False, stop=True)
                    return last

                def exponents(t):
                    d, j, first, gives = mlstm_steps(l)[t]
                    c = 2 * NJ * l + t
                    o = outputs_before(l, t)
                    js = slice(j * P, (j + 1) * P)
                    if c:
                        pe.wait_ge(s_w1, c)
                    spread(0, 0, d, j).then_inc(s_nm, 1)
                    if c:
                        pe.wait_ge(s_wie, c)
                    last = spread(1, 1, d, j)
                    if gives:
                        last = spread(2, 2, d, j)
                    last.then_inc(s_wi, 1)
                    if gives:
                        if o:
                            pe.wait_ge(s_p, o)
                        for h in range(HEADS):
                            last = pe.matmul(PS[:, 3, h * P:(h + 1) * P], kfm[:, h, js], qfm[:, h, js], start=True, stop=True)
                        last.then_inc(s_s, 1)

                steps = mlstm_steps(l)
                exponents(0)
                for t, (d, j, first, gives) in enumerate(steps):
                    c = 2 * NJ * l + t
                    o = outputs_before(l, t)
                    if t + 1 < len(steps):
                        exponents(t + 1)
                    if gives:
                        pe.wait_ge(s_p, o + 1)
                        if o:
                            pe.wait_ge(s_nde, o)
                        if not first:
                            pe.wait_ge(s_qw, weighted_before(l, t) + 1)
                            pe.wait_ge(s_st, c - 1)
                        for h in range(HEADS):
                            last = pe.matmul(PS[:, 4, h * P:(h + 1) * P], vtm[:, j, h, :], Pp[c % 2][:, h, :], start=True, stop=first)
                            if not first:
                                last = pe.matmul(PS[:, 4, h * P:(h + 1) * P], ST[d][:, h, 0, :], Qw[c % 2][:, h, :], start=False, stop=True)
                        for h in range(HEADS):
                            last = pe.matmul(PS[:, 5, h * P:(h + 1) * P], ones[:], Pp[c % 2][:, h, :], start=True, stop=first)
                            if not first:
                                last = pe.matmul(PS[:, 5, h * P:(h + 1) * P], ST[d][:, h, 1, :], Qw[c % 2][:, h, :], start=False, stop=True)
                        last.then_inc(s_nd, 1)
                    pe.wait_ge(s_ks, c + 1)
                    if c:
                        pe.wait_ge(s_st, c)
                    for h in range(HEADS):
                        out = banks(6, 8)[:, 2 * h * P:2 * (h + 1) * P]
                        pe.matmul(out[:, 0:P], Ks[c % 2][:, h, :], vtm[:, j, h, :], start=True, stop=True)
                        last = pe.matmul(out[:, P:2 * P], Ks[c % 2][:, h, :], ones[:], start=True, stop=True)
                    last.then_inc(s_u, 1)

            def mixer_stats(l):
                w = width(l)
                for h in range(HEADS):
                    pe.wait_ge(s_hsq, 4 * l + h + 1)
                    for a, b in ranges(w):
                        last = pe.matmul(banks(2 * h, 2 * h + 2)[:, a:b], ones[:], Z[:, h, a:b], start=True, stop=True)
                    last.then_inc(s_hss, 1)

            def conv_sum(l, src, bank, signal):
                for f in range(2):
                    for a, b in ranges(width(l)):
                        last = pe.matmul(banks(bank, bank + 2)[:, a:b], ones[:], src[:, f, a:b], start=f == 0, stop=f == 1)
                last.then_inc(signal, 1)

            pe.wait_ge(s_one, 3)
            pe.wait_ge(s_const, 16 * 7)
            for l in range(DEPTH):
                n0 = l * LAYER_TILES
                if l == 0:
                    pe.wait_ge(s_cact, 1)
                    for m in range(MODS - MOD_V):
                        pe.wait_ge(s_modw[m % MOD_P], 16 * (m // MOD_P + 1))
                        for k in range(KT):
                            last = pe.matmul(PS[:, 5, 2 * m:2 * m + 2], modp[m % MOD_P][:, k, :], cact[:, k, :],
                                             start=k == 0, stop=k == KT - 1)
                        last.then_inc(s_modd, 1)
                norm(2 * l, T)
                first_tiles(pe, n0, XH, XL, width(l), s_xl, 2 * KT * l)
                for t in range(2, N_IN):
                    gemm_tile(pe, n0 + t, XH, XL, width(l, t))
                    if t in (9, 10):
                        pe.wait_ge(s_gel, 2 * l + t - 8)
                        transpose_tile(l, t - 9, Z[:, t - 9 + 2], width(l) // P)
                    if 11 <= t < 15:
                        pe.wait_ge(s_evac, n0 + t - 2)
                        transpose_tile(l, t - 9, kfm[:, t - 11], NJ)
                    if 15 <= t < 19:
                        pe.wait_ge(s_evac, n0 + t - 2)
                        transpose_tile(l, t - 9, Z[:, t - 15], NJ)
                    if t in (18, 19):
                        sgu_mix(l, t - 18)
                    if t == 20:
                        pe.wait_ge(s_mixu, 2 * (l + 1))
                        conv_sum(l, AC, 6, s_csum)
                        gates(l)
                    if t == 22:
                        forget_sums(l)
                        pe.wait_ge(s_csq, l + 1)
                        conv_sum(l, Z, 6, s_cvar)
                mlstm(l)
                mixer_stats(l)
                pe.wait_ge(s_hln, l + 1)
                first_tiles(pe, n0 + N_IN, XH, XL, width(l), s_y, KT * l)
                for u in range(2, KT):
                    gemm_tile(pe, n0 + N_IN + u, XH, XL, width(l))
                norm(2 * l + 1, width(l))
                for p, (h0, hn) in enumerate(PARTS):
                    s = part_start(l, p)
                    if p == 0:
                        first_tiles(pe, s, XH, XL, width(l), s_xl, KT * (2 * l + 1))
                        for u in (2, 3):
                            gemm_tile(pe, s + u, XH, XL, width(l))
                    with pe.Fori(p == 0, 2 * hn // 4) as i:
                        for u in range(4):
                            gemm_tile(pe, s + u, XH, XL, width(l), 4 * i)


                    def hidden_ready(k):
                        pe.wait_ge(s_used, used(s + 2 * k + 1))
                    with pe.Fori(0, 2) as i:
                        for u in range(4):
                            gemm_tile(pe, s + 2 * hn + u, HH, HL, width(l), 4 * i, hn, hidden_ready if u == 0 else None)
            norm(2 * DEPTH, SEQ)
            second_pe(pe)

        @block.scalar
        def _(act):
            links = [0]

            def link(ins):
                links[0] += 1
                ins.then_inc(s_ach, 1)
                act.wait_ge(s_ach, links[0])

            def rstd(dst, src, scale, eps=0):
                link(act.activation(dst, src, ACT.Ln, bias=eps_c[:, eps:eps + 1], scale=scale))
                return act.activation(dst, dst, ACT.Exp, scale=-0.5)

            def norm(q, l, w):
                act.wait_ge(s_squ, q + 1)
                rs = MT if q in (0, 2) else TH
                rstd(rs[:, 0:w], banks(6, 8)[:, 0:w], 1.0 / D).then_inc(s_rstd, 1)
                for k in range(KT):
                    act.wait_ge(s_xn, KT * q + k + 1)
                    for n, (a, b) in enumerate(ranges(w)):
                        last = act.activation(XH[:, k, a:b], Z[:, k % 4, a:b], ACT.Identity, bias=mods[l][:, 24 * (q % 2) + k, n:n + 1])
                    last.then_inc(s_xh, 1)
                act.wait_ge(s_xl, KT * (q + 1))

            def load_mod(l, slot, m):
                act.dma_start(modv[4 + slot][:], m).then_inc(s_mvw[4 + slot], 16)

            def mod_tile(l, m):
                return wmod_d[l][bass.ds(m, 1)].rearrange("a p n -> (a p) n")

            def silu_c(l):
                if l:
                    act.dma_start(cb[:].rearrange("p a k -> p (a k)"), cb_d).then_inc(s_cb, 16)
                act.wait_ge(s_cb, 16 * (l + 1))
                act.activation(cbt[:], cb[:], ACT.Tanh, scale=0.5).then_inc(s_cbt, 1)

            def evacuate(s, out, func=ACT.Identity, bias=0.0, scale=1.0, w=T, dyn=0, need=None, signal=True):
                act.wait_ge(s_tile, s + 1 + dyn)
                if need is not None:
                    act.wait_ge(s_used, need)
                ins = act.activation(out, acc(s)[:, 0:w], func, bias=bias, scale=scale)
                return ins.then_inc(s_evac, 1) if signal else ins

            def residual_tiles(s0, l, gate, dyn, w, u, q=None):
                s = s0 + u
                act.wait_ge(s_tile, s + 1 + dyn)
                act.wait_ge(s_used, used(s - 4) + dyn)
                for n, (a, b) in enumerate(ranges(w)):
                    last = act.activation(Z[:, s % 4, a:b], acc(s)[:, a:b], ACT.Identity,
                                          scale=mods[l][:, bass.ds(gate + u + dyn, 1), n:n + 1].rearrange("p a b -> p (a b)"))
                last.then_inc(s_evac, 1)
                if q is not None:
                    act.wait_ge(s_used, used(s) + dyn)
                    act.wait_ge(s_acc, KT * q + u - 1 + dyn)
                    x = X[:, bass.ds(u + dyn, 1), 0:w].rearrange("p a t -> p (a t)")
                    act.activation(SQ[1][u % 2][:, 0:w], x, ACT.Square).then_inc(s_sq, 1)

            act.wait_ge(s_const, 16 * 7)
            act.wait_ge(s_one, 3)
            act.activation(cth[:], cact[:], ACT.Tanh, scale=0.5).then_inc(s_cth, 1)
            silu_c(0)
            act.wait_ge(s_x, 16)
            for k in range(KT):
                if k >= 2:
                    act.wait_ge(s_acc, k - 1)
                act.activation(SQ[0][k % 2][:], X[:, k], ACT.Square).then_inc(s_sq, 1)
            for l in range(DEPTH):
                n0 = l * LAYER_TILES
                w = width(l)
                act.wait_ge(s_par, 48 * (l + 1))
                act.activation(wgh[:], wg[:], ACT.Copy).then_inc(s_wgh, 1)
                act.wait_ge(s_mod, l + 1)
                norm(2 * l, l, T)
                for t in range(N_IN):
                    n = n0 + t
                    b = bcol[:, t:t + 1]
                    slot = Z[:, n % 4, 0:w]
                    if t in (0, 2):
                        evacuate(n, slot, ACT.Tanh, b, 0.5, w)
                    elif t < K_T:
                        evacuate(n, slot, ACT.Identity, b, 1.0, w, need=used(n - 4) if t >= 4 else None)
                    elif t < V_T:
                        evacuate(n, kfm[:, t - K_T], ACT.Identity, b, K_SCALE)
                    elif t < Q_T:
                        act.wait_ge(s_tre, 10 * l + 2)
                        act.wait_ge(s_used, used(n0 + U_T + 1))
                        evacuate(n, Z[:, n % 4], ACT.Identity, b, 1.0)
                    elif t < O_T:
                        act.wait_ge(s_gel, 2 * (l + 1))
                        evacuate(n, qfm[:, t - Q_T, 0:w], ACT.Identity, b, 1.0, w)
                    else:
                        act.wait_ge(s_mix, 2 * (l + 1))
                        evacuate(n, tho[:, t - O_T, 0:w], ACT.Tanh, b, 0.5, w)
                    if 6 <= t < 10:
                        act.wait_ge(s_gin, 4 * l + t - 5)
                        g = GT[:, t - 6, 0:w]
                        act.activation(g, g, ACT.Tanh, scale=GELU_C).then_inc(s_gth, 1)
                    if t == 11:
                        act.wait_ge(s_svv, l + 1)
                        rstd(bmv[:, 0:w // P, 1:2], bmv[:, 0:w // P, 1:2], 1.0).then_inc(s_svr, 1)
                    if t == 20:
                        act.wait_ge(s_csum, l + 1)
                        act.activation(MU[:, 0:w], banks(6, 8)[:, 0:w], ACT.Copy, scale=1.0 / 256).then_inc(s_cmu, 1)
                        act.wait_ge(s_grow, l + 1)
                        act.activation(grow[:], banks(4, 6)[0:16, 0:T], ACT.Copy).then_inc(s_growe, 1)
                    if t == 21:
                        act.wait_ge(s_gtm, l + 1)
                        sp = lf[:, 0].rearrange("p j (d h) -> p j d h", d=2)
                        for j in range(NJ):
                            last = act.activation(sp[:, j], gt[:, j, :, 1, :], ACT.Abs)
                        link(last)
                        link(act.activation(lf[:, 0], lf[:, 0], ACT.Exp, scale=-1.0))
                        act.activation(lf[:, 0], lf[:, 0], ACT.Ln, bias=1.0).then_inc(s_lfa, 1)
                        act.wait_ge(s_cd, l + 1)
                        act.activation(Z[:, 0:2, 0:w], AC[:, :, 0:w], ACT.Square).then_inc(s_csq, 1)
                    if t == 22:
                        act.wait_ge(s_cvar, l + 1)
                        rstd(MU[:, 0:w], banks(6, 8)[:, 0:w], 1.0 / 256).then_inc(s_crs, 1)
                    if t == 23:
                        act.wait_ge(s_cl, l + 1)
                        act.activation(Z[:, 0:2, 0:w], AC[:, :, 0:w], ACT.Tanh, scale=0.5).then_inc(s_cta, 1)
                act.wait_ge(s_row, l + 1)
                for i, r in enumerate((ri, rb, rf)):
                    act.activation(rhl[i][0][:], r[:], ACT.Copy).then_inc(s_rowh, 1)

                def exponentials(t):
                    gives = mlstm_steps(l)[t][3]
                    c = 2 * NJ * l + t
                    act.wait_ge(s_wi, c + 1)
                    if c >= 2:
                        act.wait_ge(s_st, c - 1)
                    if weighted_before(l, max(t - 1, 0)):
                        act.wait_ge(s_qw, weighted_before(l, max(t - 1, 0)))
                    last = act.activation(WIs[c % 2][:], PS[:, 1, :].rearrange("p (h t) -> p h t", h=HEADS), ACT.Exp)
                    if gives:
                        if outputs_of_slot(l, t):
                            act.wait_ge(s_h, outputs_of_slot(l, t))
                        last = act.activation(EMs[c % 2][:], PS[:, 2, :].rearrange("p (h t) -> p h t", h=HEADS), ACT.Exp)
                    last.then_inc(s_wie, 1)
                    act.wait_ge(s_w1, c + 1)
                    if c >= 2:
                        act.wait_ge(s_ks, c - 1)
                    if outputs_of_slot(l, t):
                        act.wait_ge(s_p, outputs_of_slot(l, t))
                    act.activation(Ee[c % 2][:], W1[:], ACT.Exp).then_inc(s_e, 1)

                steps = mlstm_steps(l)
                exponentials(0)
                for t, (d, j, first, gives) in enumerate(steps):
                    if t + 1 < len(steps):
                        exponentials(t + 1)
                    if gives:
                        o = outputs_before(l, t)
                        act.wait_ge(s_nd, o + 1)
                        if o:
                            act.wait_ge(s_h, o)
                        act.activation(AD[:], PS[:, 5, :].rearrange("p (h t) -> p h t", h=HEADS), ACT.Abs)
                        act.activation(HN[:], PS[:, 4, :].rearrange("p (h t) -> p h t", h=HEADS), ACT.Copy).then_inc(s_nde, 1)
                act.wait_ge(s_h, outputs_before(l + 1, 0))
                act.wait_ge(s_st, 2 * NJ * (l + 1))
                for h in range(HEADS):
                    act.activation(Z[:, h, 0:w], H[:, h, 0:w], ACT.Square).then_inc(s_hsq, 1)
                for i in range(4):
                    src = Ug[:, i] if i < 2 else AC[:, i - 2]
                    act.activation(XH[:, i, 0:w], src[:, 0:w], ACT.Copy).then_inc(s_yh, 1)
                for h in range(HEADS):
                    act.wait_ge(s_hss, 4 * l + h + 1)
                    last = act.activation(RH[:, h, 0:w], banks(2 * h, 2 * h + 2)[:, 0:w], ACT.Ln, bias=eps_c[:, 0:1], scale=1.0 / HD)
                    if h == 1:
                        last.then_inc(s_hln, 1)
                link(last)
                for h in range(HEADS):
                    act.activation(RH[:, h, 0:w], RH[:, h, 0:w], ACT.Exp, scale=-0.5).then_inc(s_hr, 1)
                for h in range(HEADS):
                    act.wait_ge(s_yf, HEADS * l + h + 1)
                    act.activation(XH[:, 4 + h, 0:w], H[:, h, 0:w], ACT.Copy).then_inc(s_yh, 1)
                with act.Fori(0, 2) as i:
                    for u in range(4):
                        residual_tiles(n0 + N_IN, l, 16, 4 * i, w, u, 2 * l + 1)
                norm(2 * l + 1, l, w)
                more = l + 1 < DEPTH
                if more:
                    for m in range(2):
                        load_mod(l + 1, m, wmod_d[l + 1, m])
                    silu_c(l + 1)
                    act.wait_ge(s_cba, l + 2)
                    for m in range(2, 4):
                        load_mod(l + 1, m, wmod_d[l + 1, m])
                for p, (h0, hn) in enumerate(PARTS):
                    s = part_start(l, p)
                    with act.Fori(0, 2 * hn // 4) as i:
                        for e in range(2):
                            n = s + 2 * e
                            pair = FT * l + h0 + e
                            act.wait_ge(s_tile, n + 1 + 4 * i)
                            act.wait_ge(s_used, used(n - 4) + 4 * i)
                            if pair:
                                act.wait_ge(s_hf, pair + 2 * i)
                            act.activation(Z[:, n % 4, 0:w], acc(n)[:, 0:w], ACT.Identity)
                            act.activation(TH[:, 0:w], acc(n)[:, 0:w], ACT.Tanh, scale=0.5).then_inc(s_evac, 1)
                            evacuate(n + 1, Z[:, (n + 1) % 4, 0:w], w=w, dyn=4 * i, need=used(n - 3) + 4 * i)
                            act.wait_ge(s_hf, pair + 1 + 2 * i)
                            act.activation(HH[:, bass.ds(2 * i + e, 1), 0:w].rearrange("p a t -> p (a t)"), Z[:, (n + 1) % 4, 0:w],
                                           ACT.Copy).then_inc(s_hh, 1)
                        if more:
                            for u in range(4):
                                m = 2 * h0 + u
                                act.wait_ge(s_mvd, MOD_V + m + 1 + 4 * i)
                                load_mod(l + 1, u, mod_tile(l + 1, m + 4 + 4 * i))
                    with act.Fori(0, 2) as i:
                        for u in range(4):
                            residual_tiles(s + 2 * hn, l, 40, 4 * i, w, u, 2 * l + 2 if p == len(PARTS) - 1 else None)
            second_act(act, link, rstd, evacuate)

        @block.vector
        def _(dve):
            links = [0]

            def link(ins):
                links[0] += 1
                ins.then_inc(s_dch, 1)
                dve.wait_ge(s_dch, links[0])

            def linked_loop(n, per, body):
                start = links[0]
                with dve.Fori(0, n) as i:
                    count = [0]

                    def link_in(ins):
                        count[0] += 1
                        ins.then_inc(s_dch, 1)
                        dve.wait_ge(s_dch, start + count[0] + per * i)
                    body(i, link_in)
                    assert count[0] == per, count
                links[0] = start + n * per

            def col(l, name, i=0):
                return pc[:, l, PC[name] + i:PC[name] + i + 1]

            def norm(q, l, w):
                rs = MT if q in (0, 2) else TH
                second = q % 2
                dve.wait_ge(s_rstd, q + 1)

                def scaled(k):
                    if k >= 4:
                        dve.wait_ge(s_xl, KT * q + k - 3)
                    for n, (a, b) in enumerate(ranges(w)):
                        last = dve.scalar_tensor_tensor(out=Z[:, k % 4, a:b], in0=X[:, k, a:b], scalar=nsc[:, second, k, n:n + 1],
                                                        in1=rs[:, a:b], op0=ALU.mult, op1=ALU.mult)
                    last.then_inc(s_xn, 1)

                def lower(k):
                    dve.wait_ge(s_xh, KT * q + k + 1)
                    for n, (a, b) in enumerate(ranges(w)):
                        last = dve.scalar_tensor_tensor(out=XL[:, k, a:b], in0=Z[:, k % 4, a:b], scalar=mods[l][:, 24 * second + k, n:n + 1],
                                                        in1=XH[:, k, a:b].bitcast(FP32), op0=ALU.add, op1=ALU.subtract)
                    last.then_inc(s_xl, 1)
                scaled(0)
                for k in range(1, KT):
                    scaled(k)
                    lower(k - 1)
                lower(KT - 1)

            def activate_c(l):
                dve.wait_ge(s_cbt, l + 1)
                link(dve.scalar_tensor_tensor(out=cb[:], in0=cbt[:], scalar=1.0, in1=cb[:], op0=ALU.add, op1=ALU.mult))
                dve.tensor_scalar(cb[:], cb[:], 0.5, None, ALU.mult).then_inc(s_cba, 1)
                dve.wait_ge(s_cba, l + 1)

            def mod_tiles(l, first, dyn, slots, loads, link_in):
                for u in range(4):
                    dve.wait_ge(s_mvw[slots + u], 16 * loads + 4 * dyn)
                    for n in range(2):
                        last = dve.tensor_tensor_reduce(out=cprod[:], in0=modv[slots + u][:], in1=cb[:, n, :], scale=1.0, scalar=0.0,
                                                        op0=ALU.mult, op1=ALU.add, accum_out=macc[:, u, n:n + 1])
                        if n == 0:
                            link_in(last)
                    last.then_inc(s_mvd, 1)
                    dve.wait_ge(s_mvd, (MOD_V if l else 0) + first + u + 1 + dyn)
                at = bass.ds(first + dyn, 4)
                link_in(dve.tensor_copy(mods[l][:, at, :], macc[:]))

            def convolve(l, w, part, parts):
                grid = lambda v: v.rearrange("p (r c) -> p r c", c=GRID)
                todo = [(0, GRID, 1, CONV_K // 2, grid, 0, SEQ), (1, SEQ, GRID, SEQ // GRID - 1, None, 0, SEQ)]
                if w == T:
                    todo += [(f, CTX, 1, CONV_K // 2, None, SEQ, T) for f in range(2)]
                taps = [(line, o) for line in todo for o in [0] + [o for o in range(-line[3], line[3] + 1) if o]]
                for (f, n, step, reach, shape, t0, t1), o in taps[part * len(taps) // parts:(part + 1) * len(taps) // parts]:
                    src, dst = YC[:, f, t0:t1], AC[:, f, t0:t1]
                    tap = col(l, "cw", f * CONV_K + CONV_K // 2 + o)
                    if o == 0:
                        link(dve.tensor_scalar(dst, src, tap, col(l, "cb", f), ALU.mult, ALU.add))
                        continue
                    a, b = max(0, -o * step), n - max(0, o * step)
                    if shape:
                        cut = lambda v, p, q: shape(v)[:, :, p:q]
                    else:
                        cut = lambda v, p, q: v[:, p:q]
                    link(dve.scalar_tensor_tensor(out=cut(dst, a, b), in0=cut(src, a + o * step, b + o * step),
                                                  scalar=tap, in1=cut(dst, a, b), op0=ALU.mult, op1=ALU.add))

            def add_residual(s0, u, dyn, w, q=None):
                s = s0 + u
                dve.wait_ge(s_evac, s + 1 + dyn)
                x = X[:, bass.ds(u + dyn, 1), 0:w].rearrange("p a t -> p (a t)")
                dve.tensor_tensor(x, x, Z[:, s % 4, 0:w], ALU.add).then_inc(s_used, 1)
                if q is not None:
                    dve.wait_ge(s_sq, KT * q + u + 1 + dyn)
                    dve.wait_ge(s_acc, KT * q + u + dyn)
                    dve.tensor_tensor(SS[1][:, 0:w], SS[1][:, 0:w], SQ[1][u % 2][:, 0:w], ALU.add).then_inc(s_acc, 1)

            dve.wait_ge(s_const, 16 * 7)
            dve.wait_ge(s_cth, 1)
            link(dve.scalar_tensor_tensor(out=cth[:], in0=cth[:], scalar=1.0, in1=cact[:], op0=ALU.add, op1=ALU.mult))
            dve.tensor_scalar(cact[:], cth[:], 0.5, None, ALU.mult).then_inc(s_cact, 1)
            activate_c(0)
            for g in range(MOD_V // 4):
                mod_tiles(0, 4 * g, 0, 4 * (g % 2), g // 2 + 1, link)
            for l in range(DEPTH):
                n0 = l * LAYER_TILES
                w = width(l)
                nj = w // P
                dve.wait_ge(s_wgh, l + 1)
                dve.tensor_tensor(wgl[:], wg[:], wgh[:].bitcast(FP32), ALU.subtract).then_inc(s_wgl, 1)
                mod = mods[l]
                if l == 0:
                    dve.wait_ge(s_modd, MODS - MOD_V)
                    link(dve.tensor_copy(mod[:, MOD_V:MODS, :], PS[:, 5, 0:2 * (MODS - MOD_V)].rearrange("p (m o) -> p m o", o=2)))
                mb = pc[:, l, PC["b_mod"]:PC["b_mod"] + 48].rearrange("p (m o) -> p m o", o=1).to_broadcast([P, 48, 2])
                link(dve.tensor_tensor(mod[:], mod[:], mb, ALU.add))
                for i, name in enumerate(("norm1", "norm2")):
                    g = pc[:, l, PC[name]:PC[name] + KT].rearrange("p (m o) -> p m o", o=1).to_broadcast([P, KT, 2])
                    at = 8 + 24 * i
                    link(dve.scalar_tensor_tensor(out=nsc[:, i], in0=mod[:, at:at + KT, :], scalar=1.0, in1=g, op0=ALU.add, op1=ALU.mult))
                link(dve.tensor_copy(bcol[:], pc[:, l, PC["b_in"]:PC["b_in"] + N_IN]))
                dve.tensor_scalar(bcol[:, 0:1], bcol[:, 0:1], 0.5, None, ALU.mult)
                dve.tensor_scalar(bcol[:, 2:3], bcol[:, 2:3], 0.5, None, ALU.mult)
                dve.tensor_scalar(bcol[:, O_T:N_IN], bcol[:, O_T:N_IN], 0.5, None, ALU.mult)
                dve.tensor_scalar(bcol[:, K_T:V_T], bcol[:, K_T:V_T], K_SCALE, None, ALU.mult).then_inc(s_mod, 1)
                dve.wait_ge(s_mod, l + 1)
                norm(2 * l, l, T)
                for f in range(2):
                    dve.wait_ge(s_evac, n0 + 2 * f + 2)
                    g = Z[:, 2 * f, 0:w]
                    link(dve.tensor_scalar(g, g, 1.0, 0.5, ALU.add, ALU.mult))
                    dve.tensor_tensor(YC[:, f, 0:w], g, Z[:, 2 * f + 1, 0:w], ALU.mult).then_inc(s_used, 2)
                for i in range(4):
                    dve.wait_ge(s_evac, n0 + U_T + i + 1)
                    g, z = GT[:, i, 0:w], Z[:, i, 0:w]
                    link(dve.tensor_tensor(g, z, z, ALU.mult))
                    link(dve.tensor_scalar(g, g, GELU_A, 1.0, ALU.mult, ALU.add))
                    dve.tensor_tensor(g, g, z, ALU.mult).then_inc(s_gin, 1)
                for i in range(4):
                    dve.wait_ge(s_gth, 4 * l + i + 1)
                    g, z = GT[:, i, 0:w], Z[:, i, 0:w]
                    link(dve.scalar_tensor_tensor(out=g, in0=g, scalar=1.0, in1=z, op0=ALU.add, op1=ALU.mult))
                    out = Ug[:, i, 0:w] if i < 2 else z
                    dve.tensor_scalar(out, g, 0.5, None, ALU.mult).then_inc(s_used if i < 2 else s_gel, 1)
                for e in range(2):
                    dve.wait_ge(s_tr, 10 * l + e + 1)
                    dve.tensor_copy(SVT[:, 0:nj, e * P:(e + 1) * P],
                                    banks(4, 6)[:, 0:nj * P].rearrange("p (j c) -> p j c", c=P)).then_inc(s_tre, 1)
                dve.wait_ge(s_tre, 10 * l + 2)
                dve.wait_ge(s_par, 48 * (l + 1))
                for j in range(nj):
                    last = dve.bn_stats(bst[:, j, :], SVT[:, j, :])
                link(last)
                for j in range(nj):
                    last = dve.bn_aggr(bmv[:, j, :], bst[:, j, :])
                last.then_inc(s_svv, 1)
                dve.wait_ge(s_svr, l + 1)
                for j in range(nj):
                    last = dve.tensor_scalar(SVT[:, j, :], SVT[:, j, :], bmv[:, j, 0:1], bmv[:, j, 1:2], ALU.subtract, ALU.mult)
                link(last)
                for i in range(2):
                    row = srow[:, 256 * i:256 * (i + 1)].rearrange("p (a c) -> p a c", a=1).to_broadcast([P, nj, 256])
                    last = dve.tensor_tensor(SVT[:, 0:nj, :], SVT[:, 0:nj, :], row, (ALU.mult, ALU.add)[i])
                    if i == 0:
                        link(last)
                last.then_inc(s_svt, 1)
                for e in range(2, 10):
                    dve.wait_ge(s_tr, 10 * l + e + 1)
                    dst = ktm if e < 6 else vtm
                    dve.tensor_copy(dst[:, :, (e - 2) % 4, :], banks(4, 6)[:, 0:T].rearrange("p (j c) -> p j c", c=P)).then_inc(s_tre, 1)
                    convolve(l, w, e - 2, 8)
                for f in range(2):
                    dve.wait_ge(s_mix, 2 * l + f + 1)
                    bias = srow[:, SROW_B + f * P:SROW_B + (f + 1) * P].rearrange("p (a c) -> p a c", a=1).to_broadcast([P, nj, P])
                    z = Z[:, f, 0:w].rearrange("p (j c) -> p j c", c=P)
                    dve.tensor_tensor(z, banks(6, 8)[:, 0:w].rearrange("p (j c) -> p j c", c=P), bias, ALU.add).then_inc(s_mixu, 1)
                    dve.wait_ge(s_mixu, 2 * l + f + 1)
                    link(dve.tensor_tensor(Ug[:, f, 0:w], Ug[:, f, 0:w], Z[:, f, 0:w], ALU.mult))
                dve.wait_ge(s_cmu, l + 1)
                for f in range(2):
                    last = dve.tensor_tensor(AC[:, f, 0:w], AC[:, f, 0:w], MU[:, 0:w], ALU.subtract)
                last.then_inc(s_cd, 1)
                dve.wait_ge(s_gate, l + 1)
                gb = srow[:, SROW_G:SROW_G + 16].rearrange("p (a c) -> p a c", a=1).to_broadcast([P, NJ, 16])
                dve.tensor_tensor(gt[:].rearrange("p j d i h -> p j (d i h)"), PS[:, 4, 0:16 * NJ].rearrange("p (j c) -> p j c", c=16),
                                  gb, ALU.add).then_inc(s_gtm, 1)
                dve.wait_ge(s_lfa, l + 1)
                lfv = lf[:].rearrange("p n j (d h) -> p n j d h", d=2)
                for d in range(2):
                    last = dve.tensor_scalar(lfv[:, 1, :, d, :], gt[:, :, d, 1, :], 0.0, None, ALU.min)
                link(last)
                link(dve.tensor_tensor(lf[:, 2], lf[:, 1], lf[:, 0], ALU.subtract))
                for d in range(2):
                    last = dve.tensor_copy(lfv[:, 1, :, d, :], gt[:, :, d, 0, :])
                last.then_inc(s_lf, 1)
                dve.wait_ge(s_lf, l + 1)
                dve.wait_ge(s_bt, l + 1)
                dve.tensor_copy(btm[:].rearrange("p j e -> p (j e)"), PS[:, 5, 0:NJ * 8]).then_inc(s_btm, 1)
                dve.wait_ge(s_btm, l + 1)
                link(dve.tensor_tensor(gcol[:], lf[:, 1], btm[:], ALU.subtract))
                dve.wait_ge(s_crs, l + 1)
                for f in range(2):
                    last = dve.scalar_tensor_tensor(out=AC[:, f, 0:w], in0=AC[:, f, 0:w], scalar=col(l, "cg", f), in1=MU[:, 0:w],
                                                    op0=ALU.mult, op1=ALU.mult)
                link(last)
                for f in range(2):
                    last = dve.tensor_scalar(AC[:, f, 0:w], AC[:, f, 0:w], col(l, "clb", f), None, ALU.add)
                last.then_inc(s_cl, 1)
                dve.wait_ge(s_cta, l + 1)
                link(dve.scalar_tensor_tensor(out=AC[:, :, 0:w], in0=Z[:, 0:2, 0:w], scalar=1.0, in1=AC[:, :, 0:w], op0=ALU.add, op1=ALU.mult))
                link(dve.tensor_scalar(AC[:, :, 0:w], AC[:, :, 0:w], 0.5, None, ALU.mult))
                dve.wait_ge(s_rows, l + 1)
                for i, r in enumerate((ri, rf, rb)):
                    last = dve.tensor_copy(r[:], banks(0, 5)[0:8, i * T:(i + 1) * T])
                link(last)
                scan = lambda o, f, i, m0: link(dve.tensor_tensor_scan(o, f, i, m0, ALU.add, ALU.max))
                cs, ss = slice(SEQ, T), slice(0, SEQ)
                scan(rm[:, cs], rf[:, cs], ri[:, cs], 0.0)
                scan(rm[:, ss], rf[:, ss], ri[:, ss], rm[:, T - 1:T])
                scan(r2[:, cs][:, ::-1], rf[:, cs][:, ::-1], ri[:, cs][:, ::-1], 0.0)
                scan(r2[:, ss][:, ::-1], rf[:, ss][:, ::-1], ri[:, ss][:, ::-1], r2[:, SEQ:SEQ + 1])
                link(dve.memset(mprev[:], 0.0))
                dve.tensor_copy(mprev[:, 0, NJ - 1:NJ], rm[:, T - P - 1:T - P])
                dve.tensor_copy(mprev[:, 0, 0:1], rm[:, T - 1:T])
                dve.tensor_copy(mprev[:, 0, 1:NX], rm[:, P - 1:SEQ - P:P])
                link(dve.tensor_copy(mprev[:, 1, 0:NJ - 1], r2[:, P:T:P]))
                for one, two in ((rm[:], r2[:]), (mprev[:, 0], mprev[:, 1])):
                    link(dve.tensor_scalar(one, one, dsel[:, 0:1], None, ALU.mult))
                    link(dve.scalar_tensor_tensor(out=one, in0=two, scalar=dsel[:, 1:2], in1=one, op0=ALU.mult, op1=ALU.add))
                link(dve.tensor_copy(selh[:], ident[0:8, 0:8].rearrange("p (r c) -> p r c", c=1).to_broadcast([8, 8, P])))
                link(dve.tensor_tensor(ri[:], rb[:], rm[:], ALU.subtract))
                mp = mprev[:, 0].rearrange("p (j o) -> p j o", o=1).to_broadcast([8, NJ, P])
                dve.tensor_tensor(rb[:].rearrange("p (j t) -> p j t", t=P), ri[:].rearrange("p (j t) -> p j t", t=P), mp, ALU.add)
                dve.tensor_scalar(rf[:], rm[:], -1.0, None, ALU.mult).then_inc(s_row, 1)
                for i, r in enumerate((ri, rb, rf)):
                    dve.wait_ge(s_rowh, 3 * l + i + 1)
                    dve.tensor_tensor(rhl[i][1][:], r[:], rhl[i][0][:].bitcast(FP32), ALU.subtract).then_inc(s_rowl, 1)
                written = set()
                steps = mlstm_steps(l)

                def log_weights(t):
                    d, j = steps[t][0:2]
                    c = 2 * NJ * l + t
                    dve.wait_ge(s_nm, c + 1)
                    if c:
                        dve.wait_ge(s_e, c)
                    for h in range(HEADS):
                        last = dve.scalar_tensor_tensor(out=W1[:, h, :], in0=PS[:, 0, h * P:(h + 1) * P],
                                                        scalar=gcol[:, j, 4 * d + h:4 * d + h + 1], in1=mskd[:, d, :],
                                                        op0=ALU.add, op1=ALU.min)
                    last.then_inc(s_w1, 1)

                def weighted_scores(t):
                    c = 2 * NJ * l + t
                    if steps[t][3]:
                        dve.wait_ge(s_e, c + 1)
                        dve.wait_ge(s_s, outputs_before(l, t) + 1)
                        if outputs_of_slot(l, t):
                            dve.wait_ge(s_nd, outputs_of_slot(l, t))
                        dve.tensor_tensor(Pp[c % 2][:], PS[:, 3, :].rearrange("p (h t) -> p h t", h=HEADS), Ee[c % 2][:],
                                          ALU.mult).then_inc(s_p, 1)
                log_weights(0)
                weighted_scores(0)
                log_weights(1)
                for t, (d, j, first, gives) in enumerate(steps):
                    c = 2 * NJ * l + t
                    o = outputs_before(l, t)
                    if t + 1 < len(steps):
                        weighted_scores(t + 1)
                    dve.wait_ge(s_u, c + 1)
                    dve.wait_ge(s_wie, c + 1)
                    tl = P - 1 if d == 0 else 0
                    for h in range(HEADS):
                        st = ST[d][:, h].rearrange("p a c -> p (a c)")
                        up = banks(6, 8)[:, 2 * h * P:2 * (h + 1) * P]
                        if first:
                            last = dve.tensor_copy(st, up)
                        else:
                            last = dve.scalar_tensor_tensor(out=st, in0=st, scalar=WIs[c % 2][:, h, tl:tl + 1], in1=up, op0=ALU.mult, op1=ALU.add)
                    last.then_inc(s_st, 1)
                    if t + 2 < len(steps):
                        log_weights(t + 2)
                    dve.wait_ge(s_st, c + 1)
                    if gives:
                        dve.wait_ge(s_nde, o + 1)
                        link(dve.tensor_tensor(AD[:], AD[:], EMs[c % 2][:], ALU.max))
                        link(dve.reciprocal(AD[:], AD[:]))
                        hj = H[:, :, j * P:(j + 1) * P]
                        if j in written:
                            link(dve.tensor_tensor(HN[:], HN[:], AD[:], ALU.mult))
                            dve.tensor_tensor(hj, hj, HN[:], ALU.add).then_inc(s_h, 1)
                        else:
                            dve.tensor_tensor(hj, HN[:], AD[:], ALU.mult).then_inc(s_h, 1)
                        written.add(j)
                dve.wait_ge(s_h, outputs_before(l + 1, 0))
                dve.wait_ge(s_hsq, 4 * (l + 1))
                dve.wait_ge(s_tho, l + 1)
                for h in range(HEADS):
                    last = dve.scalar_tensor_tensor(out=H[:, h, 0:w], in0=H[:, h, 0:w], scalar=col(l, "mg", h), in1=tho[:, h, 0:w],
                                                    op0=ALU.mult, op1=ALU.mult)
                link(last)

                def lower(i, src):
                    dve.wait_ge(s_yh, KT * l + i + 1)
                    dve.tensor_tensor(XL[:, i, 0:w], src[:, 0:w], XH[:, i, 0:w].bitcast(FP32), ALU.subtract).then_inc(s_y, 1)
                for i in range(4):
                    lower(i, Ug[:, i] if i < 2 else AC[:, i - 2])
                for h in range(HEADS):
                    dve.wait_ge(s_hr, HEADS * l + h + 1)
                    dve.tensor_tensor(H[:, h, 0:w], H[:, h, 0:w], RH[:, h, 0:w], ALU.mult).then_inc(s_yf, 1)
                for h in range(HEADS):
                    lower(4 + h, H[:, h])
                link(dve.memset(SS[1][:, 0:w], 0.0))
                with dve.Fori(0, 2) as i:
                    for u in range(4):
                        add_residual(n0 + N_IN, u, 4 * i, w, 2 * l + 1)
                norm(2 * l + 1, l, w)
                more = l + 1 < DEPTH
                if more:
                    activate_c(l + 1)
                for p, (h0, hn) in enumerate(PARTS):
                    s = part_start(l, p)

                    def hidden(i, link_in):
                        if more:
                            mod_tiles(l + 1, 2 * h0, 4 * i, 4, MOD_V // 8 + h0 // 2 + 1, link_in)
                        for e in range(2):
                            n = s + 2 * e
                            pair = FT * l + h0 + e
                            g, v = Z[:, n % 4, 0:w], Z[:, (n + 1) % 4, 0:w]
                            dve.wait_ge(s_evac, n + 2 + 4 * i)
                            link_in(dve.scalar_tensor_tensor(out=g, in0=TH[:, 0:w], scalar=1.0, in1=g, op0=ALU.add, op1=ALU.mult))
                            dve.scalar_tensor_tensor(out=v, in0=g, scalar=0.5, in1=v, op0=ALU.mult, op1=ALU.mult).then_inc(s_hf, 1)
                            dve.wait_ge(s_hh, pair + 1 + 2 * i)
                            at = bass.ds(2 * i + e, 1)
                            hh = HH[:, at, 0:w].rearrange("p a t -> p (a t)").bitcast(FP32)
                            dve.tensor_tensor(HL[:, at, 0:w].rearrange("p a t -> p (a t)"), v, hh, ALU.subtract).then_inc(s_used, 2)
                    linked_loop(2 * hn // 4, 7 if more else 2, hidden)
                    q = 2 * l + 2 if p == len(PARTS) - 1 else None
                    if q is not None:
                        if more:
                            mod_tiles(l + 1, MODS - 4, 0, 4, MOD_V // 8 + MODS // 4, link)
                        link(dve.memset(SS[1][:, 0:w], 0.0))
                    with dve.Fori(0, 2) as i:
                        for u in range(4):
                            add_residual(s + 2 * hn, u, 4 * i, w, q)
            second_dve(dve, link, linked_loop)

def tiles_of(w):
    k, n = w.shape[-2] // P, w.shape[-1] // P
    v = w.reshape(w.shape[:-2] + (k, P, n, P))
    m = v.ndim
    v = np.transpose(v, tuple(range(m - 4)) + (m - 2, m - 3, m - 4, m - 1))
    return np.ascontiguousarray(v.reshape(w.shape[:-2] + (n, P, k * P)))


def columns_of(v):
    v = v.reshape(v.shape[:-1] + (-1, P))
    return np.ascontiguousarray(np.moveaxis(v, -1, 0))


def kernel(**inputs):
    import concourse.bacc as _bacc
    from concourse.bass_utils import run_bass_kernel_spmd as _run
    a = {k: np.asarray(v) for k, v in inputs.items()}
    f = np.float32
    q, k, v, o, gate, sgu, conv = 0, 512, 1024, 1536, 2048, 2064, 2576
    order = [conv + 256, conv, conv + 384, conv + 128] + [sgu + i * P for i in range(4)]
    for base in (k, v, q, o):
        order += [base + i * P for i in range(4)]
    cols = np.concatenate([np.arange(c, c + P) for c in order])
    gcols = np.arange(gate, gate + 16)
    ts = np.arange(P)
    tri = (ts[:, None] <= ts[None, :]).astype(f)
    consts = np.zeros((P, N_CONST), f)
    consts[:, 0:P] = np.eye(P, dtype=f)
    consts[:, P:2 * P], consts[:, 2 * P:3 * P] = tri, tri.T
    consts[:, 3 * P:4 * P], consts[:, 4 * P:5 * P] = np.where(tri > 0, 0, NEG), np.where(tri.T > 0, 0, NEG)
    consts[0:4, 5 * P] = 1
    consts[4:8, 5 * P + 1] = 1
    par = []
    for l in range(DEPTH):
        cw = a["conv_w"][l].T.reshape(2, P, CONV_K)
        par.append(np.concatenate([columns_of(a["norm1_g"][l]), columns_of(a["norm2_g"][l]), columns_of(a["b_in"][l][cols]),
                                   columns_of(a["mlstm_g"][l]), cw[0], cw[1], columns_of(a["conv_b"][l]),
                                   columns_of(a["conv_ln_g"][l]), columns_of(a["conv_ln_b"][l]), columns_of(a["b_mod"][l])], axis=1))
    rows = []
    for l in range(DEPTH):
        sb = a["sgu_b"][l].reshape(2, 2, 1, P)
        sb = np.broadcast_to(sb, (2, 2, 64, P)).reshape(2, P, P)
        wide = lambda r: np.broadcast_to(r[None], (P, r.shape[0]))
        rows.append(np.concatenate([wide(a["sgu_ln_g"][l]), wide(a["sgu_ln_b"][l]), sb[0], sb[1], wide(a["b_in"][l][gcols])], axis=1))
    w_gu = a["w_gu"].reshape(DEPTH, D, 2, FT, P).transpose(0, 1, 3, 2, 4).reshape(DEPTH, D, 2 * FFN)
    wg = a["w_in"][:, :, gcols].reshape(DEPTH, KT, P, 16).transpose(0, 2, 1, 3)
    rows_of = a["w_mod"].transpose(0, 2, 1).reshape(DEPTH, MODS, P, D)
    wmod = np.concatenate([rows_of[0:1, 0:MOD_V], tiles_of(a["w_mod"])[0:1, MOD_V:]], axis=1)
    wmod = np.concatenate([wmod, rows_of[1:]])
    tokens = np.concatenate([a["x"][0], a["ctx"][0]], axis=0)
    feats = lambda m: np.ascontiguousarray(m.T.reshape(-1, P, m.shape[0]).transpose(1, 0, 2))
    arrays = {
        "xT": feats(tokens), "cT": feats(np.stack([a["c"][0], a["c_ctx"]])),
        "cb": np.broadcast_to(np.concatenate([a["c"][0], a["c_ctx"]])[None], (P, 2 * D)),
        "pc": np.stack(par, axis=1), "fin": columns_of(a["final_g"]), "srow": np.stack(rows), "consts": consts,
        "sguw": a["sgu_w"].transpose(0, 3, 1, 2), "wg": wg, "wmod": wmod, "win": tiles_of(a["w_in"][:, :, cols]),
        "wout": tiles_of(np.concatenate([a["w_out"][:, 512:], a["w_out"][:, :512]], axis=1)), "wgu": tiles_of(w_gu), "wdn": tiles_of(a["w_down"]),
    }
    aw = a["a_w_in_2"][0]
    per = []
    for hp in range(HP):
        c = np.arange(hp * P, hp * P + P)
        at = [(3 * g + i) * D for g in range(3) for i in range(2)] + [(3 * g + 2) * D for g in range(3)] + [9 * D]
        per += [c + b for b in at]
    arrays["wa"] = tiles_of(aw[:, np.concatenate(per)])
    arrays["wao"] = tiles_of(a["a_w_out_2"][0])
    arrays["pleg"] = tiles_of(a["ple_w_gate_2"])
    arrays["plep"] = tiles_of(a["ple_w_proj_2"])
    bw = a["b_w_in_2"][0]
    kc = np.arange(D, D + 64)
    arrays["wbk"] = tiles_of(bw[:, np.concatenate([kc, kc, kc + 64, kc + 64, np.arange(D + P, D + 2 * P)])])
    zc = D + 2 * P
    arrays["wbqz"] = tiles_of(bw[:, np.concatenate([np.concatenate([np.arange(h * P, h * P + P), np.arange(zc + h * P, zc + h * P + P)]) for h in range(HP)])])
    arrays["wbo"] = tiles_of(a["b_w_out_2"][0])
    arrays["p"] = np.stack([feats(a["p_2"][i, 0]) for i in range(DEPTH)])
    inv = (1.0 / (10000.0 ** (np.arange(0, ADIM, 2, dtype=f) / f(ADIM)))).astype(f)
    ang = np.arange(SEQ, dtype=f)[:, None] * inv[None, :]
    cos, sin = np.cos(ang).astype(f).T, np.sin(ang).astype(f).T
    rope = np.stack([np.tile(cos, (4, 1)), np.concatenate([-sin, sin, -sin, sin])], axis=1)
    am = np.full((P, 4, 768), NEG, f)
    for r in range(4):
        dist = (4 * ts[:, None] + r) - np.arange(SEQ)[None, :]
        am[:, r, 0:SEQ][(dist >= 0) & (dist <= P)] = 0
        back = ts[:, None] - ts[None, :]
        am[:, r, SEQ:SEQ + P][back >= 0] = 0
        am[:, r, SEQ + P:768][(back >= 0) & (back % 4 == 0)] = 0
    bm = np.full((P, 896), NEG, f)
    bm[:, 0:P][ts[:, None] >= ts[None, :]] = 0
    for b in range(3):
        dist = ts[:, None] + P - np.arange(2 * P)[None, :]
        bm[:, P + 2 * P * b:P + 2 * P * (b + 1)][(dist >= 0) & (dist <= P - 1)] = 0
    lnp = np.stack([columns_of(a["ln_g_2"]), columns_of(a["ln_b_2"])], axis=2).reshape(P, -1)
    sink = np.broadcast_to(a["b_sinks_2"][0][None], (P, AH))
    arrays["b2"] = np.concatenate([am.reshape(P, -1), rope.reshape(P, -1), lnp, sink], axis=1)
    arrays["bmask"] = bm
    nc = _bacc.Bacc("TRN2", target_bir_lowering=False, num_devices=1)
    names = ["xT", "cT", "cb", "pc", "fin", "srow", "consts", "sguw", "wg", "wmod", "win", "wout", "wgu", "wdn",
             "b2", "bmask", "p", "wa", "wao", "pleg", "plep", "wbk", "wbqz", "wbo"]
    arrays = {n: np.ascontiguousarray(arrays[n]) for n in names}
    args = [nc.dram_tensor("in_" + n, arrays[n].shape, mybir.dt.from_np(arrays[n].dtype), kind="ExternalInput").ap() for n in names]
    out = nc.dram_tensor("out_0_dram", (P, KT, SEQ), FP32, kind="ExternalOutput").ap()
    build_program(nc, *args, out)
    r = _run(nc, [{"in_" + n: arrays[n] for n in names}], core_ids=[0])
    got = np.asarray(r.results[0]["out_0_dram"])
    return np.ascontiguousarray(got.transpose(2, 1, 0).reshape(1, SEQ, D))
```
